# Optimizing a Trainium2 kernel written in Bass

```python
import jax
import jax.numpy as jnp
from jax import lax
import numpy as np

D_MODEL = 1024
BATCH = 1
SEQ = 512
DEPTH = 2
DEC_BATCH = 8
DEC_SEQ = 1
PAST_LEN = 256
PAGE_SIZE = 128

EPS = 1e-6
D_CONV = D_MODEL // 2
CONV_W = 3
D_CHUNK = D_MODEL // 2
N_CHUNK_HEADS = 4
CHUNK_HD = D_CHUNK // N_CHUNK_HEADS
CHUNK = 128
HEAD_DIM = 64
N_HEADS = D_MODEL // HEAD_DIM
N_KV = 4
HPG = N_HEADS // N_KV
CMP_BLOCK = 32
CMP_STRIDE = 16
SEL_BLOCK = 64
TOP_N = 16
WINDOW = 512
QBLOCK = 128
ROPE_THETA = 10000.0
SCALE = HEAD_DIM ** -0.5
NEG_INF = -1e30
FORCE_BONUS = 1e4
D_FF = ((8 * D_MODEL + 2) // 3 + 255) // 256 * 256

kernel_name = "hybrid_conv_chunkmlp_nsa_decoder_step"

def rmsnorm(x, g):
    xf = x.astype(jnp.float32)
    y = xf * lax.rsqrt(jnp.mean(xf * xf, axis=-1, keepdims=True) + EPS)
    return (y * g.astype(jnp.float32)).astype(x.dtype)

def rope(x, pos):
    half = HEAD_DIM // 2
    inv = ROPE_THETA ** (-jnp.arange(half, dtype=jnp.float32) * 2.0 / HEAD_DIM)
    ang = pos.astype(jnp.float32)[:, None] * inv[None, :]
    shape = (pos.shape[0],) + (1,) * (x.ndim - 3) + (HEAD_DIM,)
    cos = jnp.concatenate([jnp.cos(ang), jnp.cos(ang)], -1).reshape(shape)
    sin = jnp.concatenate([jnp.sin(ang), jnp.sin(ang)], -1).reshape(shape)
    xf = x.astype(jnp.float32)
    rot = jnp.concatenate([-xf[..., half:], xf[..., :half]], -1)
    return (xf * cos + rot * sin).astype(x.dtype)

def swiglu(x, w_in, w_out):
    a, b = jnp.split(x @ w_in, 2, axis=-1)
    return (jax.nn.silu(a) * b) @ w_out

def chunk_mix(v, w_spatial, b_spatial):
    n, t, _ = v.shape
    nch = -(-t // CHUNK)
    tp = nch * CHUNK
    vp = jnp.pad(v, ((0, 0), (0, tp - t), (0, 0))).reshape(n, nch, CHUNK, N_CHUNK_HEADS, CHUNK_HD)
    causal = jnp.tril(jnp.ones((CHUNK, CHUNK), dtype=bool))
    w = jnp.where(causal[None], w_spatial, 0)
    mixed = jnp.einsum('hts,ncshd->ncthd', w, vp) + b_spatial.T[:, :, None]
    return mixed.reshape(n, tp, D_CHUNK)[:, :t]

def conv_chunk_mixer(x, conv_hist, w_in0, conv_w, norm_v, w_spatial, b_spatial, w_out0):
    t = x.shape[1]
    h = x @ w_in0
    b_gate, c_gate, h_conv, u, v = jnp.split(
        h, [D_CONV, 2 * D_CONV, 3 * D_CONV, 3 * D_CONV + D_CHUNK], axis=-1)
    z = c_gate * h_conv
    zh = jnp.concatenate([conv_hist.astype(z.dtype), z], axis=1)
    conv = conv_w[0] * zh[:, 0:t]
    for j in range(1, CONV_W):
        conv = conv + conv_w[j] * zh[:, j:j + t]
    y_conv = b_gate * conv
    vn = rmsnorm(jax.nn.gelu(v), norm_v)
    y_chunk = jax.nn.gelu(u) * chunk_mix(vn, w_spatial, b_spatial)
    y = jnp.concatenate([y_conv, y_chunk], axis=-1) @ w_out0
    return y, zh[:, -(CONV_W - 1):], vn

def nsa_project(x, w_in1):
    n, t, _ = x.shape
    h = x @ w_in1
    q_dim = N_HEADS * HEAD_DIM
    kv_dim = 6 * N_KV * HEAD_DIM
    q = h[..., :q_dim].reshape(n, t, N_KV, HPG, HEAD_DIM)
    kv = h[..., q_dim:q_dim + kv_dim].reshape(n, t, 6, N_KV, HEAD_DIM)
    gates = jax.nn.sigmoid(h[..., q_dim + kv_dim:].astype(jnp.float32)).astype(x.dtype)
    return q, kv, gates.reshape(n, t, N_KV, HPG, 3)

def compress(k, pe, w):
    n, l, g, d = k.shape
    nseg = -(-l // CMP_STRIDE)
    kp = jnp.pad(k, ((0, 0), (0, nseg * CMP_STRIDE - l), (0, 0), (0, 0)))
    seg = kp.reshape(n, nseg, CMP_STRIDE, g, d)
    r = CMP_BLOCK // CMP_STRIDE
    nc = nseg - r + 1
    blocks = jnp.concatenate([seg[:, i:i + nc] for i in range(r)], axis=2)
    return jnp.einsum('nclgd,lde->ncge', blocks + pe[:, None, :], w)

def nsa_core(q, q_rot, qpos, ck, cv, fetch, wk, wv, wpos, gates, key_len):
    b, nq = q.shape[0], q.shape[1]
    nc = ck.shape[1]
    t = qpos[:, None]
    s = jnp.einsum('bqghd,bngd->bghqn', q, ck).astype(jnp.float32) * SCALE
    cvalid = (jnp.arange(nc) * CMP_STRIDE + CMP_BLOCK - 1)[None, :] <= t
    p_cmp = jnp.where(cvalid, jax.nn.softmax(jnp.where(cvalid, s, NEG_INF), axis=-1), 0.0)
    o_cmp = jnp.einsum('bghqn,bngd->bqghd', p_cmp.astype(cv.dtype), cv)
    ns = -(-key_len // SEL_BLOCK)
    cstart = jnp.arange(nc) * CMP_STRIDE
    sstart = jnp.arange(ns) * SEL_BLOCK
    overlap = ((cstart[:, None] < sstart[None, :] + SEL_BLOCK)
               & (cstart[:, None] + CMP_BLOCK > sstart[None, :])).astype(jnp.float32)
    imp = jnp.einsum('bghqn,nj->bgqj', p_cmp, overlap)
    cur = (qpos // SEL_BLOCK)[:, None]
    jj = jnp.arange(ns)[None, :]
    forced = (jj == 0) | (jj == cur) | (jj == cur - 1)
    svalid = sstart[None, :] <= t
    score = jnp.where(svalid, imp + jnp.where(forced, FORCE_BONUS, 0.0), NEG_INF)
    _, idx = lax.top_k(score, min(TOP_N, ns))
    kpos = (idx[..., None] * SEL_BLOCK + jnp.arange(SEL_BLOCK)).reshape(b, N_KV, nq, -1)
    k_sel, v_sel = fetch(kpos)
    s = jnp.einsum('bqghd,bgqkd->bghqk', q_rot, k_sel).astype(jnp.float32) * SCALE
    smask = (kpos <= qpos[None, None, :, None])[:, :, None]
    p_slc = jax.nn.softmax(jnp.where(smask, s, NEG_INF), axis=-1)
    o_slc = jnp.einsum('bghqk,bgqkd->bqghd', p_slc.astype(v_sel.dtype), v_sel)
    s = jnp.einsum('bqghd,bwgd->bghqw', q_rot, wk).astype(jnp.float32) * SCALE
    dist = t - wpos[None, :]
    wmask = (wpos[None, :] >= 0) & (dist >= 0) & (dist < WINDOW)
    p_win = jax.nn.softmax(jnp.where(wmask, s, NEG_INF), axis=-1)
    o_win = jnp.einsum('bghqw,bwgd->bqghd', p_win.astype(wv.dtype), wv)
    o = gates[..., 0:1] * o_cmp + gates[..., 1:2] * o_slc + gates[..., 2:3] * o_win
    return o.reshape(b, nq, N_HEADS * HEAD_DIM)

def nsa_prompt(x, w_in1, pe_cmp, w_cmp, w_out1):
    n, t, _ = x.shape
    pos = jnp.arange(t)
    q, kv, gates = nsa_project(x, w_in1)
    q_rot = rope(q, pos)
    k_cmp, v_cmp = kv[:, :, 0], kv[:, :, 1]
    k_slc, v_slc = rope(kv[:, :, 2], pos), kv[:, :, 3]
    k_win, v_win = rope(kv[:, :, 4], pos), kv[:, :, 5]
    ck = compress(k_cmp, pe_cmp[0], w_cmp[0])
    cv = compress(v_cmp, pe_cmp[1], w_cmp[1])
    pad = ((0, 0), (WINDOW, 0), (0, 0), (0, 0))
    kw_pad = jnp.pad(k_win, pad)
    vw_pad = jnp.pad(v_win, pad)
    bi = jnp.arange(n)[:, None, None, None]
    gi = jnp.arange(N_KV)[None, :, None, None]

    def fetch(kpos):
        p = jnp.clip(kpos, 0, t - 1)
        return k_slc[bi, p, gi], v_slc[bi, p, gi]

    def block(i):
        qs = i * QBLOCK
        qpos = qs + jnp.arange(QBLOCK)
        wpos = qs - WINDOW + jnp.arange(WINDOW + QBLOCK)
        qb = lax.dynamic_slice_in_dim(q, qs, QBLOCK, axis=1)
        qrb = lax.dynamic_slice_in_dim(q_rot, qs, QBLOCK, axis=1)
        gb = lax.dynamic_slice_in_dim(gates, qs, QBLOCK, axis=1)
        wk = lax.dynamic_slice_in_dim(kw_pad, qs, WINDOW + QBLOCK, axis=1)
        wv = lax.dynamic_slice_in_dim(vw_pad, qs, WINDOW + QBLOCK, axis=1)
        return nsa_core(qb, qrb, qpos, ck, cv, fetch, wk, wv, wpos, gb, t)

    o = lax.map(block, jnp.arange(t // QBLOCK))
    o = jnp.moveaxis(o, 0, 1).reshape(n, t, N_HEADS * HEAD_DIM)
    y = o @ w_out1
    kv_rows = jnp.stack([k_cmp, v_cmp, k_slc, v_slc], axis=2)
    win_rows = jnp.stack([k_win, v_win], axis=2)[:, t - min(WINDOW, t):]
    return y, kv_rows, win_rows

def nsa_sample(x, cache_kv, cache_win, page_table, w_in1, pe_cmp, w_cmp, w_out1):
    n, s_len, _ = x.shape
    past_len = page_table.shape[1] * PAGE_SIZE
    wb = cache_win.shape[1]
    qpos = past_len + jnp.arange(s_len)
    q, kv, gates = nsa_project(x, w_in1)
    q_rot = rope(q, qpos)
    k_cmp, v_cmp = kv[:, :, 0], kv[:, :, 1]
    k_slc, v_slc = rope(kv[:, :, 2], qpos), kv[:, :, 3]
    k_win, v_win = rope(kv[:, :, 4], qpos), kv[:, :, 5]
    past_cmp = cache_kv[page_table, :, 0:2].reshape(n, past_len, 2, N_KV, HEAD_DIM)
    ck = compress(jnp.concatenate([past_cmp[:, :, 0], k_cmp], axis=1), pe_cmp[0], w_cmp[0])
    cv = compress(jnp.concatenate([past_cmp[:, :, 1], v_cmp], axis=1), pe_cmp[1], w_cmp[1])
    bi = jnp.arange(n)[:, None, None, None]
    gi = jnp.arange(N_KV)[None, :, None, None]

    def fetch(kpos):
        pc = jnp.clip(kpos, 0, past_len - 1)
        phys = page_table[bi, pc // PAGE_SIZE]
        off = pc % PAGE_SIZE
        kp = cache_kv[phys, off, 2, gi]
        vp = cache_kv[phys, off, 3, gi]
        pn = jnp.clip(kpos - past_len, 0, s_len - 1)
        is_past = (kpos < past_len)[..., None]
        return jnp.where(is_past, kp, k_slc[bi, pn, gi]), jnp.where(is_past, vp, v_slc[bi, pn, gi])

    wk = jnp.concatenate([cache_win[:, :, 0], k_win], axis=1)
    wv = jnp.concatenate([cache_win[:, :, 1], v_win], axis=1)
    wpos = jnp.concatenate([past_len - wb + jnp.arange(wb), qpos])
    o = nsa_core(q, q_rot, qpos, ck, cv, fetch, wk, wv, wpos, gates, past_len + s_len)
    y = o @ w_out1
    kv_rows = jnp.stack([k_cmp, v_cmp, k_slc, v_slc], axis=2)
    win_rows = jnp.stack([k_win, v_win], axis=2)
    return y, kv_rows, win_rows

def setup_inputs(seed: int = 0) -> dict:
    key = jax.random.key(seed)
    ks = jax.random.split(key, 24)
    f32 = jnp.float32

    def nrm(k, shape, scale):
        return jax.random.normal(k, shape, f32) * scale

    n_pages = PAST_LEN // PAGE_SIZE
    n_used = DEC_BATCH * n_pages
    n_phys = n_used + max(1, n_used // 4)
    page_table = jax.random.permutation(ks[0], n_phys)[:n_used].reshape(DEC_BATCH, n_pages).astype(jnp.int32)
    win_buf = min(WINDOW, PAST_LEN)
    in1_cols = N_HEADS * HEAD_DIM + 6 * N_KV * HEAD_DIM + 3 * N_HEADS
    return {
        "x_prompt": nrm(ks[1], (BATCH, SEQ, D_MODEL), 1.0),
        "x_sample": nrm(ks[2], (DEC_BATCH, DEC_SEQ, D_MODEL), 1.0),
        "state_conv": nrm(ks[3], (DEC_BATCH, CONV_W - 1, D_CONV), 1.0),
        "cache_kv": nrm(ks[4], (n_phys, PAGE_SIZE, 4, N_KV, HEAD_DIM), 1.0),
        "cache_win": nrm(ks[5], (DEC_BATCH, win_buf, 2, N_KV, HEAD_DIM), 1.0),
        "page_table": page_table,
        "norm_mix": 1.0 + nrm(ks[6], (DEPTH, D_MODEL), 0.05),
        "norm_ffn": 1.0 + nrm(ks[7], (DEPTH, D_MODEL), 0.05),
        "norm_final": 1.0 + nrm(ks[8], (D_MODEL,), 0.05),
        "w_in0": nrm(ks[9], (D_MODEL, 3 * D_CONV + 2 * D_CHUNK), D_MODEL ** -0.5),
        "conv_w": nrm(ks[10], (CONV_W, D_CONV), CONV_W ** -0.5),
        "norm_v": 1.0 + nrm(ks[11], (D_CHUNK,), 0.05),
        "w_spatial": nrm(ks[12], (N_CHUNK_HEADS, CHUNK, CHUNK), CHUNK ** -0.5),
        "b_spatial": 1.0 + nrm(ks[13], (N_CHUNK_HEADS, CHUNK), 0.1),
        "w_out0": nrm(ks[14], (D_CONV + D_CHUNK, D_MODEL), (D_CONV + D_CHUNK) ** -0.5),
        "w_in1": nrm(ks[15], (D_MODEL, in1_cols), D_MODEL ** -0.5),
        "pe_cmp": nrm(ks[16], (2, CMP_BLOCK, HEAD_DIM), 0.1),
        "w_cmp": nrm(ks[17], (2, CMP_BLOCK, HEAD_DIM, HEAD_DIM), (CMP_BLOCK * HEAD_DIM) ** -0.5),
        "w_out1": nrm(ks[18], (N_HEADS * HEAD_DIM, D_MODEL), (N_HEADS * HEAD_DIM) ** -0.5),
        "w_ffn_in": nrm(ks[19], (DEPTH, D_MODEL, 2 * D_FF), D_MODEL ** -0.5),
        "w_ffn_out": nrm(ks[20], (DEPTH, D_FF, D_MODEL), D_FF ** -0.5),
    }

def reference(x_prompt, x_sample, state_conv, cache_kv, cache_win, page_table,
              norm_mix, norm_ffn, norm_final, w_in0, conv_w, norm_v, w_spatial, b_spatial, w_out0,
              w_in1, pe_cmp, w_cmp, w_out1, w_ffn_in, w_ffn_out):
    xp, xs = x_prompt, x_sample
    for layer in range(DEPTH):
        hp = rmsnorm(xp, norm_mix[layer])
        hs = rmsnorm(xs, norm_mix[layer])
        if layer % 2 == 0:
            zero_hist = jnp.zeros((xp.shape[0], CONV_W - 1, D_CONV), xp.dtype)
            yp, conv_state_prompt, _ = conv_chunk_mixer(
                hp, zero_hist, w_in0, conv_w, norm_v, w_spatial, b_spatial, w_out0)
            ys, conv_state_sample, chunk_v_sample = conv_chunk_mixer(
                hs, state_conv, w_in0, conv_w, norm_v, w_spatial, b_spatial, w_out0)
        else:
            yp, kv_prompt, win_prompt = nsa_prompt(hp, w_in1, pe_cmp, w_cmp, w_out1)
            ys, kv_sample, win_sample = nsa_sample(
                hs, cache_kv, cache_win, page_table, w_in1, pe_cmp, w_cmp, w_out1)
        xp = xp + yp
        xs = xs + ys
        xp = xp + swiglu(rmsnorm(xp, norm_ffn[layer]), w_ffn_in[layer], w_ffn_out[layer])
        xs = xs + swiglu(rmsnorm(xs, norm_ffn[layer]), w_ffn_in[layer], w_ffn_out[layer])
    y_prompt = rmsnorm(xp, norm_final)
    y_sample = rmsnorm(xs, norm_final)
    return (y_prompt, y_sample, conv_state_prompt, conv_state_sample, chunk_v_sample,
            kv_prompt, kv_sample, win_prompt, win_sample)


_drawn_inputs = setup_inputs


def setup_inputs(seed=0):
    import zlib

    import numpy as np

    out = dict(_drawn_inputs(seed))
    spreads = {}
    factors = {}
    for name, (base, spread) in spreads.items():
        noise = np.random.default_rng([zlib.crc32(name.encode()), seed]).standard_normal(out[name].shape)
        drawn = base * np.exp(spread * noise) if base else spread * noise
        out[name] = jnp.asarray(drawn.astype(out[name].dtype))
    for name, factor in factors.items():
        out[name] = (out[name] * factor).astype(out[name].dtype)
    return out
```

```python
from contextlib import ExitStack, contextmanager

import concourse.bass as bass
import numpy as np
from concourse import mybir

F32, F32R, BF16, I32 = mybir.dt.float32, mybir.dt.float32r, mybir.dt.bfloat16, mybir.dt.int32
ALU, ACT, AX = mybir.AluOpType, mybir.ActivationFunctionType, mybir.AxisListType

P = 128
D = 1024
SEQ, NS = 512, 8
T = SEQ + NS
HALF = T // 2
KD = D // P
DC = 512
FT = DC // P
FF = 2816
KF = FF // P
NH, NKV, HD = 16, 4, 64
PAST, PAGE = 256, 128
NPAGE = PAST // PAGE
SCALE = HD ** -0.5
NEG = -1e30
EPS = 1e-6
QT = SEQ // P
NC = 32
SEGS = 2 * NS * 16 + 2 * 32 + 3
NCOL = SEGS - 1
SLOT = 2048
KH = KF // 2

PHASES = [("in0", 10, 20), ("out0", 4, 8), ("up0", 22, 44), ("down0", 16, 8),
          ("inq", 4, 8), ("in1", 7, 13), ("out1", 4, 8), ("up1", 22, 44), ("down1", 16, 8)]
S0, U0 = {}, {}
_s = _u = 0
for _n, _a, _b in PHASES:
    S0[_n], U0[_n] = _s, _u
    _s, _u = _s + _a, _u + _b
RAW = {n: 64 if n in ("inq", "out1") else 32 for n, _, _ in PHASES}
RAW0, _c = {}, [0, 0]
for _n, _a, _ in PHASES:
    RAW0[_n] = tuple(_c)
    for _k in range(S0[_n], S0[_n] + _a):
        _c[_k % 2] += RAW[_n]
ORDER = [n for n, _, _ in PHASES]


def raw_of(name, j):
    b = (S0[name] + j) % 2
    slots = dict((n, k) for n, k, _ in PHASES)[name]
    if j < slots:
        return RAW0[name][b] + RAW[name] * (j // 2 + 1)
    nxt = ORDER[ORDER.index(name) + 1]
    return RAW0[nxt][b] + RAW[nxt]

G_MIX, G_FFN, G_FIN, G_CONV, G_V = (0, 8), (16, 24), 32, 40, 52
N_GAIN = 56

C_ROT, C_COS, C_SIN = 0, 128, 128 + T
C_CB = 128 + 2 * T
C_CV = C_CB + QT * NC
N_CA = C_CV + QT * NC


def consts():
    p = np.arange(P)
    eye = np.eye(P, dtype=np.float32)
    base = np.concatenate([eye, np.ones((P, P), np.float32), np.full((P, 8), EPS, np.float32)], 1)
    tril = (p[:, None] <= p[None, :]).astype(np.float32)
    rot = np.zeros((P, P), np.float32)
    for m in range(P):
        if m % 64 < 32:
            rot[m + 32, m] = -1.0
        else:
            rot[m - 32, m] = 1.0
    pos = np.concatenate([np.arange(SEQ), np.full(NS, PAST)]).astype(np.float32)
    inv = np.power(np.float32(10000.0), -np.arange(32, dtype=np.float32) * np.float32(2.0) / np.float32(HD))
    ang = inv.astype(np.float32)[p % 32][:, None] * pos[None, :]
    cb = np.zeros((P, QT, NC), np.float32)
    for i in range(QT):
        t = i * P + p[:, None]
        c = np.arange(NC)[None, :]
        cb[:, i] = ((16 * c + 31 <= t) & (c < 31)).astype(np.float32)
    att = np.concatenate([rot, np.cos(ang).astype(np.float32), np.sin(ang).astype(np.float32),
                          ((1 - cb) * np.float32(NEG)).reshape(P, -1), cb.reshape(P, -1)], 1)
    n_r, g_r = p // 16, (p % 16) // 4
    new = np.zeros((P, PAST + NS), np.float32)
    new[:, PAST:] = np.where(n_r[:, None] == np.arange(NS)[None, :], 0.0, NEG)
    cmp_ = np.where((n_r[:, None] == p[None, :] // 16) & (p[None, :] % 16 < 15), 0.0, NEG)
    grp = (g_r[:, None] == np.arange(4)[None, :]).astype(np.float32)
    smp = np.concatenate([new, cmp_, grp], 1).astype(np.float32)
    causal = np.where(p[None, :] > p[:, None], NEG, 0.0).astype(np.float32)
    return {"c_base": base, "c_tril": tril, "c_att": att, "c_smp": smp, "c_causal": causal}


class Count:

    def __init__(self, sem):
        self.sem, self.n, self.term = sem, 0, None

    def on(self, ins):
        ins.then_inc(self.sem, 1)
        self.n += 1
        return ins

    @property
    def now(self):
        return self.n if self.term is None else self.term + self.n


@contextmanager
def loop(eng, trips, per):
    with eng.Fori(0, trips) as t:
        first = {}
        for c, k in per:
            first[c] = c.n
            c.term = t * k
        yield t
        for c, k in per:
            assert c.n - first[c] == k, (c.sem, c.n - first[c], k)
    for c, k in per:
        c.term = None
        c.n += k * (trips - 1)


def program(nc, a, out):
    ctx = ExitStack()
    with ctx:
        lay = [16512]

        def at(name, shape, dt, offset):
            return nc.alloc_sbuf_tensor_at(name, shape, dt, offset=offset)

        def size(shape, dt):
            n = 2 if dt == BF16 else 4
            for k in shape[1:]:
                n *= k
            return (n + 31) // 32 * 32

        def new(name, shape, dt=F32):
            t = at(name, shape, dt, lay[0])
            lay[0] += size(shape, dt)
            return t

        def packed(offset, *tensors):
            got = []
            for name, shape, dt in tensors:
                got.append(at(name, shape, dt, offset))
                offset += size(shape, dt)
            return got, offset

        XT = new("XT", [P, KD, T])
        h_at = lay[0]
        H = new("H", [P, KD, 2, T], F32R)
        g_at = lay[0]
        G = new("G", [P, KF, 2, T], F32R)
        wr_at = lay[0]
        WR = new("WR", [P, 2, SLOT])
        WH = new("WH", [P, 2, SLOT], F32R)
        WL = new("WL", [P, 2, SLOT], F32R)
        BASE = new("BASE", [P, 2 * P + 8])
        IDENT, ONES, EPSC = BASE[:, 0:P], BASE[:, P:2 * P], BASE[:, 2 * P:2 * P + 1]
        GAINS = new("GAINS", [P, N_GAIN])
        rstd_at = lay[0]
        RSTD = new("RSTD", [P, T])
        ACC = new("ACC", [P, T])
        SQ = new("SQ", [P, 2, T])
        tmp_at = lay[0]
        TA = new("TA", [P, 2, T])
        TB = new("TB", [P, T])
        TG = new("TG", [P, 2, T])
        tmp_end = lay[0] + 2048
        assert tmp_end <= 229344, tmp_end
        s_at = g_at + 8 * 2 * T * 4
        s_end = g_at + KF * 2 * T * 4
        P0 = at("P0", [P, 21, T], F32, s_at)
        (XL, XS), _ = packed(s_at, ("XL", [P, QT, D], F32), ("XS", [NS, D], F32))
        (BSP, WT, HT, SCV, WSP, ACV, W00, TRIL, GROW, ZO, CV), e = packed(
            s_at + 20 * T * 4, ("BSP", [P, 4, P], F32), ("WT", [P, 4, P], F32), ("HT", [P, FT, 16], F32),
            ("SCV", [16, DC], F32), ("WSP", [P, 4, P], F32), ("ACV", [P, T], F32), ("W00", [P, 4, 8], F32),
            ("TRIL", [P, P], F32), ("GROW", [N_GAIN, P], F32), ("ZO", [10, DC], F32), ("CV", [NS, DC], F32))
        assert e <= s_end, (e, s_end)
        YO = at("YO", [P, QT, D], F32, wr_at)
        YS = at("YS", [NS, D], F32, wr_at + QT * D * 4)
        VT = at("VT", [P, FT, 4, P], F32, h_at)

        PG = ctx.enter_context(nc.psum_tensor("PG", [P, 2, 2, 512], F32))
        M = ctx.enter_context(nc.psum_tensor("M", [P, 4, 512], F32))

        def sem(name):
            return ctx.enter_context(nc.semaphore(name))

        CT = at("CT", [P, 16, SEGS], F32, g_at)
        NSTG = 5
        PST = at("PST", [P, NSTG, 2, 256], F32, g_at + size([P, 16, SEGS], F32))
        PEK = at("PEK", [32, 2, 2, HD], F32, g_at + size([P, 16, SEGS], F32) + NSTG * 2048)
        WBD = at("WBD", [P, 2, 32, P], F32, h_at)
        (QR, KP), e = packed(h_at, ("QR", [P, KD, T], F32), ("KP", [P, 2, NKV, SEQ], F32))
        assert e <= g_at
        (VTK, KVO), e = packed(s_at + 21 * T * 4, ("VTK", [P, QT, 2, 256], F32), ("KVO", [P, 1536], F32))
        assert e <= s_end
        (PB, PT, TC), e = packed(s_at + 8 * T * 4, ("PB", [P, 2, 4, SEQ], F32), ("PT", [P, 4, 512], F32),
                                 ("TC", [P, 4, 2, NC], F32))
        assert e <= s_at + 21 * T * 4
        (CA, CBF, GT, CVT, CKT, CVK, CKP), e = packed(
            tmp_at, ("CA", [P, N_CA], F32), ("CBF", [P, 2 * P], BF16), ("GT", [P, QT, 48], F32),
            ("CVT", [P, NCOL], F32), ("CKT", [P, NCOL], F32), ("CVK", [NC, 2, P], F32), ("CKP", [P, 2, 2, NC], F32))
        assert e <= tmp_end, (e, tmp_end)
        (KN, GS, SGT, ST8, QS, OS), e = packed(
            e, ("KN", [P, 2, 2, NS], F32), ("GS", [P, 3], F32), ("SGT", [NS, 48], F32),
            ("ST8", [P, 48], F32), ("QS", [P, KD, NS], F32), ("OS", [P, KD, NS], F32))
        assert e <= 229344, e
        VN = at("VN", [NS, 2, 256], F32, rstd_at)
        CVS = at("CVS", [P, 2, P], F32, tmp_at + size([P, N_CA], F32) + 512 + size([P, QT, 48], F32))
        PTAB = at("PTAB", [1, 16], I32, s_end - 64)
        ROT, COS, SIN = CA[:, 0:P], CA[:, C_COS:C_COS + T], CA[:, C_SIN:C_SIN + T]
        KVS = at("KVS", [P, NS, 2, 512], F32, s_at + 8 * T * 4)
        (QPD, Q2, PTP, KTS, CS, SCS, PS, OA, PTN, OM), e = packed(
            h_at, ("QPD", [P, NS, 2, P], F32), ("Q2", [P, 2, 2, P], F32), ("PTP", [P, 2, NS, P], F32),
            ("KTS", [P, 2, 2, 256], F32), ("CS", [P, 264 + P + 4], F32), ("SCS", [P, 264], F32),
            ("PS", [P, 264], F32), ("OA", [P, 256], F32), ("PTN", [P, P], F32), ("OM", [P, 2, HD], F32))
        assert e <= g_at, (e, g_at)

        w_raw = [sem("w_raw0"), sem("w_raw1")]
        w_hi = Count(sem("w_hi"))
        w_split = Count(sem("w_split"))
        half_used = Count(sem("half_used"))
        tile_done = Count(sem("tile_done"))
        tile_out = Count(sem("tile_out"))
        h_ready = Count(sem("h_ready"))
        g_ready = Count(sem("g_ready"))
        a_hi = Count(sem("a_hi"))
        a_sq = Count(sem("a_sq"))
        acc_ok = Count(sem("acc_ok"))
        st_done = Count(sem("st_done"))
        a_std = Count(sem("a_std"))
        rstd_ok = Count(sem("rstd_ok"))
        a_silu = Count(sem("a_silu"))
        t_gate = Count(sem("t_gate"))
        a_ghi = Count(sem("a_ghi"))
        d_in = sem("d_in")
        d_small = sem("d_small")
        d_out = sem("d_out")
        outs = [0]
        t_fill = Count(sem("t_fill"))
        t_drain = Count(sem("t_drain"))
        vec = Count(sem("vec"))
        vg_ok = Count(sem("vg_ok"))
        vsq_ok = Count(sem("vsq_ok"))
        accv_ok = Count(sem("accv_ok"))
        stv_done = Count(sem("stv_done"))
        stdv_ok = Count(sem("stdv_ok"))
        vn_ok = Count(sem("vn_ok"))
        vt_fill = Count(sem("vt_fill"))
        vt_drain = Count(sem("vt_drain"))
        cv_ok = Count(sem("cv_ok"))
        z_ok = Count(sem("z_ok"))
        zo_fill = Count(sem("zo_fill"))
        zo_ok = Count(sem("zo_ok"))
        mixed = Count(sem("mixed"))
        ug_ok = Count(sem("ug_ok"))
        y_ok = Count(sem("y_ok"))
        y_hi = Count(sem("y_hi"))
        at_g = Count(sem("at_g"))
        passed = sem("passed")
        q_fill = Count(sem("q_fill"))
        q_v = Count(sem("q_v"))
        q_a = Count(sem("q_a"))
        ct_prompt = Count(sem("ct_prompt"))
        cmp_done = Count(sem("cmp_done"))
        ck_ok = Count(sem("ck_ok"))
        rope_p = Count(sem("rope_p"))
        rope_in = Count(sem("rope_in"))
        rope_ok = Count(sem("rope_ok"))
        kp_ok = Count(sem("kp_ok"))
        qs_ok = Count(sem("qs_ok"))
        gt_ok = Count(sem("gt_ok"))
        cs_done = Count(sem("cs_done"))
        cs_out = Count(sem("cs_out"))
        c_max = Count(sem("c_max"))
        c_exp = Count(sem("c_exp"))
        c_ready = Count(sem("c_ready"))
        s_done = Count(sem("s_done"))
        nb_ok = Count(sem("nb_ok"))
        exp_done = Count(sem("exp_done"))
        p_ready = Count(sem("p_ready"))
        pv_done = Count(sem("pv_done"))
        o_hi = Count(sem("o_hi"))
        o_out = Count(sem("o_out"))
        qpd_ok = Count(sem("qpd_ok"))
        ss_done = Count(sem("ss_done"))
        snb_ok = Count(sem("snb_ok"))
        sp_ok = Count(sem("sp_ok"))
        sv_done = Count(sem("sv_done"))
        spv_done = Count(sem("spv_done"))
        oa_ok = Count(sem("oa_ok"))
        om_ok = Count(sem("om_ok"))
        os_hi = Count(sem("os_hi"))
        kts_used = Count(sem("kts_used"))
        d_ca, d_pt, d_pe, d_wc = (sem(n) for n in ("d_ca", "d_pt", "d_pe", "d_wc"))
        d_kv, d_gs, d_cs = (sem(n) for n in ("d_kv", "d_gs", "d_cs"))
        d_page = [sem(f"d_page{n}") for n in range(NSTG)]
        d_kvs = [sem(f"d_kvs{n}") for n in range(NS)]
        N_PHYS = a["cache_kv"].shape[0]
        fin_p = Count(sem("fin_p"))
        fin_v = Count(sem("fin_v"))


        def one(i):
            return bass.ds(i, 1)

        def sets(par):
            return PG[:, par, :, 0:HALF]

        def halves(x):
            return x.rearrange("p (h c) -> p h c", h=2)

        def row(x, m):
            return x[:, one(m), :].rearrange("p a (h c) -> p (a h) c", h=2)

        w0 = a["w_in0"].rearrange("(k p) c -> p k c", p=P)
        wo0 = a["w_out0"].rearrange("(k p) c -> p k c", p=P)
        w1 = a["w_in1"].rearrange("(k p) c -> p k c", p=P)
        wo1 = a["w_out1"].rearrange("(g e j d) c -> g j e d c", g=2, e=2, j=4)
        wup = [a["w_ffn_in"][l].rearrange("(k p) c -> p k c", p=P) for l in range(2)]
        wdn = [a["w_ffn_out"][l].rearrange("(k p) c -> p k c", p=P) for l in range(2)]

        def raw(b, cols=256):
            return WR[:, b, 0:KD * 256].rearrange("p (k c) -> p k c", c=256)

        def slot_free(sp, s):
            sp.wait_ge(w_split.sem, s + 1)

        def load_cols(sp, s, b, w, col):
            slot_free(sp, s)
            for j in range(2):
                sp.dma_start(raw(b)[:, 4 * j:4 * j + 4, :],
                             w[:, 4 * j:4 * j + 4, bass.ds(col, 256)]).then_inc(w_raw[b], 16)

        def load_up(sp, s, b, w, m):
            slot_free(sp, s)
            for j in range(2):
                sp.dma_start(raw(b)[:, :, j * P:(j + 1) * P],
                             w[:, :, bass.ds(m * P + j * FF, P)]).then_inc(w_raw[b], 16)

        def load_down(sp, s, b, w, m, half):
            slot_free(sp, s)
            dst = WR[:, b, 0:KH * P].rearrange("p (k c) -> p k c", c=P)
            for lo, hi in ((0, 5), (5, KH)):
                sp.dma_start(dst[:, lo:hi, :],
                             w[:, half * KH + lo:half * KH + hi, bass.ds(m * P, P)]).then_inc(w_raw[b], 16)

        def sp_cols(sp, name, w, trips):
            with sp.Fori(0, trips) as t:
                for j in range(2):
                    load_cols(sp, t * 2 + S0[name] + j, (S0[name] + j) % 2, w, t * 512 + j * 256)

        def sp_up(sp, name, w):
            with sp.Fori(0, KF // 2) as t:
                for j in range(2):
                    load_up(sp, t * 2 + S0[name] + j, (S0[name] + j) % 2, w, t * 2 + j)

        def sp_down(sp, name, w):
            with sp.Fori(0, KD) as t:
                for half in range(2):
                    load_down(sp, t * 2 + S0[name] + half, (S0[name] + half) % 2, w, t, half)

        def gemm_tile(pe, src, k0, nk, b, first_col, step, par, first, last, ready=None):
            for kk in range(nk):
                if ready is not None:
                    pe.wait_ge(ready[0].sem, ready[1] + k0 + kk + 1)
                c = kk * step + first_col
                wh, wl = WH[:, b, c:c + P], WL[:, b, c:c + P]
                for hf in range(2):
                    cols = slice(hf * HALF, (hf + 1) * HALF)
                    xh, xl = src[:, k0 + kk, 0, cols], src[:, k0 + kk, 1, cols]
                    for n, (w, x) in enumerate(((wh, xh), (wh, xl), (wl, xh))):
                        mm = pe.matmul(PG[:, par, hf, 0:HALF], w, x,
                                       start=(first and kk == 0 and n == 0),
                                       stop=(last and kk == nk - 1 and n == 2))
            return mm

        def pe_wide(pe, name, src, trips, ready, tail=False):
            def body(t, slots, tiles_of):
                for j in range(slots):
                    s, b = t * 2 + S0[name] + j, (S0[name] + j) % 2
                    pe.wait_ge(w_split.sem, s + 3)
                    for c in range(tiles_of):
                        u, par = t * 4 + U0[name] + 2 * j + c, (U0[name] + c) % 2
                        pe.wait_ge(tile_out.sem, u + 1)
                        tile_done.on(gemm_tile(pe, src, 0, KD, b, c * P, 256, par, True, True,
                                               ready if j == 0 and c == 0 else None))
            with loop(pe, trips, [(tile_done, 4)]) as t:
                body(t, 2, 2)
            if tail:
                body(trips, 1, 1)

        def pe_down(pe, name, ready):
            with loop(pe, KD // 2, [(tile_done, 2), (half_used, 2)]) as t:
                for c in range(2):
                    u, par = t * 2 + U0[name] + c, (U0[name] + c) % 2
                    pe.wait_ge(tile_out.sem, u + 1)
                    for half in range(2):
                        s, b = t * 4 + S0[name] + 2 * c + half, (S0[name] + half) % 2
                        pe.wait_ge(w_split.sem, s + 3)
                        mm = gemm_tile(pe, G, half * KH, KH, b, 0, P, par, half == 0, half == 1,
                                       ready if c == 0 else None)
                        (tile_done if half else half_used).on(mm)

        def pe_stat(pe, i):
            pe.wait_ge(acc_ok.sem, 9 * i + 9)
            for hf in range(2):
                mm = pe.matmul(M[:, hf, 0:HALF], ONES, ACC[:, hf * HALF:(hf + 1) * HALF], start=True, stop=True)
            st_done.on(mm)

        N_SMALL = 11

        def plain(act):
            act.sem_inc(passed, 1)

        def split_hi(act, b, raw_count, freed=None):
            act.wait_ge(w_raw[b], raw_count)
            if freed is not None:
                act.wait_ge(freed[0].sem, freed[1])
            plain(act)
            w_hi.on(act.activation(WH[:, b, :], WR[:, b, :], ACT.Copy))

        def split_next_wide(act, name, t, j):
            b = (S0[name] + j + 1) % 2
            count = raw_of(name, 2 * t + j + 1) if isinstance(t, int) else t * 32 + raw_of(name, j + 1)
            split_hi(act, b, count, (tile_done, t * 4 + U0[name] + 2 * j))

        def split_next_down(act, name, t, j):
            b = (S0[name] + j + 1) % 2
            n = 8 * (name == "down1")
            freed = (tile_done, t * 2 + U0[name] + j // 2) if j % 2 == 0 else \
                (half_used, t * 2 + n + j // 2 + 1)
            count = raw_of(name, 4 * t + j + 1) if isinstance(t, int) else t * 64 + raw_of(name, j + 1)
            split_hi(act, b, count, freed)

        def res_act(act, i, m, gcol, par, new_x):
            act.wait_ge(*new_x)
            plain(act)
            if i < 4:
                a_hi.on(act.activation(H[:, one(m), 0, :], XT[:, one(m), :], ACT.Copy,
                                       scale=GAINS[:, bass.ds(m + gcol, 1)]))
            if not (i == 0 and m == 0):
                act.wait_ge(acc_ok.sem, m + 9 * i)
            plain(act)
            a_sq.on(act.activation(SQ[:, par, :], XT[:, one(m), :].rearrange("p a c -> p (a c)"), ACT.Square))

        def res_dve(dve, i, m, gcol, par, done):
            r = m + 8 * i
            if i < 4:
                dve.wait_ge(a_hi.sem, r + 1)
                dve.wait_ge(*done)
                h_ready.on(dve.scalar_tensor_tensor(
                    out=row2(H, m, 1), in0=row1(XT, m), scalar=GAINS[:, bass.ds(m + gcol, 1)],
                    in1=row2(H, m, 0).bitcast(F32), op0=ALU.mult, op1=ALU.subtract))
            dve.wait_ge(a_sq.sem, r + 1)
            dve.wait_ge(acc_ok.sem, acc_ok.now)
            acc_ok.on(dve.tensor_tensor(ACC[:, :], ACC[:, :], SQ[:, par, :], ALU.add))

        def row1(x, m):
            return x[:, one(m), :].rearrange("p a c -> p (a c)")

        def row2(x, m, part):
            return x[:, one(m), part, :].rearrange("p a c -> p (a c)")

        def norm_act(act, i):
            act.wait_ge(st_done.sem, i + 1)
            a_std.on(act.activation(halves(RSTD[:, :]), M[:, 0:2, 0:HALF], ACT.Sqrt, bias=EPSC, scale=1.0 / D))

        def norm_dve(dve, i):
            dve.wait_ge(a_std.sem, i + 1)
            rstd_ok.on(dve.reciprocal(RSTD[:, :], RSTD[:, :]))
            acc_ok.on(dve.memset(ACC[:, :], 0.0))
            dve.wait_ge(rstd_ok.sem, rstd_ok.now)

        def dve_project(dve, name, trips, tail=False, first=0):
            def drain(m, c):
                dve.wait_ge(tile_done.sem, m + U0[name] + 1)
                tile_out.on(dve.tensor_tensor(row(P0, m + first), sets((U0[name] + c) % 2), halves(RSTD[:, :]), ALU.mult))
            with loop(dve, trips, [(tile_out, 4)]) as t:
                for c in range(4):
                    drain(t * 4 + c, c)
            if tail:
                drain(4 * trips, 0)

        def dve_residual(dve, name, i, gcol, per):
            with loop(dve, KD // per, [(tile_out, per), (acc_ok, per)] + [(h_ready, per)] * (i < 4)) as t:
                for c in range(per):
                    m = t * per + c
                    dve.wait_ge(tile_done.sem, m + U0[name] + 1)
                    tile_out.on(dve.tensor_tensor(row(XT, m), row(XT, m), sets((U0[name] + c) % 2), ALU.add))
                    res_dve(dve, i, m, gcol, c % 2, (tile_out.sem, tile_out.now))

        def act_residual(act, name, i, gcol, per, final=False):
            def body(t, last):
                for c in range(per):
                    m = t * per + c
                    if name.startswith("out"):
                        if c % 2 == 0:
                            split_next_wide(act, name, t, c // 2)
                    else:
                        split_next_down(act, name, t, 2 * c)
                        if not (last and c == per - 1):
                            split_next_down(act, name, t, 2 * c + 1)
                    res_act(act, i, m, gcol, c % 2, (tile_out.sem, m + U0[name] + 3))
            trips = KD // per
            if name == "out1":
                for t in range(trips):
                    body(t, False)
                return
            peel = final or name == "down0"
            with loop(act, trips - peel, [(w_hi, per // 2 if name.startswith("out") else 2 * per), (a_sq, per)]
                      + [(a_hi, per)] * (i < 4)) as t:
                body(t, False)
            if peel:
                body(trips - 1, final)

        def dve_up(dve, name, l):
            def body(t, j):
                m = t * 2 + j
                ua = m * 2 + U0[name]
                dve.wait_ge(tile_done.sem, ua + 1)
                tile_out.on(dve.tensor_tensor(halves(TA[:, j, :]), sets(U0[name] % 2), halves(RSTD[:, :]), ALU.mult))
                dve.wait_ge(tile_done.sem, ua + 2)
                tile_out.on(dve.tensor_tensor(halves(TB[:, :]), sets((U0[name] + 1) % 2), halves(RSTD[:, :]), ALU.mult))
                dve.wait_ge(a_silu.sem, m + KF * l + 1)
                dve.wait_ge(tile_out.sem, tile_out.now)
                t_gate.on(dve.tensor_tensor(TG[:, j, :], TA[:, j, :], TB[:, :], ALU.mult))
                dve.wait_ge(a_ghi.sem, m + KF * l + 1)
                dve.wait_ge(t_gate.sem, t_gate.now)
                g_ready.on(dve.tensor_tensor(row2(G, m, 1), TG[:, j, :], row2(G, m, 0).bitcast(F32), ALU.subtract))
            with loop(dve, KF // 2, [(tile_out, 4), (t_gate, 2), (g_ready, 2)]) as t:
                for j in range(2):
                    body(t, j)

        def act_up(act, name, l):
            with loop(act, KF // 2, [(w_hi, 2), (a_silu, 2), (a_ghi, 2)]) as t:
                for j in range(2):
                    m = t * 2 + j
                    split_next_wide(act, name, t, j)
                    act.wait_ge(tile_out.sem, m * 2 + U0[name] + 3)
                    plain(act)
                    a_silu.on(act.activation(TA[:, j, :], TA[:, j, :], ACT.Silu))
                    act.wait_ge(t_gate.sem, m + KF * l + 1)
                    plain(act)
                    a_ghi.on(act.activation(row2(G, m, 0), TG[:, j, :], ACT.Copy))

        PAIRS = [(gp, i) for gp in range(2) for i in range(QT)]
        UNITS = [(gp, i, e) for gp, i in PAIRS for e in range(2)]
        STEPS = [(gp, i, e, br) for gp, i, e in UNITS for br in range(2)]
        Q_GATE, Q_TOK = 0, 2
        Q_CMP = Q_TOK + 3 * (QT + 1)
        Q_CV = Q_CMP + 2 * (NS + 1)
        Q_ATT = Q_CV + 2
        q_unit, q_step, q = [], [], Q_ATT
        for _, i, _ in UNITS:
            q_unit.append(q)
            q += 1
            for _ in range(2):
                q_step.append(q)
                q += i + 1
        Q_SMP = q
        KV_TILE = (12, 16)

        def q_wait_drained(eng, q):
            if q % 2 == 0:
                eng.wait_ge(q_v.sem, q // 2 + 1)
            else:
                eng.wait_ge(q_a.sem, q // 2 + 1)

        def q_bank(pe, q):
            if q >= 2:
                q_wait_drained(pe, q - 2)
            return M[:, q % 2, :]

        def drains(eng, mine, q, copies, after=()):
            if q % 2 != mine:
                return
            eng.wait_ge(q_fill.sem, q + 1)
            for s, v in after:
                eng.wait_ge(s, v)
            for dst, src in copies:
                ins = eng.activation(dst, src, ACT.Copy) if mine else eng.tensor_copy(dst, src)
            (q_a if mine else q_v).on(ins)

        def drain_tokens(eng, mine, q0, rows, i):
            for b in range(3):
                src = M[0:rows, (q0 + b) % 2, :]
                copies = [(KVO[0:rows, b * 512:(b + 1) * 512], src)]
                if b:
                    dst = VTK[:, i, b - 1, :] if i < QT else VN[:, b - 1, :]
                    copies.append((dst, src[:, 256:512]))
                drains(eng, mine, q0 + b, copies, [(d_kv, 32 * i)] if i else [])

        def drain_setup(eng, mine):
            for i in range(QT):
                drain_tokens(eng, mine, Q_TOK + 3 * i, P, i)
            drain_tokens(eng, mine, Q_TOK + 3 * QT, NS, QT)

        def drain_cmp(eng, mine, kv):
            if kv:
                eng.wait_ge(cmp_done.sem, 1)
            for n in range(NS):
                q = Q_CMP + (NS + 1) * kv + n
                src = M[:, q % 2, :].rearrange("p (g s r) -> p g s r", g=2, r=16)
                copies = [(CT[:, :, g * P + n * 16:g * P + n * 16 + 16], src[:, g].rearrange("p s r -> p r s"))
                          for g in range(2)]
                drains(eng, mine, q, copies)
            q = Q_CMP + (NS + 1) * kv + NS
            drains(eng, mine, q, [(CT[:, :, NCOL - 2:NCOL], M[:, q % 2, 0:32].rearrange("p (h r) -> p r h", h=2))])

        def drain_cv(eng, mine):
            drains(eng, mine, Q_CV, [(CVK[:, :, :].rearrange("c g d -> c (g d)"), M[0:NC, Q_CV % 2, 0:2 * P])])
            drains(eng, mine, Q_CV + 1, [(CVS[:, :, :].rearrange("c g d -> c (g d)"), M[:, (Q_CV + 1) % 2, 0:2 * P])])

        def sp_layer1(sp):
            with sp.Fori(0, 2) as t:
                for j in range(2):
                    b = (S0["inq"] + j) % 2
                    slot_free(sp, t * 2 + S0["inq"] + j)
                    for jj in range(2):
                        for e in range(2):
                            sp.dma_start(raw(b)[:, :, jj * P + e * HD:jj * P + (e + 1) * HD],
                                         w1[:, :, bass.ds(t * 512 + 256 * e + P * j + HD * jj, HD)]
                                         ).then_inc(w_raw[b], 16)
            with sp.Fori(0, 3) as t:
                for j in range(2):
                    load_cols(sp, t * 2 + S0["in1"] + j, (S0["in1"] + j) % 2, w1, t * 512 + D + j * 256)
            s = S0["in1"] + 6
            slot_free(sp, s)
            for j in range(2):
                sp.dma_start(raw(s % 2)[:, 4 * j:4 * j + 4, 0:P],
                             w1[:, 4 * j:4 * j + 4, 2480:2608]).then_inc(w_raw[s % 2], 16)
            load_out1(sp, 0)
            load_out1(sp, 1)
            sp.wait_ge(g_ready.sem, 8 + KF)
            sp.wait_ge(tile_done.sem, U0["inq"])
            sp.dma_start(CA[:, :], a["c_att"]).then_inc(d_ca, 16)
            sp.wait_ge(rstd_ok.sem, 3)
            sp.dma_start(SQ[:, 0, 0:P], a["c_causal"]).then_inc(d_ca, 16)
            sp.dma_start(PTAB[:, :], a["page_table"].rearrange("n g -> (n g)").rearrange("(o x) -> o x", o=1)
                         ).then_inc(d_pt, 16)
            for e in range(2):
                for kv in range(2):
                    sp.dma_start(PEK[:, kv, e, :], a["pe_cmp"][kv]).then_inc(d_pe, 16)
            sp.wait_ge(d_pt, 16)
            for x in range(NSTG):
                load_page(sp, x)
            sp.wait_ge(tile_done.sem, U0["out1"])
            for kk in range(2):
                for e in range(2):
                    r = slice(e * HD, (e + 1) * HD)
                    sp.dma_start(WBD[r, kk, :, r], a["w_cmp"][kk].rearrange("l d e -> d l e")).then_inc(d_wc, 16)
            for i in range(QT + 1):
                for b in range(3):
                    q_wait_drained(sp, Q_TOK + 3 * i + b)
                n = P if i < QT else NS
                kv = out[5][0, i * P:(i + 1) * P] if i < QT else out[6][:, 0]
                win = out[7][0, i * P:(i + 1) * P] if i < QT else out[8][:, 0]
                sp.dma_start(kv.rearrange("n a g d -> n (a g d)"), KVO[0:n, 0:1024]).then_inc(d_kv, 16)
                sp.dma_start(win.rearrange("n a g d -> n (a g d)"), KVO[0:n, 1024:1536]).then_inc(d_kv, 16)
            for x in range(NSTG, 2 * NS):
                sp.wait_ge(q_fill.sem, q_of_page(x - NSTG) + 1)
                load_page(sp, x)
            sp.wait_ge(q_a.sem, 1)
            sp.dma_start(GS[:, :], SGT[:, :]).then_inc(d_gs, 16)
            sp.wait_ge(pv_done.sem, Q_SMP - Q_ATT)
            sp.wait_ge(o_out.sem, len(UNITS))
            sp.wait_ge(d_kv, 32 * (QT + 1))
            sp.dma_start(CS[:, :], a["c_smp"]).then_inc(d_cs, 16)
            for br in range(2):
                for n in range(NS):
                    if br:
                        sp.wait_ge(spv_done.sem, 1)
                    for g in range(NPAGE):
                        if br == 0:
                            page = sp.value_load(PTAB[0:1, n * NPAGE + g:n * NPAGE + g + 1], min_val=0, max_val=N_PHYS - 1)
                            src = a["cache_kv"][bass.ds(page, 1), :, 2:4, :, :].rearrange("a p b g d -> p (a b g d)")
                        else:
                            src = a["cache_win"][n, g * P:(g + 1) * P].rearrange("p b g d -> p (b g d)")
                        sp.dma_start(KVS[:, n, g, :], src).then_inc(d_kvs[n], 16)
            sp.wait_ge(d_kv, 32 * (QT + 1))

        def load_page(sp, x):
            kv, n = x // NS, x % NS
            for g in range(NPAGE):
                page = sp.value_load(PTAB[0:1, n * NPAGE + g:n * NPAGE + g + 1], min_val=0, max_val=N_PHYS - 1)
                sp.dma_start(PST[:, x % NSTG, g, :],
                             a["cache_kv"][bass.ds(page, 1), :, kv, :, :].rearrange("a p g d -> p (a g d)")
                             ).then_inc(d_page[x % NSTG], 16)

        def q_of_page(x):
            return Q_CMP + (NS + 1) * (x // NS) + x % NS

        def load_out1(sp, m):
            s = S0["out1"] + m
            slot_free(sp, s)
            for e in range(2):
                for g in range(2):
                    sp.dma_start(WR[e * HD:(e + 1) * HD, s % 2, g * 1024:(g + 1) * 1024].rearrange("d (j c) -> d j c", j=4),
                                 wo1[g, :, e, :, m * 256:(m + 1) * 256].rearrange("j d c -> d j c")
                                 ).then_inc(w_raw[s % 2], 16)

        def sp_cols_out1(sp):
            load_out1(sp, 2)
            load_out1(sp, 3)

        def pool_layer1(pool):
            def clear(x):
                if at_g.n:
                    pool.wait_ge(at_g.sem, at_g.now)
                at_g.on(pool.memset(x, 0.0))
            pool.wait_ge(w_split.sem, 2 + S0["out1"] + 1)
            pool.wait_ge(tile_done.sem, U0["inq"])
            clear(CT[:, :, NCOL:SEGS])
            pool.wait_ge(tile_done.sem, U0["out1"])
            clear(WBD[0:HD, :, :, HD:P])
            clear(WBD[HD:P, :, :, 0:HD])
            pool.wait_ge(g_ready.sem, 8 + KF)
            clear(CKP[0:HD, :, 1, :])
            clear(CKP[HD:P, :, 0, :])
            pool.wait_ge(cmp_done.sem, 2)
            clear(KP[0:HD, :, 1:NKV:2, :])
            clear(KP[HD:P, :, 0:NKV:2, :])
            pool.wait_ge(s_done.sem, 4 * len(STEPS))
            pool.wait_ge(qs_ok.sem, 1)
            clear(QPD[:, :, :, :])
            clear(Q2[:, :, :, :])
            clear(PTP[:, :, :, :])

        def rope_pe(pe, r, m):
            pe.wait_ge(tile_out.sem, U0["out1"] + 2)
            if r >= 2:
                pe.wait_ge(rope_in.sem, r - 1)
            for hf in range(2):
                mm = pe.matmul(PG[:, r % 2, hf, 0:HALF], ROT, P0[:, m, hf * HALF:(hf + 1) * HALF], start=True, stop=True)
            rope_p.on(mm)

        def rope_dve(dve, r, m, dst):
            dve.wait_ge(rope_p.sem, r + 1)
            rope_in.on(dve.tensor_tensor(halves(SQ[:, r % 2, :]), sets(r % 2), halves(SIN), ALU.mult))
            vec.on(dve.tensor_tensor(dst, P0[:, m, :], COS, ALU.mult))
            dve.wait_ge(rope_in.sem, rope_in.now)
            dve.wait_ge(vec.sem, vec.now)
            rope_ok.on(dve.tensor_tensor(dst, dst, SQ[:, r % 2, :], ALU.add))

        ROPE_K = (12, 13, 16, 17)

        def pe_attention(pe):
            pe.wait_ge(d_ca, 32)
            for r, m in enumerate(ROPE_K):
                rope_pe(pe, r, m)
            bank = q_bank(pe, Q_GATE)
            for i in range(QT):
                mm = pe.transpose(bank[:, i * P:(i + 1) * P], P0[:, 20, i * P:(i + 1) * P], IDENT)
            q_fill.on(mm)
            q_fill.on(pe.transpose(q_bank(pe, Q_GATE + 1)[0:NS, 0:P], P0[:, 20, SEQ:T], IDENT))
            pe.wait_ge(rope_ok.sem, 4)
            for i in range(QT + 1):
                rows, cols = (P, slice(i * P, (i + 1) * P)) if i < QT else (NS, slice(SEQ, T))
                for b in range(3):
                    bank = q_bank(pe, Q_TOK + 3 * i + b)
                    for c in range(4):
                        mm = pe.transpose(bank[0:rows, c * P:(c + 1) * P], P0[:, 8 + 4 * b + c, cols], IDENT)
                    q_fill.on(mm)
            for kv in range(2):
                for n in range(NS):
                    x = kv * NS + n
                    bank = q_bank(pe, q_of_page(x))
                    pe.wait_ge(d_page[x % NSTG], 32 * (x // NSTG + 1))
                    for gp in range(2):
                        for kt in range(NPAGE):
                            c = (2 * gp + kt) * P
                            mm = pe.transpose(bank[:, c:c + P], PST[:, x % NSTG, kt, gp * P:(gp + 1) * P], IDENT)
                    q_fill.on(mm)
                bank = q_bank(pe, Q_CMP + (NS + 1) * kv + NS)
                pe.wait_ge(d_pe, 64)
                q_fill.on(pe.transpose(bank[:, 0:32], PEK[:, kv, :, :].rearrange("l e d -> l (e d)"), IDENT[0:32, 0:32]))
                q_wait_drained(pe, Q_CMP + (NS + 1) * kv + NS)
                q_wait_drained(pe, Q_CMP + (NS + 1) * kv + NS - 1)
                pe.wait_ge(ct_prompt.sem, kv + 1)
                pe.wait_ge(d_wc, 64)
                pe.wait_ge(at_g.sem, 3)
                if kv:
                    pe.wait_ge(ck_ok.sem, 1)
                for l in range(32):
                    h = l // 16
                    mm = pe.matmul(M[:, 3, 0:NCOL], WBD[:, kv, l, :], CT[:, l % 16, h:h + NCOL],
                                   start=l == 0, stop=l == 31)
                cmp_done.on(mm)
            bank = q_bank(pe, Q_CV)
            pe.wait_ge(ck_ok.sem, 2)
            for gp in range(2):
                mm = pe.transpose(bank[0:NC, gp * P:(gp + 1) * P], CVT[:, 256 + gp * NC:256 + (gp + 1) * NC], IDENT)
            q_fill.on(mm)
            bank = q_bank(pe, Q_CV + 1)
            for gp in range(2):
                mm = pe.transpose(bank[:, gp * P:(gp + 1) * P], CVT[:, gp * P:(gp + 1) * P], IDENT)
            q_fill.on(mm)
            for m in range(KD):
                rope_pe(pe, 4 + m, m)
            pe.wait_ge(rope_ok.sem, 4 + KD)
            pe.wait_ge(kp_ok.sem, 1)
            pe.wait_ge(at_g.sem, 7)

            def cmp_scores(cu):
                gp, i = PAIRS[cu]
                if cu:
                    pe.wait_ge(cs_out.sem, cu)
                for j in range(4):
                    mm = pe.matmul(M[:, 3, j * 2 * NC:(j + 1) * 2 * NC], P0[:, gp * 4 + j, i * P:(i + 1) * P],
                                   CKP[:, gp, :, :].rearrange("p e c -> p (e c)"), start=True, stop=True)
                cs_done.on(mm)

            def scores(hu):
                gp, i, e, br = STEPS[hu]
                n = (i + 1) * P
                for j in range(4):
                    if hu:
                        pe.wait_ge(exp_done.sem, 4 * (hu - 1) + j + 1)
                    bank = PG[:, j // 2, j % 2, :]
                    pe.matmul(bank[:, 0:n], QR[:, gp * 4 + j, i * P:(i + 1) * P], KP[:, br, 2 * gp + e, 0:n],
                              start=True, stop=False)
                    s_done.on(pe.matmul(bank[:, n - P:n], CBF[:, 0:P], CBF[:, P:2 * P], start=False, stop=True))

            def pv(q, lhsT, rows, first, last):
                q_wait_drained(pe, q)
                pv_done.on(pe.matmul(M[:, 2, :], lhsT, PT[0:rows, (q - Q_ATT) % 4, :], start=first, stop=last))

            cmp_scores(0)
            scores(0)
            for un, (gp, i, e) in enumerate(UNITS):
                q = q_unit[un]
                bank = q_bank(pe, q)
                pe.wait_ge(c_ready.sem, un // 2 + 1)
                for j in range(4):
                    mm = pe.transpose(bank[0:NC, j * P:(j + 1) * P], TC[:, j, e, :], IDENT)
                q_fill.on(mm)
                if un:
                    pe.wait_ge(o_out.sem, un)
                pv(q, CVK[:, gp, :], NC, True, False)
                for br in range(2):
                    hu = 2 * un + br
                    if hu + 1 < len(STEPS):
                        if (hu + 1) % 4 == 0:
                            cmp_scores((hu + 1) // 4)
                        scores(hu + 1)
                    q = q_step[hu]
                    pe.wait_ge(p_ready.sem, hu + 1)
                    for kt in range(i + 2):
                        if kt <= i:
                            bank = q_bank(pe, q + kt)
                            for j in range(4):
                                mm = pe.transpose(bank[:, j * P:(j + 1) * P], PB[:, hu % 2, j, kt * P:(kt + 1) * P], IDENT)
                            q_fill.on(mm)
                        if kt:
                            pv(q + kt - 1, VTK[:, kt - 1, br, gp * P:(gp + 1) * P], P, False, br == 1 and kt == i + 1)
            pe_samples(pe)

        def pe_samples(pe):
            S, O = PG[:, 0, 0, :], PG[:, 0, 1, :]
            pe.wait_ge(qpd_ok.sem, 1)
            pe.wait_ge(exp_done.sem, 4 * len(STEPS))
            for gp in range(2):
                mm = pe.matmul(S[:, 0:P], Q2[:, 1, gp, :], CKT[:, gp * P:(gp + 1) * P], start=gp == 0, stop=gp == 1)
            ss_done.on(mm)
            q = Q_SMP
            bank = q_bank(pe, q)
            pe.wait_ge(sp_ok.sem, 1)
            q_fill.on(pe.transpose(bank[:, 0:P], PS[:, 0:P], IDENT))
            q_wait_drained(pe, q)
            q_wait_drained(pe, Q_CV + 1)
            sv_done.on(pe.matmul(O[:, 0:256], PTN[:, :], CVS[:, :, :].rearrange("c g d -> c (g d)"), start=True, stop=True))
            for br in range(2):
                q0 = Q_SMP + 1 + (NS + 1) * br
                for n in range(NS + 1):
                    if n < NS:
                        bank = q_bank(pe, q0 + n)
                        pe.wait_ge(d_kvs[n], 32 * (br + 1))
                        for gp in range(2):
                            for kt in range(NPAGE):
                                c = (2 * gp + kt) * P
                                mm = pe.transpose(bank[:, c:c + P], KVS[:, n, kt, gp * P:(gp + 1) * P], IDENT)
                        q_fill.on(mm)
                    if n:
                        q_wait_drained(pe, q0 + n - 1)
                        for gp in range(2):
                            mm = pe.matmul(S[:, 0:256], QPD[:, n - 1, gp, :], KTS[:, (n - 1) % 2, gp, :],
                                           start=n == 1 and gp == 0, stop=n == NS and gp == 1)
                        kts_used.on(mm)
                for gp in range(2):
                    mm = pe.matmul(S[:, 256:264], Q2[:, 0, gp, :], KN[:, br, gp, :], start=gp == 0, stop=gp == 1)
                ss_done.on(mm)
                q = q0 + NS
                bank = q_bank(pe, q)
                pe.wait_ge(sp_ok.sem, br + 2)
                for kt in range(2):
                    pe.transpose(bank[:, kt * P:(kt + 1) * P], PS[:, kt * P:(kt + 1) * P], IDENT)
                q_fill.on(pe.transpose(bank[0:NS, 2 * P:3 * P], PS[:, 256:264], IDENT))
                q_wait_drained(pe, q)
                pe.wait_ge(oa_ok.sem, br + 1)
                for n in range(NS):
                    for kt in range(2):
                        pe.matmul(O[:, 0:256], PTP[:, kt, n, :], KVS[:, n, kt, 256:512], start=n == 0 and kt == 0, stop=False)
                spv_done.on(pe.matmul(O[:, 0:256], PTN[0:NS, :], VN[:, br, :], start=False, stop=True))
            q = Q_SMP + 1 + 2 * (NS + 1)
            bank = q_bank(pe, q)
            pe.wait_ge(om_ok.sem, 1)
            q_fill.on(pe.transpose(bank[:, 0:P], OM[:, :, :].rearrange("p e d -> p (e d)"), IDENT))

        def split_heads(gp, e):
            r = slice(e * HD, (e + 1) * HD)
            return r, slice(gp * 4, gp * 4 + 4), (2 * gp + e) * 4

        def dve_attention(dve):
            dve.wait_ge(d_ca, 32)
            dve.tensor_copy(CBF[:, 0:P], IDENT)
            vec.on(dve.tensor_copy(CBF[:, P:2 * P], SQ[:, 0, 0:P]))
            dve.wait_ge(vec.sem, vec.now)
            for r, m in enumerate(ROPE_K):
                rope_dve(dve, r, m, P0[:, m, :])
            dve.wait_ge(q_fill.sem, Q_GATE + 1)
            q_v.on(dve.tensor_copy(GT[:, :, :], M[:, Q_GATE % 2, :].rearrange("p (i c) -> p i c", i=QT)[:, :, 80:128]))
            dve.wait_ge(rope_ok.sem, 4)
            for br in range(2):
                for gp in range(2):
                    kn = dve.tensor_copy(KN[:, br, gp, :], P0[:, KV_TILE[br] + gp, SEQ:T])
            vec.on(kn)
            drain_setup(dve, 0)
            for kv in range(2):
                if kv:
                    dve.wait_ge(cmp_done.sem, 1)
                for gp in range(2):
                    c = dve.tensor_copy(CT[:, :, 256 + gp * NC:256 + (gp + 1) * NC],
                                        P0[:, 8 + 2 * kv + gp, 0:SEQ].rearrange("p (s r) -> p r s", r=16))
                ct_prompt.on(c)
                drain_cmp(dve, 0, kv)
                dve.wait_ge(cmp_done.sem, kv + 1)
                vec.on(dve.tensor_copy(ST8[:, 0:1], M[:, 3, NCOL - 2:NCOL - 1]))
                dve.wait_ge(vec.sem, vec.now)
                ck_ok.on(dve.tensor_scalar((CKT, CVT)[kv][:, :], M[:, 3, 0:NCOL], ST8[:, 0:1], None, ALU.add))
            dve.wait_ge(ck_ok.sem, 2)
            drain_cv(dve, 0)
            for gp in range(2):
                for e in range(2):
                    r = slice(e * HD, (e + 1) * HD)
                    dve.tensor_copy(CKP[r, gp, e, :], CKT[r, 256 + gp * NC:256 + (gp + 1) * NC])
                    for br in range(2):
                        c = dve.tensor_copy(KP[r, br, 2 * gp + e, :], P0[r, KV_TILE[br] + gp, 0:SEQ])
            kp_ok.on(c)
            for m in range(KD):
                rope_dve(dve, 4 + m, m, QR[:, m, :])
            dve.wait_ge(rope_ok.sem, 4 + KD)
            qs_ok.on(dve.tensor_copy(QS[:, :, :], QR[:, :, SEQ:T]))
            MX, NB, SUM, F, CM = (ST8[:, 8 * n:8 * n + 8] for n in range(5))
            CX = ST8[:, 40:48]

            def bias01(base, i):
                return CA[:, base + i * NC:base + (i + 1) * NC].unsqueeze(1).to_broadcast([P, 8, NC])

            TC8 = TC[:, :, :, :].rearrange("p j e c -> p (j e) c")

            def chain(ins):
                vec.on(ins)
                dve.wait_ge(vec.sem, vec.now)

            def cmp_max(cu):
                gp, i = PAIRS[cu]
                dve.wait_ge(cs_done.sem, cu + 1)
                if cu:
                    dve.wait_ge(q_fill.sem, q_unit[2 * cu - 1] + 1)
                cs_out.on(dve.scalar_tensor_tensor(
                    out=TC8, in0=M[:, 3, 0:8 * NC].rearrange("p (x c) -> p x c", c=NC), scalar=SCALE,
                    in1=bias01(C_CB, i), op0=ALU.mult, op1=ALU.add))
                dve.wait_ge(cs_out.sem, cs_out.now)
                chain(dve.tensor_reduce(CM, TC8, AX.X, ALU.max))
                c_max.on(dve.tensor_tensor(TC8, TC8, CM.unsqueeze(2).to_broadcast([P, 8, NC]), ALU.subtract))

            def cmp_probs(cu):
                gp, i = PAIRS[cu]
                dve.wait_ge(c_exp.sem, cu + 1)
                chain(dve.tensor_tensor(TC8, TC8, bias01(C_CV, i), ALU.mult))
                chain(dve.tensor_reduce(CX, TC8, AX.X, ALU.add))
                chain(dve.tensor_scalar(CX, CX, 1e-30, None, ALU.max))
                chain(dve.reciprocal(CX, CX))
                g = GT[:, i, :].rearrange("p (g j b) -> p g j b", g=NKV, b=3)[:, 2 * gp:2 * gp + 2, :, 0]
                chain(dve.tensor_tensor(CX.rearrange("p (j e) -> p e j", e=2), CX.rearrange("p (j e) -> p e j", e=2),
                                        g, ALU.mult))
                c_ready.on(dve.tensor_tensor(TC8, TC8, CX.unsqueeze(2).to_broadcast([P, 8, NC]), ALU.mult))

            def row_max(hu):
                gp, i, e, br = STEPS[hu]
                o = 4 * (hu % 2)
                for j in range(4):
                    dve.wait_ge(s_done.sem, 4 * hu + j + 1)
                    c = dve.tensor_reduce(MX[:, o + j:o + j + 1], PG[:, j // 2, j % 2, 0:(i + 1) * P], AX.X, ALU.max)
                chain(c)
                nb_ok.on(dve.tensor_scalar(NB[:, o:o + 4], MX[:, o:o + 4], -SCALE, None, ALU.mult))

            def scale_probs(hu):
                gp, i, e, br = STEPS[hu]
                o = 4 * (hu % 2)
                dve.wait_ge(exp_done.sem, 4 * hu + 4)
                chain(dve.reciprocal(F[:, o:o + 4], SUM[:, o:o + 4]))
                g = GT[:, i, :].rearrange("p (g j b) -> p g j b", g=NKV, b=3)[:, 2 * gp + e, :, 1 + br]
                chain(dve.tensor_tensor(F[:, o:o + 4], F[:, o:o + 4], g, ALU.mult))
                for j in range(4):
                    pj = PB[:, hu % 2, j, 0:(i + 1) * P]
                    c = dve.tensor_scalar(pj, pj, F[:, o + j:o + j + 1], None, ALU.mult)
                p_ready.on(c)

            dve.wait_ge(gt_ok.sem, 1)
            cmp_max(0)
            row_max(0)
            cmp_probs(0)
            for un, (gp, i, e) in enumerate(UNITS):
                drain_pt(dve, 0, q_unit[un], NC)
                for br in range(2):
                    hu = 2 * un + br
                    if hu + 1 < len(STEPS):
                        new_pair = (hu + 1) % 4 == 0
                        if new_pair:
                            cmp_max((hu + 1) // 4)
                        row_max(hu + 1)
                    scale_probs(hu)
                    for kt in range(i + 1):
                        drain_pt(dve, 0, q_step[hu] + kt, P)
                    if hu + 1 < len(STEPS) and new_pair:
                        cmp_probs((hu + 1) // 4)
                r = slice(e * HD, (e + 1) * HD)
                dve.wait_ge(o_hi.sem, un + 1)
                o_out.on(dve.tensor_tensor(
                    G[r, gp * 4:gp * 4 + 4, 1, i * P:(i + 1) * P], M[r, 2, :].rearrange("p (j q) -> p j q", j=4),
                    G[r, gp * 4:gp * 4 + 4, 0, i * P:(i + 1) * P].bitcast(F32), ALU.subtract))
            dve_samples(dve, chain)

        def drain_pt(eng, mine, q, rows):
            x = q - Q_ATT
            drains(eng, mine, q, [(PT[0:rows, x % 4, :], M[0:rows, q % 2, :])], [(pv_done.sem, x - 3)] if x >= 4 else [])

        def dve_samples(dve, chain):
            MXS, NBS, SMS, FS = (ST8[:, n:n + 1] for n in range(4))
            S, O = PG[:, 0, 0, :], PG[:, 0, 1, :]
            dve.wait_ge(at_g.sem, 10)
            for gp in range(2):
                for e in range(2):
                    r, tiles, row0 = split_heads(gp, e)
                    for rot, src in ((0, QS[r, tiles, :]), (1, P0[r, tiles, SEQ:T])):
                        q2 = Q2[r, rot, gp, :].rearrange("p (n h) -> p h n", h=16)[:, row0:row0 + 4, :]
                        c = dve.tensor_copy(q2, src)
                    for n in range(NS):
                        c = dve.tensor_copy(QPD[r, n, gp, n * 16 + row0:n * 16 + row0 + 4], QS[r, tiles, n])
            qpd_ok.on(c)
            for n in range(3):
                w, base = (P, 264) if n == 0 else (264, 0)
                if n:
                    q0 = Q_SMP + 1 + (NS + 1) * (n - 1)
                    for k2 in range(NS):
                        drain_kts(dve, 0, q0, n - 1, k2)
                dve.wait_ge(ss_done.sem, n + 1)
                dve.wait_ge(d_cs, 16)
                chain(dve.scalar_tensor_tensor(out=SCS[:, 0:w], in0=S[:, 0:w], scalar=SCALE, in1=CS[:, base:base + w],
                                               op0=ALU.mult, op1=ALU.add))
                chain(dve.tensor_reduce(MXS, SCS[:, 0:w], AX.X, ALU.max))
                snb_ok.on(dve.tensor_scalar(NBS, MXS, -1.0, None, ALU.mult))
                dve.wait_ge(sp_ok.sem, n + 1)
                dve.wait_ge(d_gs, 16)
                chain(dve.reciprocal(FS, SMS))
                chain(dve.tensor_tensor(FS, FS, GS[:, n:n + 1], ALU.mult))
                drain_p(dve, 0, n)
                if n == 0:
                    dve.wait_ge(sv_done.sem, 1)
                    oa_ok.on(dve.tensor_scalar(OA[:, :], O[:, 0:256], FS, None, ALU.mult))
                else:
                    dve.wait_ge(spv_done.sem, n)
                    dve.wait_ge(oa_ok.sem, oa_ok.now)
                    oa_ok.on(dve.scalar_tensor_tensor(out=OA[:, :], in0=O[:, 0:256], scalar=FS, in1=OA[:, :],
                                                      op0=ALU.mult, op1=ALU.add))
            dve.wait_ge(oa_ok.sem, 3)
            for e in range(2):
                chain(dve.tensor_scalar(OM[:, e, :], OA[:, e * HD:(e + 1) * HD], CS[:, 264 + P + e:264 + P + e + 1],
                                        None, ALU.mult))
                c = dve.scalar_tensor_tensor(
                    out=OM[:, e, :], in0=OA[:, (2 + e) * HD:(3 + e) * HD], scalar=CS[:, 264 + P + 2 + e:264 + P + 3 + e],
                    in1=OM[:, e, :], op0=ALU.mult, op1=ALU.add)
            om_ok.on(c)
            drain_os(dve, 0)
            dve.wait_ge(os_hi.sem, 1)
            q_wait_drained(dve, Q_SMP + 1 + 2 * (NS + 1))
            for m in range(KD):
                g_ready.on(dve.tensor_tensor(G[:, m, 1, SEQ:T], OS[:, m, :], G[:, m, 0, SEQ:T].bitcast(F32), ALU.subtract))

        def drain_kts(eng, mine, q0, br, n):
            x = NS * br + n
            drains(eng, mine, q0 + n, [(KTS[:, n % 2, :, :].rearrange("p g k -> p (g k)"), M[:, (q0 + n) % 2, :])],
                   [(kts_used.sem, x - 1)] if x >= 2 else [])

        def drain_p(eng, mine, n):
            if n == 0:
                drains(eng, mine, Q_SMP, [(PTN[:, :], M[:, Q_SMP % 2, 0:P])], [(at_g.sem, 10)])
                return
            q = Q_SMP + (NS + 1) * n
            src = M[:, q % 2, :]
            copies = [(PTP[:, kt, s, s * 16:(s + 1) * 16], src[:, kt * P + s * 16:kt * P + (s + 1) * 16])
                      for kt in range(2) for s in range(NS)]
            copies.append((PTN[0:NS, :], src[0:NS, 2 * P:3 * P]))
            drains(eng, mine, q, copies, [(spv_done.sem, 1)] if n == 2 else [(sv_done.sem, 1)])

        def drain_os(eng, mine):
            q = Q_SMP + 1 + 2 * (NS + 1)
            src = M[:, q % 2, 0:P].rearrange("p (n h) -> p h n", h=16)
            drains(eng, mine, q, [(OS[r, tiles, :], src[r, row0:row0 + 4, :])
                                  for gp in range(2) for e in range(2) for r, tiles, row0 in (split_heads(gp, e),)])

        def act_attention(act):
            act.wait_ge(q_fill.sem, Q_GATE + 2)
            act.wait_ge(g_ready.sem, 8 + KF)
            q_a.on(act.activation(SGT[:, :], M[0:NS, (Q_GATE + 1) % 2, 80:128], ACT.Sigmoid))
            act.wait_ge(q_v.sem, 1)
            gt_ok.on(act.activation(GT[:, :, :], GT[:, :, :], ACT.Sigmoid))
            drain_setup(act, 1)
            for kv in range(2):
                drain_cmp(act, 1, kv)
            drain_cv(act, 1)
            MX, NB, SUM, F, CM = (ST8[:, 8 * n:8 * n + 8] for n in range(5))

            def cmp_exp(cu):
                act.wait_ge(c_max.sem, cu + 1)
                c_exp.on(act.activation(TC[:, :, :, :], TC[:, :, :, :], ACT.Exp))

            def exps(hu):
                gp, i, e, br = STEPS[hu]
                o, n = 4 * (hu % 2), (i + 1) * P
                act.wait_ge(nb_ok.sem, hu + 1)
                if hu >= 2:
                    act.wait_ge(q_fill.sem, q_step[hu - 2] + STEPS[hu - 2][1] + 1)
                for j in range(4):
                    exp_done.on(act.activation(PB[:, hu % 2, j, 0:n], PG[:, j // 2, j % 2, 0:n], ACT.Exp,
                                               bias=NB[:, o + j:o + j + 1], scale=SCALE,
                                               accum_out=SUM[:, o + j:o + j + 1]))
            cmp_exp(0)
            exps(0)
            for un, (gp, i, e) in enumerate(UNITS):
                drain_pt(act, 1, q_unit[un], NC)
                for br in range(2):
                    hu = 2 * un + br
                    if hu + 1 < len(STEPS):
                        if (hu + 1) % 4 == 0:
                            cmp_exp((hu + 1) // 4)
                        exps(hu + 1)
                    for kt in range(i + 1):
                        drain_pt(act, 1, q_step[hu] + kt, P)
                act.wait_ge(pv_done.sem, q_step[2 * un + 1] + i + 1 - Q_ATT)
                r = slice(e * HD, (e + 1) * HD)
                o_hi.on(act.activation(G[r, gp * 4:gp * 4 + 4, 0, i * P:(i + 1) * P],
                                       M[r, 2, :].rearrange("p (j q) -> p j q", j=4), ACT.Copy))
            act.wait_ge(at_g.sem, 10)
            for n in range(3):
                w = P if n == 0 else 264
                if n:
                    q0 = Q_SMP + 1 + (NS + 1) * (n - 1)
                    for k2 in range(NS):
                        drain_kts(act, 1, q0, n - 1, k2)
                act.wait_ge(snb_ok.sem, n + 1)
                sp_ok.on(act.activation(PS[:, 0:w], SCS[:, 0:w], ACT.Exp, bias=ST8[:, 1:2], scale=1.0,
                                        accum_out=ST8[:, 2:3]))
                drain_p(act, 1, n)
            drain_os(act, 1)
            q_wait_drained(act, Q_SMP + 1 + 2 * (NS + 1))
            os_hi.on(act.activation(G[:, 0:KD, 0, SEQ:T], OS[:, :, :], ACT.Copy))

        G0 = {"out0": 0, "down0": 8, "out1": 8 + KF, "down1": 16 + KF}
        block = ctx.enter_context(nc.Block())
        layer1 = FULL

        @block.sync
        def _(sp):
            sp.dma_start(XL[:, :, :], a["x_prompt"][0].rearrange("(i p) c -> p i c", p=P)).then_inc(d_in, 16)
            sp.dma_start(XS[:, :], a["x_sample"][:, 0, :]).then_inc(d_in, 16)
            sp.dma_start(BASE[:, :], a["c_base"]).then_inc(d_small, 16)
            for r, x in ((0, a["norm_mix"].rearrange("l (k p) -> (l k) p", p=P)),
                         (16, a["norm_ffn"].rearrange("l (k p) -> (l k) p", p=P)),
                         (32, a["norm_final"].rearrange("(k p) -> k p", p=P)),
                         (40, a["conv_w"].rearrange("j (k p) -> (j k) p", p=P)),
                         (52, a["norm_v"].rearrange("(k p) -> k p", p=P))):
                sp.dma_start(GROW[r:r + x.shape[0], :], x).then_inc(d_small, 16)
            sp.dma_start(TRIL[:, :], a["c_tril"]).then_inc(d_small, 16)
            sp.dma_start(SCV[:, :], a["state_conv"].rearrange("n j c -> (n j) c")).then_inc(d_small, 16)
            sp.dma_start(WSP[:, :, :], a["w_spatial"].rearrange("h t s -> t h s")).then_inc(d_small, 16)
            sp.dma_start(BSP[:, :, :].rearrange("p h t -> p (h t)"),
                         a["b_spatial"].rearrange("h t -> (h t)").partition_broadcast(P)
                         ).then_inc(d_small, 16)
            sp.dma_start(W00[:, :, :], a["w_spatial"][:, 0, 0:8].partition_broadcast(P)).then_inc(d_small, 16)
            sp_cols(sp, "in0", w0, 5)
            sp_cols(sp, "out0", wo0, 2)
            sp.dma_start(out[3][:, 0, :], a["state_conv"][:, 1, :]).then_inc(d_out, 16)
            sp.wait_ge(cv_ok.sem, 1)
            sp.dma_start(out[4][:, 0, :], CV[:, :]).then_inc(d_out, 16)
            sp.wait_ge(zo_ok.sem, 1)
            sp.dma_start(out[2][0], ZO[0:2, :]).then_inc(d_out, 16)
            sp.dma_start(out[3][:, 1, :], ZO[2:10, :]).then_inc(d_out, 16)
            outs[0] += 4
            sp_up(sp, "up0", wup[0])
            sp_down(sp, "down0", wdn[0])
            if layer1:
                sp_layer1(sp)
                sp_cols_out1(sp)
                sp_up(sp, "up1", wup[1])
                sp_down(sp, "down1", wdn[1])
            for i in range(QT):
                sp.wait_ge(fin_v.sem, 8 + 2 * (i + 1))
                sp.dma_start(out[0][0, i * P:(i + 1) * P, :], YO[:, i, :]).then_inc(d_out, 16)
                outs[0] += 1
            sp.wait_ge(fin_v.sem, 8 + 10)
            sp.dma_start(out[1][:, 0, :], YS[:, :]).then_inc(d_out, 16)
            outs[0] += 1
            sp.wait_ge(d_out, 16 * outs[0])

        @block.gpsimd
        def _(pool):
            pool.sem_inc(w_split.sem, 2)
            def split_lo(s, b):
                pool.wait_ge(w_hi.sem, s + 1)
                w_split.on(pool.tensor_tensor(WL[:, b, :], WR[:, b, :], WH[:, b, :].bitcast(F32), ALU.subtract))
            def split_slots(s0, n):
                with pool.Fori(0, n // 2) as t:
                    for b in range(2):
                        split_lo(t * 2 + s0 + b, (s0 + b) % 2)
                if n % 2:
                    split_lo(s0 + n - 1, (s0 + n - 1) % 2)
            if not layer1:
                split_slots(0, S0["inq"])
            else:
                split_slots(0, S0["out1"] + 1)
                pool_layer1(pool)
                pool.wait_ge(at_g.sem, at_g.now)
                split_slots(S0["out1"] + 1, _s - S0["out1"] - 1)

        @block.tensor
        def _(pe):
            fills = [0]

            def fill_start():
                if fills[0] >= 4:
                    pe.wait_ge(t_drain.sem, fills[0] - 3)
                return M[:, fills[0] % 4, :]

            def fill_end(mm):
                t_fill.on(mm)
                fills[0] += 1

            pe.wait_ge(d_small, 16 * N_SMALL)
            bank = fill_start()
            fill_end(pe.transpose(bank[:, 0:N_GAIN], GROW[:, :], IDENT[0:N_GAIN, 0:N_GAIN]))
            bank = fill_start()
            for f in range(FT):
                mm = pe.transpose(bank[:, 16 * f:16 * f + 16], SCV[:, f * P:(f + 1) * P], IDENT[0:16, 0:16])
            fill_end(mm)
            bank = fill_start()
            for h in range(4):
                mm = pe.transpose(bank[:, h * P:(h + 1) * P], WSP[:, h, :], IDENT)
            fill_end(mm)
            pe.wait_ge(d_in, 32)
            bank = fill_start()
            for kk in range(KD):
                mm = pe.transpose(bank[:, 8 * kk:8 * kk + 8], XS[:, kk * P:(kk + 1) * P], IDENT[0:NS, 0:NS])
            fill_end(mm)
            for kk in range(KD):
                bank = fill_start()
                for i in range(QT):
                    mm = pe.transpose(bank[:, i * P:(i + 1) * P], XL[:, i, kk * P:(kk + 1) * P], IDENT)
                fill_end(mm)
            pe.wait_ge(t_drain.sem, 12)
            pe_stat(pe, 0)
            pe_wide(pe, "in0", H, 5, (h_ready, 0))
            pe.wait_ge(accv_ok.sem, FT)
            for hf in range(2):
                mm = pe.matmul(M[:, hf, 0:HALF], ONES, ACV[:, hf * HALF:(hf + 1) * HALF], start=True, stop=True)
            stv_done.on(mm)
            for f in range(FT):
                pe.wait_ge(vn_ok.sem, f + 1)
                if f >= 2:
                    pe.wait_ge(vt_drain.sem, f - 1)
                v = P0[:, 16 + f, :]
                pe.transpose(M[0:NS, 0, f * P:(f + 1) * P], v[:, SEQ:T], IDENT)
                for c in range(QT):
                    mm = pe.transpose(M[:, 2 + f % 2, c * P:(c + 1) * P], v[:, c * P:(c + 1) * P], IDENT)
                vt_fill.on(mm)
            pe.wait_ge(z_ok.sem, FT)
            for f in range(FT):
                mm = pe.transpose(M[0:10, 1, f * P:(f + 1) * P], P0[:, 8 + f, SEQ - 2:T], IDENT)
            zo_fill.on(mm)
            pe.wait_ge(vt_drain.sem, FT)
            for f, bank in enumerate((2, 3, 0, 1)):
                if f == 2:
                    pe.wait_ge(cv_ok.sem, 1)
                if f == 3:
                    pe.wait_ge(zo_ok.sem, 1)
                for c in range(QT):
                    mm = pe.matmul(M[:, bank, c * P:(c + 1) * P], VT[:, f, c, :], WT[:, f, :], start=True, stop=True)
                mixed.on(mm)
            pe_wide(pe, "out0", G, 2, (g_ready, G0["out0"]))
            pe_stat(pe, 1)
            pe_wide(pe, "up0", H, KF // 2, (h_ready, 8))
            pe_down(pe, "down0", (g_ready, G0["down0"]))
            pe_stat(pe, 2)
            if layer1:
                pe_wide(pe, "inq", H, 2, (h_ready, 16))
                pe_wide(pe, "in1", H, 3, None, tail=True)
                pe_attention(pe)
                pe_wide(pe, "out1", G, 2, (g_ready, G0["out1"]))
                pe_stat(pe, 3)
                pe_wide(pe, "up1", H, KF // 2, (h_ready, 24))
                pe_down(pe, "down1", (g_ready, G0["down1"]))
                pe_stat(pe, 4)
            pe.wait_ge(fin_v.sem, 8)
            for i in range(QT):
                for hf in range(2):
                    n = 2 * i + hf
                    if n >= 4:
                        pe.wait_ge(fin_v.sem, 8 + n - 3)
                    for kk in range(4):
                        mm = pe.transpose(M[:, n % 4, kk * P:(kk + 1) * P],
                                          XT[:, 4 * hf + kk, i * P:(i + 1) * P], IDENT)
                    fin_p.on(mm)
            for hf in range(2):
                pe.wait_ge(fin_v.sem, 8 + 5 + hf)
                for kk in range(4):
                    mm = pe.transpose(M[0:NS, hf, kk * P:(kk + 1) * P], XT[:, 4 * hf + kk, SEQ:T], IDENT)
                fin_p.on(mm)

        @block.scalar
        def _(act):
            split_hi(act, 0, 32)
            for m in range(KD):
                res_act(act, 0, m, G_MIX[0], m % 2, (t_drain.sem, 5 + m))
            norm_act(act, 0)
            split_hi(act, 1, 32)
            with loop(act, 4, [(w_hi, 2)]) as t:
                for j in (1, 2):
                    s = j + 1
                    split_hi(act, s % 2, t * 32 + 32 * (s // 2 + 1), (tile_done, t * 4 + 2 * j))
            split_hi(act, 0, 32 * 6, (tile_done, 18))
            for f in range(FT):
                act.wait_ge(tile_out.sem, U0["in0"] + 16 + f + 3)
                vg_ok.on(act.activation(P0[:, 16 + f, :], P0[:, 16 + f, :], ACT.Gelu_apprx_tanh))
                act.wait_ge(vg_ok.sem, vg_ok.now)
                if f >= 2:
                    act.wait_ge(accv_ok.sem, f - 1)
                vsq_ok.on(act.activation(SQ[:, f % 2, :], P0[:, 16 + f, :], ACT.Square))
            for f in range(FT):
                ug_ok.on(act.activation(P0[:, 12 + f, :], P0[:, 12 + f, :], ACT.Gelu_apprx_tanh))
            act.wait_ge(stv_done.sem, 1)
            stdv_ok.on(act.activation(halves(ACV[:, :]), M[:, 0:2, 0:HALF], ACT.Sqrt, bias=EPSC, scale=1.0 / DC))
            for f in range(2 * FT):
                act.wait_ge(y_ok.sem, f + 1)
                y_hi.on(act.activation(G[:, f, 0, :], TG[:, f % 2, :], ACT.Copy))
            act_residual(act, "out0", 1, G_FFN[0], 4)
            norm_act(act, 1)
            act_up(act, "up0", 0)
            if not layer1:
                act_residual(act, "down0", 2, G_MIX[1], 2, final=True)
                norm_act(act, 2)
            else:
                act_residual(act, "down0", 2, G_MIX[1], 2)
                norm_act(act, 2)
                for t in range(2):
                    for j in range(2):
                        split_next_wide(act, "inq", t, j)
                with loop(act, 3, [(w_hi, 2)]) as t:
                    for j in range(2):
                        split_next_wide(act, "in1", t, j)
                split_next_wide(act, "in1", 3, 0)
                act_attention(act)
                act_residual(act, "out1", 3, G_FFN[1], 4)
                norm_act(act, 3)
                act_up(act, "up1", 1)
                act_residual(act, "down1", 4, G_FIN, 2, final=True)
                norm_act(act, 4)

        @block.vector
        def _(dve):
            dve.sem_inc(tile_out.sem, 2)
            tile_out.n = 2
            acc_ok.on(dve.memset(ACC[:, :], 0.0))

            def take(n, dst, src):
                dve.wait_ge(t_fill.sem, n + 1)
                return dve.tensor_copy(dst, src)
            t_drain.on(take(0, GAINS[:, :], M[:, 0, 0:N_GAIN]))
            t_drain.on(take(1, HT[:, :, :].rearrange("p f n -> p (f n)"), M[:, 1, 0:64]))
            dve.wait_ge(t_fill.sem, 3)
            t_drain.on(dve.tensor_tensor(WT[:, :, :], M[:, 2, :].rearrange("p (h t) -> p h t", h=4),
                                         TRIL[:, :].unsqueeze(1).to_broadcast([P, 4, P]), ALU.mult))
            t_drain.on(take(3, XT[:, :, SEQ:T], M[:, 3, 0:64].rearrange("p (k n) -> p k n", k=KD)))
            for m in range(KD):
                t_drain.on(take(4 + m, XT[:, m, 0:SEQ], M[:, m % 4, :]))
            for m in range(KD):
                res_dve(dve, 0, m, G_MIX[0], m % 2, (t_drain.sem, 5 + m))
            norm_dve(dve, 0)
            dve_project(dve, "in0", 5)
            for f in range(FT):
                dve.wait_ge(vsq_ok.sem, f + 1)
                if f == 0:
                    accv_ok.on(dve.tensor_copy(ACV[:, :], SQ[:, 0, :]))
                else:
                    dve.wait_ge(accv_ok.sem, f)
                    accv_ok.on(dve.tensor_tensor(ACV[:, :], ACV[:, :], SQ[:, f % 2, :], ALU.add))
            for f in range(FT):
                z_ok.on(dve.tensor_tensor(P0[:, 8 + f, :], P0[:, 4 + f, :], P0[:, 8 + f, :], ALU.mult))
            dve.wait_ge(stdv_ok.sem, 1)
            vec.on(dve.reciprocal(ACV[:, :], ACV[:, :]))
            dve.wait_ge(vec.sem, vec.now)
            for f in range(FT):
                v = P0[:, 16 + f, :]
                vn_ok.on(dve.scalar_tensor_tensor(out=v, in0=v, scalar=GAINS[:, G_V + f:G_V + f + 1],
                                                  in1=ACV[:, :], op0=ALU.mult, op1=ALU.mult))
            for f in range(FT):
                dve.wait_ge(vt_fill.sem, f + 1)
                vt_drain.on(dve.tensor_copy(VT[:, f, :, :].rearrange("p c s -> p (c s)"), M[:, 2 + f % 2, :]))
            cv_ok.on(dve.tensor_copy(CV[:, :], M[0:NS, 0, :]))
            dve.wait_ge(zo_fill.sem, 1)
            zo_ok.on(dve.tensor_copy(ZO[:, :], M[0:10, 1, :]))

            def y_low(f):
                dve.wait_ge(y_hi.sem, f + 1)
                g_ready.on(dve.tensor_tensor(G[:, f, 1, :], TG[:, f % 2, :], G[:, f, 0, :].bitcast(F32), ALU.subtract))

            for f in range(FT):
                z, co = P0[:, 8 + f, :], TA[:, f % 2, :]

                def tap(j):
                    c = G_CONV + j * FT + f
                    return GAINS[:, c:c + 1]

                def mac(dst, src, j):
                    dve.wait_ge(vec.sem, vec.now)
                    vec.on(dve.scalar_tensor_tensor(out=dst, in0=src, scalar=tap(j), in1=dst,
                                                    op0=ALU.mult, op1=ALU.add))
                dve.wait_ge(z_ok.sem, FT)
                vec.on(dve.tensor_scalar(co, z, tap(2), None, ALU.mult))
                mac(co[:, 1:SEQ], z[:, 0:SEQ - 1], 1)
                mac(co[:, 2:SEQ], z[:, 0:SEQ - 2], 0)
                mac(co[:, SEQ:T], HT[:, f, 1:16:2], 1)
                mac(co[:, SEQ:T], HT[:, f, 0:16:2], 0)
                dve.wait_ge(vec.sem, vec.now)
                y_ok.on(dve.tensor_tensor(TG[:, f % 2, :], P0[:, f, :], co, ALU.mult))
                dve.wait_ge(y_ok.sem, y_ok.now)
                y_low(f)
            for f, bank in enumerate((2, 3, 0, 1)):
                mv = TA[:, f % 2, :]
                dve.wait_ge(mixed.sem, f + 1)
                dve.tensor_tensor(mv[:, 0:SEQ].rearrange("p (c t) -> p c t", c=QT),
                                  M[:, bank, :].rearrange("p (c t) -> p c t", c=QT),
                                  BSP[:, f, :].unsqueeze(1).to_broadcast([P, QT, P]), ALU.add)
                vec.on(dve.tensor_scalar(mv[:, SEQ:T], P0[:, 16 + f, SEQ:T], W00[:, f, 0:1], BSP[:, f, 0:1],
                                         ALU.mult, ALU.add))
                dve.wait_ge(ug_ok.sem, f + 1)
                dve.wait_ge(vec.sem, vec.now)
                y_ok.on(dve.tensor_tensor(TG[:, f % 2, :], P0[:, 12 + f, :], mv, ALU.mult))
                dve.wait_ge(y_ok.sem, y_ok.now)
                y_low(FT + f)
            dve_residual(dve, "out0", 1, G_FFN[0], 4)
            norm_dve(dve, 1)
            dve_up(dve, "up0", 0)
            dve_residual(dve, "down0", 2, G_MIX[1], 2)
            norm_dve(dve, 2)
            g_fin = G_MIX[1]
            if layer1:
                dve_project(dve, "inq", 2)
                dve_project(dve, "in1", 3, tail=True, first=8)
                dve_attention(dve)
                dve_residual(dve, "out1", 3, G_FFN[1], 4)
                norm_dve(dve, 3)
                dve_up(dve, "up1", 1)
                dve_residual(dve, "down1", 4, G_FIN, 2)
                norm_dve(dve, 4)
                g_fin = G_FIN
            for m in range(KD):
                fin_v.on(dve.scalar_tensor_tensor(out=XT[:, m, :], in0=XT[:, m, :], scalar=GAINS[:, g_fin + m:g_fin + m + 1],
                                                  in1=RSTD[:, :], op0=ALU.mult, op1=ALU.mult))
            for n in range(2 * QT):
                i, hf = n // 2, n % 2
                dve.wait_ge(fin_p.sem, n + 1)
                fin_v.on(dve.tensor_copy(YO[:, i, hf * 512:(hf + 1) * 512], M[:, n % 4, :]))
            for hf in range(2):
                dve.wait_ge(fin_p.sem, 9 + hf)
                fin_v.on(dve.tensor_copy(YS[:, hf * 512:(hf + 1) * 512], M[0:NS, hf, :]))


OUTS = [(1, SEQ, D), (NS, 1, D), (1, 2, DC), (NS, 2, DC), (NS, 1, DC), (1, SEQ, 4, NKV, HD),
        (NS, 1, 4, NKV, HD), (1, SEQ, 2, NKV, HD), (NS, 1, 2, NKV, HD)]
FULL = True


def kernel(**inputs):
    import concourse.bacc as bacc
    from concourse.bass_utils import run_bass_kernel_spmd

    nc = bacc.Bacc("TRN2", target_bir_lowering=False, num_devices=1)
    arrays, aps = {}, {}
    for name, x in {**inputs, **consts()}.items():
        x = np.ascontiguousarray(x)
        arrays["in_" + name] = x
        aps[name] = nc.dram_tensor("in_" + name, x.shape, mybir.dt.from_np(x.dtype), kind="ExternalInput").ap()
    outs = [nc.dram_tensor(f"out_{i}", s, F32, kind="ExternalOutput").ap() for i, s in enumerate(OUTS)]
    program(nc, aps, outs)
    r = run_bass_kernel_spmd(nc, [arrays], core_ids=[0])
    return tuple(r.results[0][f"out_{i}"] for i in range(len(OUTS)))
```

```python
from contextlib import ExitStack, contextmanager

import concourse.bass as bass
import numpy as np
from concourse import mybir

F32, F32R, BF16, I32 = mybir.dt.float32, mybir.dt.float32r, mybir.dt.bfloat16, mybir.dt.int32
ALU, ACT, AX = mybir.AluOpType, mybir.ActivationFunctionType, mybir.AxisListType

P = 128
D = 1024
SEQ, NS = 512, 8
T = SEQ + NS
HALF = T // 2
KD = D // P
DC = 512
FT = DC // P
FF = 2816
KF = FF // P
NH, NKV, HD = 16, 4, 64
PAST, PAGE = 256, 128
NPAGE = PAST // PAGE
SCALE = HD ** -0.5
NEG = -1e30
EPS = 1e-6
QT = SEQ // P
NC = 32
SEGS = 2 * NS * 16 + 2 * 32 + 3
NCOL = SEGS - 1
SLOT = 2048
KH = KF // 2

PHASES = [("in0", 10, 20), ("out0", 4, 8), ("up0", 22, 44), ("down0", 16, 8),
          ("in1", 7, 13), ("inq", 4, 8), ("out1", 4, 8), ("up1", 22, 44), ("down1", 16, 8)]
S0, U0 = {}, {}
_s = _u = 0
for _n, _a, _b in PHASES:
    S0[_n], U0[_n] = _s, _u
    _s, _u = _s + _a, _u + _b
RAW = {n: 64 if n in ("inq", "out1") else 32 for n, _, _ in PHASES}
RAW0, _c = {}, [0, 0]
for _n, _a, _ in PHASES:
    RAW0[_n] = tuple(_c)
    for _k in range(S0[_n], S0[_n] + _a):
        _c[_k % 2] += RAW[_n]
ORDER = [n for n, _, _ in PHASES]


def raw_of(name, j):
    b = (S0[name] + j) % 2
    slots = dict((n, k) for n, k, _ in PHASES)[name]
    if j < slots:
        return RAW0[name][b] + RAW[name] * (j // 2 + 1)
    nxt = ORDER[ORDER.index(name) + 1]
    return RAW0[nxt][b] + RAW[nxt]

G_MIX, G_FFN, G_FIN, G_CONV, G_V = (0, 8), (16, 24), 32, 40, 52
N_GAIN = 56

C_ROT, C_COS, C_SIN = 0, 128, 128 + T
C_CB = 128 + 2 * T
C_CV = C_CB + QT * NC
N_CA = C_CV + QT * NC


def consts():
    p = np.arange(P)
    eye = np.eye(P, dtype=np.float32)
    base = np.concatenate([eye, np.ones((P, P), np.float32), np.full((P, 8), EPS, np.float32)], 1)
    tril = (p[:, None] <= p[None, :]).astype(np.float32)
    rot = np.zeros((P, P), np.float32)
    for m in range(P):
        if m % 64 < 32:
            rot[m + 32, m] = -1.0
        else:
            rot[m - 32, m] = 1.0
    pos = np.concatenate([np.arange(SEQ), np.full(NS, PAST)]).astype(np.float32)
    inv = np.power(np.float32(10000.0), -np.arange(32, dtype=np.float32) * np.float32(2.0) / np.float32(HD))
    ang = inv.astype(np.float32)[p % 32][:, None] * pos[None, :]
    cb = np.zeros((P, QT, NC), np.float32)
    for i in range(QT):
        t = i * P + p[:, None]
        c = np.arange(NC)[None, :]
        cb[:, i] = ((16 * c + 31 <= t) & (c < 31)).astype(np.float32)
    att = np.concatenate([rot, np.cos(ang).astype(np.float32), np.sin(ang).astype(np.float32),
                          ((1 - cb) * np.float32(NEG)).reshape(P, -1), cb.reshape(P, -1)], 1)
    n_r, g_r = p // 16, (p % 16) // 4
    new = np.zeros((P, PAST + NS), np.float32)
    new[:, PAST:] = np.where(n_r[:, None] == np.arange(NS)[None, :], 0.0, NEG)
    cmp_ = np.where((n_r[:, None] == p[None, :] // 16) & (p[None, :] % 16 < 15), 0.0, NEG)
    grp = (g_r[:, None] == np.arange(4)[None, :]).astype(np.float32)
    smp = np.concatenate([new, cmp_, grp], 1).astype(np.float32)
    causal = np.where(p[None, :] > p[:, None], NEG, 0.0).astype(np.float32)
    return {"c_base": base, "c_tril": tril, "c_att": att, "c_smp": smp, "c_causal": causal}


class Count:

    def __init__(self, sem):
        self.sem, self.n, self.term = sem, 0, None

    def on(self, ins):
        ins.then_inc(self.sem, 1)
        self.n += 1
        return ins

    @property
    def now(self):
        return self.n if self.term is None else self.term + self.n


@contextmanager
def loop(eng, trips, per):
    with eng.Fori(0, trips) as t:
        first = {}
        for c, k in per:
            first[c] = c.n
            c.term = t * k
        yield t
        for c, k in per:
            assert c.n - first[c] == k, (c.sem, c.n - first[c], k)
    for c, k in per:
        c.term = None
        c.n += k * (trips - 1)


def program(nc, a, out):
    ctx = ExitStack()
    with ctx:
        lay = [16512]

        def at(name, shape, dt, offset):
            return nc.alloc_sbuf_tensor_at(name, shape, dt, offset=offset)

        def size(shape, dt):
            n = 2 if dt == BF16 else 4
            for k in shape[1:]:
                n *= k
            return (n + 31) // 32 * 32

        def new(name, shape, dt=F32):
            t = at(name, shape, dt, lay[0])
            lay[0] += size(shape, dt)
            return t

        def packed(offset, *tensors):
            got = []
            for name, shape, dt in tensors:
                got.append(at(name, shape, dt, offset))
                offset += size(shape, dt)
            return got, offset

        XT = new("XT", [P, KD, T])
        h_at = lay[0]
        H = new("H", [P, KD, 2, T], F32R)
        g_at = lay[0]
        G = new("G", [P, KF, 2, T], F32R)
        wr_at = lay[0]
        WR = new("WR", [P, 2, SLOT])
        wh_at = lay[0]
        WH = new("WH", [P, 2, SLOT], F32R)
        WL = new("WL", [P, 2, SLOT], F32R)
        BASE = new("BASE", [P, 2 * P + 8])
        IDENT, ONES, EPSC = BASE[:, 0:P], BASE[:, P:2 * P], BASE[:, 2 * P:2 * P + 1]
        GAINS = new("GAINS", [P, N_GAIN])
        rstd_at = lay[0]
        RSTD = new("RSTD", [P, T])
        ACC = new("ACC", [P, T])
        SQ = new("SQ", [P, 2, T])
        tmp_at = lay[0]
        TA = new("TA", [P, 2, T])
        TB = new("TB", [P, T])
        TG = new("TG", [P, 2, T])
        tmp_end = lay[0] + 2048
        assert tmp_end <= 229344, tmp_end
        s_at = g_at + 8 * 2 * T * 4
        s_end = g_at + KF * 2 * T * 4
        P0 = at("P0", [P, 21, T], F32, s_at)
        (XL, XS), _ = packed(s_at, ("XL", [P, QT, D], F32), ("XS", [NS, D], F32))
        (BSP, WT, HT, SCV, WSP, ACV, W00, TRIL, GROW, ZO, CV), e = packed(
            s_at + 20 * T * 4, ("BSP", [P, 4, P], F32), ("WT", [P, 4, P], F32), ("HT", [P, FT, 16], F32),
            ("SCV", [16, DC], F32), ("WSP", [P, 4, P], F32), ("ACV", [P, T], F32), ("W00", [P, 4, 8], F32),
            ("TRIL", [P, P], F32), ("GROW", [N_GAIN, P], F32), ("ZO", [10, DC], F32), ("CV", [NS, DC], F32))
        assert e <= s_end, (e, s_end)
        YO = at("YO", [P, QT, D], F32, wr_at)
        YS = at("YS", [NS, D], F32, wr_at + QT * D * 4)
        VT = at("VT", [P, FT, 4, P], F32, h_at)

        PG = ctx.enter_context(nc.psum_tensor("PG", [P, 2, 2, 512], F32))
        M = ctx.enter_context(nc.psum_tensor("M", [P, 4, 512], F32))

        def sem(name):
            return ctx.enter_context(nc.semaphore(name))

        CT = at("CT", [P, 16, SEGS], F32, g_at)
        NSTG = 5
        PST = at("PST", [P, NSTG, 2, 256], F32, g_at + size([P, 16, SEGS], F32))
        PEK = at("PEK", [32, 2, 2, HD], F32, g_at + size([P, 16, SEGS], F32) + NSTG * 2048)
        WBD = at("WBD", [P, 2, 32, P], F32, wh_at)
        (QR, KP), e = packed(h_at, ("QR", [P, KD, T], F32), ("KP", [P, 2, NKV, SEQ], F32))
        assert e <= g_at
        (VTK, KVO), e = packed(s_at + 21 * T * 4, ("VTK", [P, QT, 2, 256], F32), ("KVO", [P, 1536], F32))
        assert e <= s_end
        (PB, PT), e = packed(s_at + 8 * T * 4, ("PB", [P, 2, 4, SEQ], F32), ("PT", [P, 4, 512], F32))
        assert e <= s_at + 21 * T * 4
        TC = [at(f"TC{gp}", [P, QT, 8, NC], F32, s_at + gp * 4 * T * 4) for gp in range(2)]
        (CA, CBF, GT, CVT, CKT, CVK, CKP), e = packed(
            tmp_at, ("CA", [P, N_CA], F32), ("CBF", [P, 2 * P], BF16), ("GT", [P, QT, 48], F32),
            ("CVT", [P, NCOL], F32), ("CKT", [P, NCOL], F32), ("CVK", [NC, 2, P], F32), ("CKP", [P, 2, 2, NC], F32))
        assert e <= tmp_end, (e, tmp_end)
        (KN, GS, SGT, ST8, QS, QU, OS), e = packed(
            e, ("KN", [P, 2, 2, NS], F32), ("GS", [P, 3], F32), ("SGT", [NS, 48], F32),
            ("ST8", [P, 96], F32), ("QS", [P, KD, NS], F32), ("QU", [P, KD, NS], F32), ("OS", [P, KD, NS], F32))
        assert e <= 229344, e
        VN = [KVO[0:NS, 512 * b + 768:512 * b + 1024] for b in range(2)]
        CVS = at("CVS", [P, 2, P], F32, tmp_at + size([P, N_CA], F32) + 512 + size([P, QT, 48], F32))
        PTAB = at("PTAB", [1, 16], I32, s_end - 64)
        ROT, COS, SIN = CA[:, 0:P], CA[:, C_COS:C_COS + T], CA[:, C_SIN:C_SIN + T]
        KVS = at("KVS", [P, NS, 2, 512], F32, s_at + 8 * T * 4)
        (QPD, Q2, PTP, KTS, CS, SCS, PS, OA, PTN, OM), e = packed(
            h_at, ("QPD", [P, NS, 2, P], F32), ("Q2", [P, 2, 2, P], F32), ("PTP", [P, 2, NS, P], F32),
            ("KTS", [P, 2, 2, 256], F32), ("CS", [P, 264 + P + 4], F32), ("SCS", [P, 264], F32),
            ("PS", [P, 264], F32), ("OA", [P, 256], F32), ("PTN", [P, P], F32), ("OM", [P, 2, HD], F32))
        assert e <= g_at, (e, g_at)

        w_raw = [sem("w_raw0"), sem("w_raw1")]
        w_hi = Count(sem("w_hi"))
        w_split = Count(sem("w_split"))
        half_used = Count(sem("half_used"))
        tile_done = Count(sem("tile_done"))
        tile_out = Count(sem("tile_out"))
        h_ready = Count(sem("h_ready"))
        g_ready = Count(sem("g_ready"))
        a_hi = Count(sem("a_hi"))
        a_sq = Count(sem("a_sq"))
        acc_ok = Count(sem("acc_ok"))
        st_done = Count(sem("st_done"))
        a_std = Count(sem("a_std"))
        rstd_ok = Count(sem("rstd_ok"))
        a_silu = Count(sem("a_silu"))
        t_gate = Count(sem("t_gate"))
        a_ghi = Count(sem("a_ghi"))
        d_in = sem("d_in")
        d_small = sem("d_small")
        d_out = sem("d_out")
        outs = [0]
        t_fill = Count(sem("t_fill"))
        t_drain = Count(sem("t_drain"))
        vec = Count(sem("vec"))
        vg_ok = Count(sem("vg_ok"))
        vsq_ok = Count(sem("vsq_ok"))
        accv_ok = Count(sem("accv_ok"))
        stv_done = Count(sem("stv_done"))
        stdv_ok = Count(sem("stdv_ok"))
        vn_ok = Count(sem("vn_ok"))
        vt_fill = Count(sem("vt_fill"))
        vt_drain = Count(sem("vt_drain"))
        cv_ok = Count(sem("cv_ok"))
        z_ok = Count(sem("z_ok"))
        zo_fill = Count(sem("zo_fill"))
        zo_ok = Count(sem("zo_ok"))
        mixed = Count(sem("mixed"))
        ug_ok = Count(sem("ug_ok"))
        y_ok = Count(sem("y_ok"))
        y_hi = Count(sem("y_hi"))
        at_g = Count(sem("at_g"))
        passed = sem("passed")
        q_fill = Count(sem("q_fill"))
        q_v = Count(sem("q_v"))
        q_a = Count(sem("q_a"))
        ct_prompt = Count(sem("ct_prompt"))
        cmp_done = Count(sem("cmp_done"))
        ck_ok = Count(sem("ck_ok"))
        rope_p = Count(sem("rope_p"))
        rope_in = Count(sem("rope_in"))
        rope_ok = Count(sem("rope_ok"))
        kp_ok = Count(sem("kp_ok"))
        qs_ok = Count(sem("qs_ok"))
        gt_ok = Count(sem("gt_ok"))
        cs_done = Count(sem("cs_done"))
        cs_out = Count(sem("cs_out"))
        c_max = Count(sem("c_max"))
        c_exp = Count(sem("c_exp"))
        ckp_ok = Count(sem("ckp_ok"))
        c_ready = Count(sem("c_ready"))
        s_done = Count(sem("s_done"))
        nb_ok = Count(sem("nb_ok"))
        exp_done = Count(sem("exp_done"))
        p_ready = Count(sem("p_ready"))
        pv_done = Count(sem("pv_done"))
        o_hi = Count(sem("o_hi"))
        o_out = Count(sem("o_out"))
        qpd_ok = Count(sem("qpd_ok"))
        ss_done = Count(sem("ss_done"))
        snb_ok = Count(sem("snb_ok"))
        sp_ok = Count(sem("sp_ok"))
        sv_done = Count(sem("sv_done"))
        spv_done = Count(sem("spv_done"))
        oa_ok = Count(sem("oa_ok"))
        om_ok = Count(sem("om_ok"))
        os_hi = Count(sem("os_hi"))
        kts_used = Count(sem("kts_used"))
        d_ca, d_pt, d_pe = (sem(n) for n in ("d_ca", "d_pt", "d_pe"))
        d_wc = [sem("d_wc_k"), sem("d_wc_v")]
        d_kv, d_gs, d_cs = (sem(n) for n in ("d_kv", "d_gs", "d_cs"))
        d_page = [sem(f"d_page{n}") for n in range(NSTG)]
        d_kvs = [sem(f"d_kvs{n}") for n in range(NS)]
        N_PHYS = a["cache_kv"].shape[0]
        fin_p = Count(sem("fin_p"))
        fin_v = Count(sem("fin_v"))


        def one(i):
            return bass.ds(i, 1)

        def sets(par):
            return PG[:, par, :, 0:HALF]

        def halves(x):
            return x.rearrange("p (h c) -> p h c", h=2)

        def row(x, m):
            return x[:, one(m), :].rearrange("p a (h c) -> p (a h) c", h=2)

        w0 = a["w_in0"].rearrange("(k p) c -> p k c", p=P)
        wo0 = a["w_out0"].rearrange("(k p) c -> p k c", p=P)
        w1 = a["w_in1"].rearrange("(k p) c -> p k c", p=P)
        wo1 = a["w_out1"].rearrange("(g e j d) c -> g j e d c", g=2, e=2, j=4)
        wup = [a["w_ffn_in"][l].rearrange("(k p) c -> p k c", p=P) for l in range(2)]
        wdn = [a["w_ffn_out"][l].rearrange("(k p) c -> p k c", p=P) for l in range(2)]

        def raw(b, cols=256):
            return WR[:, b, 0:KD * 256].rearrange("p (k c) -> p k c", c=256)

        def slot_free(sp, s):
            sp.wait_ge(w_split.sem, s + 1)

        def load_cols(sp, s, b, w, col):
            slot_free(sp, s)
            for j in range(2):
                sp.dma_start(raw(b)[:, 4 * j:4 * j + 4, :],
                             w[:, 4 * j:4 * j + 4, bass.ds(col, 256)]).then_inc(w_raw[b], 16)

        def load_up(sp, s, b, w, m):
            slot_free(sp, s)
            for j in range(2):
                sp.dma_start(raw(b)[:, :, j * P:(j + 1) * P],
                             w[:, :, bass.ds(m * P + j * FF, P)]).then_inc(w_raw[b], 16)

        def load_down(sp, s, b, w, m, half):
            slot_free(sp, s)
            dst = WR[:, b, 0:KH * P].rearrange("p (k c) -> p k c", c=P)
            for lo, hi in ((0, 5), (5, KH)):
                sp.dma_start(dst[:, lo:hi, :],
                             w[:, half * KH + lo:half * KH + hi, bass.ds(m * P, P)]).then_inc(w_raw[b], 16)

        def sp_cols(sp, name, w, trips):
            with sp.Fori(0, trips) as t:
                for j in range(2):
                    load_cols(sp, t * 2 + S0[name] + j, (S0[name] + j) % 2, w, t * 512 + j * 256)

        def sp_up(sp, name, w):
            with sp.Fori(0, KF // 2) as t:
                for j in range(2):
                    load_up(sp, t * 2 + S0[name] + j, (S0[name] + j) % 2, w, t * 2 + j)

        def sp_down(sp, name, w):
            with sp.Fori(0, KD) as t:
                for half in range(2):
                    load_down(sp, t * 2 + S0[name] + half, (S0[name] + half) % 2, w, t, half)

        def gemm_tile(pe, src, k0, nk, b, first_col, step, par, first, last, ready=None, between=None):
            for kk in range(nk):
                if ready is not None:
                    pe.wait_ge(ready[0].sem, ready[1] + k0 + kk + 1)
                c = kk * step + first_col
                wh, wl = WH[:, b, c:c + P], WL[:, b, c:c + P]
                for hf in range(2):
                    cols = slice(hf * HALF, (hf + 1) * HALF)
                    xh, xl = src[:, k0 + kk, 0, cols], src[:, k0 + kk, 1, cols]
                    for n, (w, x) in enumerate(((wh, xh), (wh, xl), (wl, xh))):
                        mm = pe.matmul(PG[:, par, hf, 0:HALF], w, x,
                                       start=(first and kk == 0 and n == 0),
                                       stop=(last and kk == nk - 1 and n == 2))
                if between is not None and kk % 2 and kk < nk - 1:
                    between()
            return mm

        def pe_wide(pe, name, src, trips, ready, tail=False):
            def body(t, slots, tiles_of):
                for j in range(slots):
                    s, b = t * 2 + S0[name] + j, (S0[name] + j) % 2
                    pe.wait_ge(w_split.sem, s + 3)
                    for c in range(tiles_of):
                        u, par = t * 4 + U0[name] + 2 * j + c, (U0[name] + c) % 2
                        pe.wait_ge(tile_out.sem, u + 1)
                        tile_done.on(gemm_tile(pe, src, 0, KD, b, c * P, 256, par, True, True,
                                               ready if j == 0 and c == 0 else None))
            with loop(pe, trips, [(tile_done, 4)]) as t:
                body(t, 2, 2)
            if tail:
                body(trips, 1, 1)

        def pe_down(pe, name, ready):
            with loop(pe, KD // 2, [(tile_done, 2), (half_used, 2)]) as t:
                for c in range(2):
                    u, par = t * 2 + U0[name] + c, (U0[name] + c) % 2
                    pe.wait_ge(tile_out.sem, u + 1)
                    for half in range(2):
                        s, b = t * 4 + S0[name] + 2 * c + half, (S0[name] + half) % 2
                        pe.wait_ge(w_split.sem, s + 3)
                        mm = gemm_tile(pe, G, half * KH, KH, b, 0, P, par, half == 0, half == 1,
                                       ready if c == 0 else None)
                        (tile_done if half else half_used).on(mm)

        def pe_stat(pe, i):
            pe.wait_ge(acc_ok.sem, 9 * i + 9)
            for hf in range(2):
                mm = pe.matmul(M[:, hf, 0:HALF], ONES, ACC[:, hf * HALF:(hf + 1) * HALF], start=True, stop=True)
            st_done.on(mm)

        N_SMALL = 11

        def plain(act):
            act.sem_inc(passed, 1)

        def split_hi(act, b, raw_count, freed=None):
            act.wait_ge(w_raw[b], raw_count)
            if freed is not None:
                act.wait_ge(freed[0].sem, freed[1])
            plain(act)
            w_hi.on(act.activation(WH[:, b, :], WR[:, b, :], ACT.Copy))

        def split_next_wide(act, name, t, j):
            b = (S0[name] + j + 1) % 2
            count = raw_of(name, 2 * t + j + 1) if isinstance(t, int) else t * 32 + raw_of(name, j + 1)
            split_hi(act, b, count, (tile_done, t * 4 + U0[name] + 2 * j))

        def split_next_down(act, name, t, j):
            b = (S0[name] + j + 1) % 2
            n = 8 * (name == "down1")
            freed = (tile_done, t * 2 + U0[name] + j // 2) if j % 2 == 0 else \
                (half_used, t * 2 + n + j // 2 + 1)
            count = raw_of(name, 4 * t + j + 1) if isinstance(t, int) else t * 64 + raw_of(name, j + 1)
            split_hi(act, b, count, freed)

        def res_act(act, i, m, gcol, par, new_x):
            act.wait_ge(*new_x)
            plain(act)
            if i < 4:
                a_hi.on(act.activation(H[:, one(m), 0, :], XT[:, one(m), :], ACT.Copy,
                                       scale=GAINS[:, bass.ds(m + gcol, 1)]))
            if not (i == 0 and m == 0):
                act.wait_ge(acc_ok.sem, m + 9 * i)
            plain(act)
            a_sq.on(act.activation(SQ[:, par, :], XT[:, one(m), :].rearrange("p a c -> p (a c)"), ACT.Square))

        def res_dve(dve, i, m, gcol, par, done):
            r = m + 8 * i
            if i < 4:
                dve.wait_ge(a_hi.sem, r + 1)
                dve.wait_ge(*done)
                h_ready.on(dve.scalar_tensor_tensor(
                    out=row2(H, m, 1), in0=row1(XT, m), scalar=GAINS[:, bass.ds(m + gcol, 1)],
                    in1=row2(H, m, 0).bitcast(F32), op0=ALU.mult, op1=ALU.subtract))
            dve.wait_ge(a_sq.sem, r + 1)
            dve.wait_ge(acc_ok.sem, acc_ok.now)
            acc_ok.on(dve.tensor_tensor(ACC[:, :], ACC[:, :], SQ[:, par, :], ALU.add))

        def row1(x, m):
            return x[:, one(m), :].rearrange("p a c -> p (a c)")

        def row2(x, m, part):
            return x[:, one(m), part, :].rearrange("p a c -> p (a c)")

        def norm_act(act, i):
            act.wait_ge(st_done.sem, i + 1)
            a_std.on(act.activation(halves(RSTD[:, :]), M[:, 0:2, 0:HALF], ACT.Sqrt, bias=EPSC, scale=1.0 / D))

        def norm_dve(dve, i):
            dve.wait_ge(a_std.sem, i + 1)
            rstd_ok.on(dve.reciprocal(RSTD[:, :], RSTD[:, :]))
            acc_ok.on(dve.memset(ACC[:, :], 0.0))
            dve.wait_ge(rstd_ok.sem, rstd_ok.now)

        def dve_project(dve, name, trips, tail=False, first=0):
            def drain(m, c):
                dve.wait_ge(tile_done.sem, m + U0[name] + 1)
                tile_out.on(dve.tensor_tensor(row(P0, m + first), sets((U0[name] + c) % 2), halves(RSTD[:, :]), ALU.mult))
            with loop(dve, trips, [(tile_out, 4)]) as t:
                for c in range(4):
                    drain(t * 4 + c, c)
            if tail:
                drain(4 * trips, 0)

        def dve_residual(dve, name, i, gcol, per):
            with loop(dve, KD // per, [(tile_out, per), (acc_ok, per)] + [(h_ready, per)] * (i < 4)) as t:
                for c in range(per):
                    m = t * per + c
                    dve.wait_ge(tile_done.sem, m + U0[name] + 1)
                    tile_out.on(dve.tensor_tensor(row(XT, m), row(XT, m), sets((U0[name] + c) % 2), ALU.add))
                    res_dve(dve, i, m, gcol, c % 2, (tile_out.sem, tile_out.now))

        def act_residual(act, name, i, gcol, per, final=False):
            def body(t, last):
                for c in range(per):
                    m = t * per + c
                    if name.startswith("out"):
                        if c % 2 == 0:
                            split_next_wide(act, name, t, c // 2)
                    else:
                        split_next_down(act, name, t, 2 * c)
                        if not (last and c == per - 1):
                            split_next_down(act, name, t, 2 * c + 1)
                    res_act(act, i, m, gcol, c % 2, (tile_out.sem, m + U0[name] + 3))
            trips = KD // per
            if name == "out1":
                for t in range(trips):
                    body(t, False)
                return
            peel = final or name == "down0"
            with loop(act, trips - peel, [(w_hi, per // 2 if name.startswith("out") else 2 * per), (a_sq, per)]
                      + [(a_hi, per)] * (i < 4)) as t:
                body(t, False)
            if peel:
                body(trips - 1, final)

        def dve_up(dve, name, l):
            def body(t, j):
                m = t * 2 + j
                ua = m * 2 + U0[name]
                dve.wait_ge(tile_done.sem, ua + 1)
                tile_out.on(dve.tensor_tensor(halves(TA[:, j, :]), sets(U0[name] % 2), halves(RSTD[:, :]), ALU.mult))
                dve.wait_ge(tile_done.sem, ua + 2)
                tile_out.on(dve.tensor_tensor(halves(TB[:, :]), sets((U0[name] + 1) % 2), halves(RSTD[:, :]), ALU.mult))
                dve.wait_ge(a_silu.sem, m + KF * l + 1)
                dve.wait_ge(tile_out.sem, tile_out.now)
                t_gate.on(dve.tensor_tensor(TG[:, j, :], TA[:, j, :], TB[:, :], ALU.mult))
                dve.wait_ge(a_ghi.sem, m + KF * l + 1)
                dve.wait_ge(t_gate.sem, t_gate.now)
                g_ready.on(dve.tensor_tensor(row2(G, m, 1), TG[:, j, :], row2(G, m, 0).bitcast(F32), ALU.subtract))
            with loop(dve, KF // 2, [(tile_out, 4), (t_gate, 2), (g_ready, 2)]) as t:
                for j in range(2):
                    body(t, j)

        def act_up(act, name, l):
            with loop(act, KF // 2, [(w_hi, 2), (a_silu, 2), (a_ghi, 2)]) as t:
                for j in range(2):
                    m = t * 2 + j
                    split_next_wide(act, name, t, j)
                    act.wait_ge(tile_out.sem, m * 2 + U0[name] + 3)
                    plain(act)
                    a_silu.on(act.activation(TA[:, j, :], TA[:, j, :], ACT.Silu))
                    act.wait_ge(t_gate.sem, m + KF * l + 1)
                    plain(act)
                    a_ghi.on(act.activation(row2(G, m, 0), TG[:, j, :], ACT.Copy))

        PAIRS = [(gp, i) for gp in range(2) for i in range(QT)]
        UNITS = [(gp, i, e) for gp, i in PAIRS for e in range(2)]
        STEPS = [(gp, i, e, br) for gp, i, e in UNITS for br in range(2)]
        SETUP = [("rope", 0), ("gate", 0), ("rope", 1), ("gate", 1), ("rope", 2), ("page", 0), ("rope", 3), ("page", 1)]
        for _i in range(QT + 1):
            SETUP += [("tok", _i, _b) for _b in range(3)] + [("page", _i + 2)]
        SETUP += [("page", NS - 1), ("pe", 0)]
        SETUP_V = [("page", NS + _n) for _n in range(NS)] + [("pe", 1)]
        Q_OF = {x: n for n, x in enumerate(x for x in SETUP + SETUP_V if x[0] != "rope")}
        Q_CV = len(Q_OF)
        Q_ATT = Q_CV + 2
        q_unit, q_step, q = [], [], Q_ATT
        for _, i, _ in UNITS:
            q_unit.append(q)
            q += 1
            for _ in range(2):
                q_step.append(q)
                q += i + 1
        Q_SMP = q
        KV_TILE = (12, 16)

        def q_wait_drained(eng, q):
            if q % 2 == 0:
                eng.wait_ge(q_v.sem, q // 2 + 1)
            else:
                eng.wait_ge(q_a.sem, q // 2 + 1)

        def q_bank(pe, q):
            if q >= 2:
                q_wait_drained(pe, q - 2)
            return M[:, q % 2, :]

        def drains(eng, mine, q, copies, after=()):
            if q % 2 != mine:
                return
            eng.wait_ge(q_fill.sem, q + 1)
            for s, v in after:
                eng.wait_ge(s, v)
            for dst, src in copies:
                ins = eng.activation(dst, src, ACT.Copy) if mine else eng.tensor_copy(dst, src)
            (q_a if mine else q_v).on(ins)

        def drain_job(eng, mine, job):
            q = Q_OF[job]
            bank = M[:, q % 2, :]
            if job[0] == "gate":
                copies = [(SGT[:, :], bank[0:NS, 80:128]) if job[1] else
                          (GT[:, :, :], bank.rearrange("p (i c) -> p i c", i=QT)[:, :, 80:128])]
                drains(eng, mine, q, copies)
            elif job[0] == "tok":
                _, i, b = job
                rows = P if i < QT else NS
                copies = [(KVO[0:rows, b * 512:(b + 1) * 512], bank[0:rows])]
                if b and i < QT:
                    copies.append((VTK[:, i, b - 1, :], bank[:, 256:512]))
                drains(eng, mine, q, copies, [(d_kv, 32 * i)] if i else [])
            elif job[0] == "page":
                src = bank.rearrange("p (g s r) -> p g s r", g=2, r=16)
                n = job[1] % NS
                drains(eng, mine, q, [(CT[:, :, g * P + n * 16:g * P + n * 16 + 16], src[:, g].rearrange("p s r -> p r s"))
                                      for g in range(2)])
            else:
                drains(eng, mine, q, [(CT[:, :, NCOL - 2:NCOL], bank[:, 0:32].rearrange("p (h r) -> p r h", h=2))])

        def drain_cv(eng, mine):
            drains(eng, mine, Q_CV, [(CVK[:, :, :].rearrange("c g d -> c (g d)"), M[0:NC, Q_CV % 2, 0:2 * P])])
            drains(eng, mine, Q_CV + 1, [(CVS[:, :, :].rearrange("c g d -> c (g d)"), M[:, (Q_CV + 1) % 2, 0:2 * P])])

        def sp_layer1(sp):
            with sp.Fori(0, 3) as t:
                for j in range(2):
                    load_cols(sp, t * 2 + S0["in1"] + j, (S0["in1"] + j) % 2, w1, t * 512 + D + j * 256)
            s = S0["in1"] + 6
            slot_free(sp, s)
            for j in range(2):
                sp.dma_start(raw(s % 2)[:, 4 * j:4 * j + 4, 0:P],
                             w1[:, 4 * j:4 * j + 4, 2480:2608]).then_inc(w_raw[s % 2], 16)
            sp.wait_ge(g_ready.sem, 8 + KF)
            sp.wait_ge(tile_done.sem, U0["in1"])
            sp.dma_start(CA[:, :], a["c_att"]).then_inc(d_ca, 16)
            sp.wait_ge(rstd_ok.sem, 3)
            sp.dma_start(SQ[:, 0, 0:P], a["c_causal"]).then_inc(d_ca, 16)
            sp.dma_start(PTAB[:, :], a["page_table"].rearrange("n g -> (n g)").rearrange("(o x) -> o x", o=1)
                         ).then_inc(d_pt, 16)
            for e in range(2):
                for kv in range(2):
                    sp.dma_start(PEK[:, kv, e, :], a["pe_cmp"][kv]).then_inc(d_pe, 16)
            sp.wait_ge(d_pt, 16)
            for x in range(NSTG):
                load_page(sp, x)
            for m in range(4):
                b = (S0["inq"] + m) % 2
                slot_free(sp, S0["inq"] + m)
                for jj in range(2):
                    for e in range(2):
                        sp.dma_start(raw(b)[:, :, jj * P + e * HD:jj * P + (e + 1) * HD],
                                     w1[:, :, bass.ds(m // 2 * 512 + 256 * e + P * (m % 2) + HD * jj, HD)]
                                     ).then_inc(w_raw[b], 16)
            for job in SETUP:
                if job[0] == "tok" and job[2] == 2:
                    i = job[1]
                    for b in range(3):
                        q_wait_drained(sp, Q_OF["tok", i, b])
                    n = P if i < QT else NS
                    kv = out[5][0, i * P:(i + 1) * P] if i < QT else out[6][:, 0]
                    win = out[7][0, i * P:(i + 1) * P] if i < QT else out[8][:, 0]
                    sp.dma_start(kv.rearrange("n a g d -> n (a g d)"), KVO[0:n, 0:1024]).then_inc(d_kv, 16)
                    sp.dma_start(win.rearrange("n a g d -> n (a g d)"), KVO[0:n, 1024:1536]).then_inc(d_kv, 16)
                elif job[0] == "page":
                    sp.wait_ge(q_fill.sem, Q_OF[job] + 1)
                    load_page(sp, job[1] + NSTG)
            load_out1(sp, 0)
            load_out1(sp, 1)
            sp.wait_ge(tile_done.sem, U0["out1"])
            for kk in range(2):
                for e in range(2):
                    r = slice(e * HD, (e + 1) * HD)
                    sp.dma_start(WBD[r, kk, :, r], a["w_cmp"][kk].rearrange("l d e -> d l e")).then_inc(d_wc[kk], 16)
            for x in range(NS, 2 * NS - NSTG):
                sp.wait_ge(q_fill.sem, Q_OF["page", x] + 1)
                load_page(sp, x + NSTG)
            sp.wait_ge(gt_ok.sem, 2)
            sp.dma_start(GS[:, :], SGT[:, :]).then_inc(d_gs, 16)
            sp.wait_ge(pv_done.sem, Q_SMP - Q_ATT)
            sp.wait_ge(o_out.sem, len(UNITS))
            sp.wait_ge(d_kv, 32 * (QT + 1))
            sp.dma_start(CS[:, :], a["c_smp"]).then_inc(d_cs, 16)
            for br in range(2):
                for n in range(NS):
                    if br:
                        sp.wait_ge(spv_done.sem, 1)
                    for g in range(NPAGE):
                        if br == 0:
                            page = sp.value_load(PTAB[0:1, n * NPAGE + g:n * NPAGE + g + 1], min_val=0, max_val=N_PHYS - 1)
                            src = a["cache_kv"][bass.ds(page, 1), :, 2:4, :, :].rearrange("a p b g d -> p (a b g d)")
                        else:
                            src = a["cache_win"][n, g * P:(g + 1) * P].rearrange("p b g d -> p (b g d)")
                        sp.dma_start(KVS[:, n, g, :], src).then_inc(d_kvs[n], 16)
            sp.wait_ge(d_kv, 32 * (QT + 1))

        def load_page(sp, x):
            kv, n = x // NS, x % NS
            for g in range(NPAGE):
                page = sp.value_load(PTAB[0:1, n * NPAGE + g:n * NPAGE + g + 1], min_val=0, max_val=N_PHYS - 1)
                sp.dma_start(PST[:, x % NSTG, g, :],
                             a["cache_kv"][bass.ds(page, 1), :, kv, :, :].rearrange("a p g d -> p (a g d)")
                             ).then_inc(d_page[x % NSTG], 16)

        def load_out1(sp, m):
            s = S0["out1"] + m
            slot_free(sp, s)
            for e in range(2):
                for g in range(2):
                    sp.dma_start(WR[e * HD:(e + 1) * HD, s % 2, g * 1024:(g + 1) * 1024].rearrange("d (j c) -> d j c", j=4),
                                 wo1[g, :, e, :, m * 256:(m + 1) * 256].rearrange("j d c -> d j c")
                                 ).then_inc(w_raw[s % 2], 16)

        def sp_cols_out1(sp):
            load_out1(sp, 2)
            load_out1(sp, 3)

        def pool_layer1(pool, split_lo):
            def clear(x):
                if at_g.n:
                    pool.wait_ge(at_g.sem, at_g.now)
                at_g.on(pool.memset(x, 0.0))
            pool.wait_ge(tile_done.sem, U0["in1"])
            clear(CT[:, :, NCOL:SEGS])
            pool.wait_ge(g_ready.sem, 8 + KF)
            clear(CKP[0:HD, :, 1, :])
            clear(CKP[HD:P, :, 0, :])
            pool.wait_ge(tile_done.sem, U0["out1"])
            clear(WBD[0:HD, :, :, HD:P])
            clear(WBD[HD:P, :, :, 0:HD])
            clear(KP[0:HD, :, 1:NKV:2, :])
            clear(KP[HD:P, :, 0:NKV:2, :])
            pool.wait_ge(at_g.sem, at_g.now)
            split_lo(S0["out1"], S0["out1"] % 2)
            pool.wait_ge(w_split.sem, 2 + S0["out1"] + 1)
            pool.wait_ge(s_done.sem, 4 * len(STEPS))
            pool.wait_ge(qs_ok.sem, 1)
            clear(QPD[:, :, :, :])
            clear(Q2[:, :, :, :])
            clear(PTP[:, :, :, :])

        def rope_banks(r):
            return M[:, 2:4, 0:HALF] if r < 4 else sets(r % 2)

        def rope_pe(pe, r, m):
            if r == 4:
                pe.wait_ge(tile_out.sem, U0["out1"] + 2)
            if 1 <= r < 4:
                pe.wait_ge(rope_in.sem, r)
            elif r >= 6:
                pe.wait_ge(rope_in.sem, r - 1)
            for hf in range(2):
                mm = pe.matmul(rope_banks(r)[:, hf, :], ROT, P0[:, m, hf * HALF:(hf + 1) * HALF], start=True, stop=True)
            rope_p.on(mm)

        def rope_dve(dve, r, m, dst):
            dve.wait_ge(rope_p.sem, r + 1)
            rope_in.on(dve.tensor_tensor(halves(SQ[:, r % 2, :]), rope_banks(r), halves(SIN), ALU.mult))
            vec.on(dve.tensor_tensor(dst, P0[:, m, :], COS, ALU.mult))
            dve.wait_ge(rope_in.sem, rope_in.now)
            dve.wait_ge(vec.sem, vec.now)
            rope_ok.on(dve.tensor_tensor(dst, dst, SQ[:, r % 2, :], ALU.add))

        ROPE_K = (12, 13, 16, 17)

        def pe_job(pe, job):
            if job[0] == "rope":
                return rope_pe(pe, job[1], ROPE_K[job[1]])
            bank = q_bank(pe, Q_OF[job])
            if job[0] == "gate":
                if job[1]:
                    mm = pe.transpose(bank[0:NS, 0:P], P0[:, 20, SEQ:T], IDENT)
                else:
                    for i in range(QT):
                        mm = pe.transpose(bank[:, i * P:(i + 1) * P], P0[:, 20, i * P:(i + 1) * P], IDENT)
            elif job[0] == "tok":
                _, i, b = job
                rows, cols = (P, slice(i * P, (i + 1) * P)) if i < QT else (NS, slice(SEQ, T))
                if b:
                    pe.wait_ge(rope_ok.sem, 2 * b)
                for c in range(4):
                    mm = pe.transpose(bank[0:rows, c * P:(c + 1) * P], P0[:, 8 + 4 * b + c, cols], IDENT)
            elif job[0] == "page":
                x = job[1]
                pe.wait_ge(d_page[x % NSTG], 32 * (x // NSTG + 1))
                for gp in range(2):
                    for kt in range(NPAGE):
                        c = (2 * gp + kt) * P
                        mm = pe.transpose(bank[:, c:c + P], PST[:, x % NSTG, kt, gp * P:(gp + 1) * P], IDENT)
            else:
                pe.wait_ge(d_pe, 64)
                mm = pe.transpose(bank[:, 0:32], PEK[:, job[1], :, :].rearrange("l e d -> l (e d)"), IDENT[0:32, 0:32])
            q_fill.on(mm)

        def pe_inq(pe):
            jobs = iter(SETUP)

            def setup():
                job = next(jobs, None)
                if job is not None:
                    pe_job(pe, job)
            pe.wait_ge(d_ca, 32)
            pe.wait_ge(tile_out.sem, U0["inq"] + 2)
            for u in range(KD):
                n, b = U0["inq"] + u, (S0["inq"] + u // 2) % 2
                if u % 2 == 0:
                    pe.wait_ge(w_split.sem, S0["inq"] + u // 2 + 3)
                pe.wait_ge(tile_out.sem, n + 1)
                tile_done.on(gemm_tile(pe, H, 0, KD, b, u % 2 * P, 256, n % 2, True, True, between=setup))
                setup()
            assert next(jobs, None) is None

        def pe_attention(pe):
            def compress(kv, between):
                q_wait_drained(pe, Q_OF["pe", kv])
                q_wait_drained(pe, Q_OF["pe", kv] - 1)
                pe.wait_ge(ct_prompt.sem, kv + 1)
                pe.wait_ge(d_wc[kv], 32)
                pe.wait_ge(at_g.sem, 5)
                if kv:
                    pe.wait_ge(ck_ok.sem, 1)
                for l in range(32):
                    if l in between:
                        between[l]()
                    h = l // 16
                    mm = pe.matmul(M[:, 3, 0:NCOL], WBD[:, kv, l, :], CT[:, l % 16, h:h + NCOL],
                                   start=l == 0, stop=l == 31)
                cmp_done.on(mm)

            def cmp_scores(cu):
                gp, i = PAIRS[cu]
                if cu == 0:
                    pe.wait_ge(ckp_ok.sem, 1)
                    pe.wait_ge(rope_in.sem, 4 + KD)
                for j in range(4):
                    c = i % 2 * 256 + j * 2 * NC
                    mm = pe.matmul(PG[:, gp, i // 2, c:c + 2 * NC], P0[:, gp * 4 + j, i * P:(i + 1) * P],
                                   CKP[:, gp, :, :].rearrange("p e c -> p (e c)"), start=True, stop=True)
                cs_done.on(mm)

            def scores(hu):
                gp, i, e, br = STEPS[hu]
                n = (i + 1) * P
                if hu == 0:
                    pe.wait_ge(cs_out.sem, 2)
                    pe.wait_ge(rope_ok.sem, 4 + KD)
                    pe.wait_ge(kp_ok.sem, 1)
                    pe.wait_ge(at_g.sem, 7)
                for j in range(4):
                    if hu:
                        pe.wait_ge(exp_done.sem, 4 * (hu - 1) + j + 1)
                    bank = PG[:, j // 2, j % 2, :]
                    pe.matmul(bank[:, 0:n], QR[:, gp * 4 + j, i * P:(i + 1) * P], KP[:, br, 2 * gp + e, 0:n],
                              start=True, stop=False)
                    s_done.on(pe.matmul(bank[:, n - P:n], CBF[:, 0:P], CBF[:, P:2 * P], start=False, stop=True))

            for m in range(3):
                rope_pe(pe, 4 + m, m)
            compress(0, {2 + 6 * n: (lambda m=3 + n: rope_pe(pe, 4 + m, m)) for n in range(5)})
            for n, job in enumerate(SETUP_V):
                if n == 0:
                    pe.wait_ge(cmp_done.sem, 1)
                pe_job(pe, job)
                if n >= 1:
                    cmp_scores(n - 1)
            compress(1, {16: lambda: scores(0)})

            def banks(hu):
                gp, i, e, br = STEPS[hu]
                return [(q_unit[hu // 2], None)] * (br == 0) + [(q_step[hu] + kt, kt) for kt in range(i + 1)]

            def turn(hu, q, kt):
                gp, i, e, br = STEPS[hu]
                bank = q_bank(pe, q)
                if kt is None:
                    pe.wait_ge(c_ready.sem, gp + 1)
                else:
                    pe.wait_ge(p_ready.sem, hu + 1)
                for j in range(4):
                    if kt is None:
                        mm = pe.transpose(bank[0:NC, j * P:(j + 1) * P], TC[gp][:, i, 2 * j + e, :], IDENT)
                    else:
                        mm = pe.transpose(bank[:, j * P:(j + 1) * P], PB[:, hu % 2, j, kt * P:(kt + 1) * P], IDENT)
                q_fill.on(mm)

            def pv(hu, q, kt):
                gp, i, e, br = STEPS[hu]
                q_wait_drained(pe, q)
                lhsT, rows = (CVK[:, gp, :], NC) if kt is None else (VTK[:, kt, br, gp * P:(gp + 1) * P], P)
                pv_done.on(pe.matmul(M[:, 2 + hu // 2 % 2, :], lhsT, PT[0:rows, (q - Q_ATT) % 4, :],
                                     start=kt is None, stop=br == 1 and kt == i))

            bank = q_bank(pe, Q_CV)
            pe.wait_ge(ck_ok.sem, 2)
            for gp in range(2):
                mm = pe.transpose(bank[0:NC, gp * P:(gp + 1) * P], CVT[:, 256 + gp * NC:256 + (gp + 1) * NC], IDENT)
            q_fill.on(mm)
            bank = q_bank(pe, Q_CV + 1)
            for gp in range(2):
                mm = pe.transpose(bank[:, gp * P:(gp + 1) * P], CVT[:, gp * P:(gp + 1) * P], IDENT)
            q_fill.on(mm)
            for hu in range(len(STEPS)):
                bs = banks(hu)
                for q, kt in bs[:2]:
                    turn(hu, q, kt)
                if hu + 1 < len(STEPS):
                    scores(hu + 1)
                if hu % 2 == 0 and hu >= 4:
                    pe.wait_ge(o_out.sem, hu // 2 - 1)
                if hu == 0:
                    q_wait_drained(pe, Q_CV)
                for n, (q, kt) in enumerate(bs):
                    pv(hu, q, kt)
                    if n + 2 < len(bs):
                        turn(hu, *bs[n + 2])
            pe_samples(pe)

        def pe_samples(pe):
            S, O = PG[:, 0, 0, :], PG[:, 0, 1, :]
            pe.wait_ge(qpd_ok.sem, 1)
            pe.wait_ge(exp_done.sem, 4 * len(STEPS))
            for gp in range(2):
                mm = pe.matmul(S[:, 0:P], Q2[:, 1, gp, :], CKT[:, gp * P:(gp + 1) * P], start=gp == 0, stop=gp == 1)
            ss_done.on(mm)
            q = Q_SMP
            bank = q_bank(pe, q)
            pe.wait_ge(sp_ok.sem, 1)
            q_fill.on(pe.transpose(bank[:, 0:P], PS[:, 0:P], IDENT))
            q_wait_drained(pe, q)
            q_wait_drained(pe, Q_CV + 1)
            sv_done.on(pe.matmul(O[:, 0:256], PTN[:, :], CVS[:, :, :].rearrange("c g d -> c (g d)"), start=True, stop=True))
            for br in range(2):
                q0 = Q_SMP + 1 + (NS + 1) * br
                for n in range(NS + 1):
                    if n < NS:
                        bank = q_bank(pe, q0 + n)
                        pe.wait_ge(d_kvs[n], 32 * (br + 1))
                        for gp in range(2):
                            for kt in range(NPAGE):
                                c = (2 * gp + kt) * P
                                mm = pe.transpose(bank[:, c:c + P], KVS[:, n, kt, gp * P:(gp + 1) * P], IDENT)
                        q_fill.on(mm)
                    if n:
                        q_wait_drained(pe, q0 + n - 1)
                        for gp in range(2):
                            mm = pe.matmul(S[:, 0:256], QPD[:, n - 1, gp, :], KTS[:, (n - 1) % 2, gp, :],
                                           start=n == 1 and gp == 0, stop=n == NS and gp == 1)
                        kts_used.on(mm)
                for gp in range(2):
                    mm = pe.matmul(S[:, 256:264], Q2[:, 0, gp, :], KN[:, br, gp, :], start=gp == 0, stop=gp == 1)
                ss_done.on(mm)
                q = q0 + NS
                bank = q_bank(pe, q)
                pe.wait_ge(sp_ok.sem, br + 2)
                for kt in range(2):
                    pe.transpose(bank[:, kt * P:(kt + 1) * P], PS[:, kt * P:(kt + 1) * P], IDENT)
                q_fill.on(pe.transpose(bank[0:NS, 2 * P:3 * P], PS[:, 256:264], IDENT))
                q_wait_drained(pe, q)
                pe.wait_ge(oa_ok.sem, br + 1)
                for n in range(NS):
                    for kt in range(2):
                        pe.matmul(O[:, 0:256], PTP[:, kt, n, :], KVS[:, n, kt, 256:512], start=n == 0 and kt == 0, stop=False)
                spv_done.on(pe.matmul(O[:, 0:256], PTN[0:NS, :], VN[br], start=False, stop=True))
            q = Q_SMP + 1 + 2 * (NS + 1)
            bank = q_bank(pe, q)
            pe.wait_ge(om_ok.sem, 1)
            q_fill.on(pe.transpose(bank[:, 0:P], OM[:, :, :].rearrange("p e d -> p (e d)"), IDENT))

        def split_heads(gp, e):
            r = slice(e * HD, (e + 1) * HD)
            return r, slice(gp * 4, gp * 4 + 4), (2 * gp + e) * 4

        def dve_inq(dve):
            dve.wait_ge(d_ca, 32)
            dve.tensor_copy(CBF[:, 0:P], IDENT)
            vec.on(dve.tensor_copy(CBF[:, P:2 * P], SQ[:, 0, 0:P]))
            dve.wait_ge(vec.sem, vec.now)
            dve.wait_ge(tile_out.sem, U0["inq"] + 2)
            prompt_ct(dve, 0)
            for n, job in enumerate(SETUP):
                if job[0] == "rope":
                    rope_dve(dve, job[1], ROPE_K[job[1]], P0[:, ROPE_K[job[1]], :])
                else:
                    drain_job(dve, 0, job)
                if n % 4 == 3:
                    project(dve, "inq", n // 4)
                if n == 7:
                    dve.wait_ge(rope_ok.sem, 4)
                    for br in range(2):
                        for gp in range(2):
                            kn = dve.tensor_copy(KN[:, br, gp, :], P0[:, KV_TILE[br] + gp, SEQ:T])
                    vec.on(kn)
            project(dve, "inq", KD - 1)

        def project(dve, name, m):
            u = U0[name] + m
            dve.wait_ge(tile_done.sem, u + 1)
            tile_out.on(dve.tensor_tensor(row(P0, m), sets(u % 2), halves(RSTD[:, :]), ALU.mult))

        def prompt_ct(dve, kv):
            for gp in range(2):
                c = dve.tensor_copy(CT[:, :, 256 + gp * NC:256 + (gp + 1) * NC],
                                    P0[:, 8 + 2 * kv + gp, 0:SEQ].rearrange("p (s r) -> p r s", r=16))
            ct_prompt.on(c)

        def dve_attention(dve):
            MX, NB, SUM, F = (ST8[:, 8 * n:8 * n + 8] for n in range(4))
            CM = [ST8[:, 32 * n:32 * n + 32].rearrange("p (i x) -> p i x", i=QT) for n in (1, 2)]

            def chain(ins):
                vec.on(ins)
                dve.wait_ge(vec.sem, vec.now)

            def drain_ck(kv):
                dve.wait_ge(cmp_done.sem, kv + 1)
                chain(dve.tensor_copy(F[:, 0:1], M[:, 3, NCOL - 2:NCOL - 1]))
                ck_ok.on(dve.tensor_scalar((CKT, CVT)[kv][:, :], M[:, 3, 0:NCOL], F[:, 0:1], None, ALU.add))
                dve.wait_ge(ck_ok.sem, ck_ok.now)

            dve.wait_ge(tile_out.sem, tile_out.now)
            for m in range(KD):
                rope_dve(dve, 4 + m, m, QR[:, m, :])
            dve.wait_ge(rope_ok.sem, 4 + KD)
            dve.tensor_copy(QU[:, :, :], P0[:, 0:KD, SEQ:T])
            qs_ok.on(dve.tensor_copy(QS[:, :, :], QR[:, :, SEQ:T]))
            for gp in range(2):
                for e in range(2):
                    r = slice(e * HD, (e + 1) * HD)
                    for br in range(2):
                        c = dve.tensor_scalar(KP[r, br, 2 * gp + e, :], P0[r, KV_TILE[br] + gp, 0:SEQ], SCALE, None, ALU.mult)
            kp_ok.on(c)
            drain_ck(0)
            for gp in range(2):
                for e in range(2):
                    r = slice(e * HD, (e + 1) * HD)
                    c = dve.tensor_copy(CKP[r, gp, e, :], CKT[r, 256 + gp * NC:256 + (gp + 1) * NC])
            ckp_ok.on(c)
            prompt_ct(dve, 1)
            for job in SETUP_V:
                drain_job(dve, 0, job)

            def bias01(base):
                return CA[:, base:base + QT * NC].rearrange("p (i c) -> p i c", i=QT)

            dve.wait_ge(qs_ok.sem, 1)
            for gp in range(2):
                dve.wait_ge(cs_done.sem, 4 * gp + 4)
                for i in range(QT):
                    c = dve.scalar_tensor_tensor(
                        out=TC[gp][:, i], in0=PG[:, gp, i // 2, i % 2 * 256:i % 2 * 256 + 256].rearrange("p (x c) -> p x c", c=NC),
                        scalar=SCALE, in1=bias01(C_CB)[:, i].unsqueeze(1).to_broadcast([P, 8, NC]),
                        op0=ALU.mult, op1=ALU.add)
                cs_out.on(c)
            dve.wait_ge(cs_out.sem, 2)
            for gp in range(2):
                vec.on(dve.tensor_reduce(CM[gp], TC[gp][:, :, :, :], AX.X, ALU.max))
            dve.wait_ge(vec.sem, vec.now)
            for gp in range(2):
                c_max.on(dve.tensor_tensor(TC[gp][:, :, :, :], TC[gp][:, :, :, :],
                                           CM[gp].unsqueeze(3).to_broadcast([P, QT, 8, NC]), ALU.subtract))
            for gp in range(2):
                dve.wait_ge(c_exp.sem, gp + 1)
                for i in range(QT):
                    c = dve.tensor_tensor(TC[gp][:, i], TC[gp][:, i],
                                          bias01(C_CV)[:, i].unsqueeze(1).to_broadcast([P, 8, NC]), ALU.mult)
                vec.on(c)
            dve.wait_ge(vec.sem, vec.now)
            for gp in range(2):
                vec.on(dve.tensor_reduce(CM[gp], TC[gp][:, :, :, :], AX.X, ALU.add))
            CM2 = ST8[:, 32:96]
            dve.wait_ge(vec.sem, vec.now)
            chain(dve.tensor_scalar(CM2, CM2, 1e-30, None, ALU.max))
            chain(dve.reciprocal(CM2, CM2))
            dve.wait_ge(gt_ok.sem, 1)
            for gp in range(2):
                g = GT[:, :, :].rearrange("p i (g j b) -> p i g j b", g=NKV, b=3)[:, :, 2 * gp:2 * gp + 2, :, 0]
                for i in range(QT):
                    cm = CM[gp][:, i, :].rearrange("p (j e) -> p e j", e=2)
                    c = dve.tensor_tensor(cm, cm, g[:, i], ALU.mult)
            chain(c)
            for gp in range(2):
                c_ready.on(dve.tensor_tensor(TC[gp][:, :, :, :], TC[gp][:, :, :, :],
                                             CM[gp].unsqueeze(3).to_broadcast([P, QT, 8, NC]), ALU.mult))

            def row_max(hu):
                gp, i, e, br = STEPS[hu]
                o = 4 * (hu % 2)
                for j in range(4):
                    dve.wait_ge(s_done.sem, 4 * hu + j + 1)
                    nb_ok.on(dve.tensor_reduce(NB[:, o + j:o + j + 1], PG[:, j // 2, j % 2, 0:(i + 1) * P], AX.X, ALU.max,
                                               negate=True))

            def scale_probs(hu):
                gp, i, e, br = STEPS[hu]
                o = 4 * (hu % 2)
                dve.wait_ge(exp_done.sem, 4 * hu + 4)
                chain(dve.reciprocal(F[:, o:o + 4], SUM[:, o:o + 4]))
                g = GT[:, i, :].rearrange("p (g j b) -> p g j b", g=NKV, b=3)[:, 2 * gp + e, :, 1 + br]
                chain(dve.tensor_tensor(F[:, o:o + 4], F[:, o:o + 4], g, ALU.mult))
                for j in range(4):
                    pj = PB[:, hu % 2, j, 0:(i + 1) * P]
                    c = dve.tensor_scalar(pj, pj, F[:, o + j:o + j + 1], None, ALU.mult)
                p_ready.on(c)

            def o_low(un):
                gp, i, e = UNITS[un]
                r = slice(e * HD, (e + 1) * HD)
                dve.wait_ge(o_hi.sem, un + 1)
                o_out.on(dve.tensor_tensor(
                    G[r, gp * 4:gp * 4 + 4, 1, i * P:(i + 1) * P], M[r, 2 + un % 2, :].rearrange("p (j q) -> p j q", j=4),
                    G[r, gp * 4:gp * 4 + 4, 0, i * P:(i + 1) * P].bitcast(F32), ALU.subtract))

            row_max(0)
            drain_ck(1)
            drain_cv(dve, 0)
            scale_probs(0)
            for hu in range(len(STEPS)):
                bs = turned(hu)
                for q, rows in bs[:2]:
                    drain_pt(dve, 0, q, rows)
                if hu % 2 == 0 and hu:
                    o_low(hu // 2 - 1)
                if hu + 1 < len(STEPS):
                    row_max(hu + 1)
                for q, rows in bs[2:3]:
                    drain_pt(dve, 0, q, rows)
                if hu + 1 < len(STEPS):
                    scale_probs(hu + 1)
                for q, rows in bs[3:]:
                    drain_pt(dve, 0, q, rows)
            o_low(len(UNITS) - 1)
            dve_samples(dve, chain)

        def turned(hu):
            return [(q_unit[hu // 2], NC)] * (hu % 2 == 0) + [(q_step[hu] + kt, P) for kt in range(STEPS[hu][1] + 1)]

        def drain_pt(eng, mine, q, rows):
            x = q - Q_ATT
            drains(eng, mine, q, [(PT[0:rows, x % 4, :], M[0:rows, q % 2, :])], [(pv_done.sem, x - 3)] if x >= 4 else [])

        def dve_samples(dve, chain):
            MXS, NBS, SMS, FS = (ST8[:, n:n + 1] for n in range(4))
            S, O = PG[:, 0, 0, :], PG[:, 0, 1, :]
            dve.wait_ge(at_g.sem, 10)
            for gp in range(2):
                for e in range(2):
                    r, tiles, row0 = split_heads(gp, e)
                    for rot, src in ((0, QS[r, tiles, :]), (1, QU[r, tiles, :])):
                        q2 = Q2[r, rot, gp, :].rearrange("p (n h) -> p h n", h=16)[:, row0:row0 + 4, :]
                        c = dve.tensor_copy(q2, src)
                    for n in range(NS):
                        c = dve.tensor_copy(QPD[r, n, gp, n * 16 + row0:n * 16 + row0 + 4], QS[r, tiles, n])
            qpd_ok.on(c)
            for n in range(3):
                w, base = (P, 264) if n == 0 else (264, 0)
                if n:
                    q0 = Q_SMP + 1 + (NS + 1) * (n - 1)
                    for k2 in range(NS):
                        drain_kts(dve, 0, q0, n - 1, k2)
                dve.wait_ge(ss_done.sem, n + 1)
                dve.wait_ge(d_cs, 16)
                chain(dve.scalar_tensor_tensor(out=SCS[:, 0:w], in0=S[:, 0:w], scalar=SCALE, in1=CS[:, base:base + w],
                                               op0=ALU.mult, op1=ALU.add))
                chain(dve.tensor_reduce(MXS, SCS[:, 0:w], AX.X, ALU.max))
                snb_ok.on(dve.tensor_scalar(NBS, MXS, -1.0, None, ALU.mult))
                dve.wait_ge(sp_ok.sem, n + 1)
                dve.wait_ge(d_gs, 16)
                chain(dve.reciprocal(FS, SMS))
                chain(dve.tensor_tensor(FS, FS, GS[:, n:n + 1], ALU.mult))
                drain_p(dve, 0, n)
                if n == 0:
                    dve.wait_ge(sv_done.sem, 1)
                    oa_ok.on(dve.tensor_scalar(OA[:, :], O[:, 0:256], FS, None, ALU.mult))
                else:
                    dve.wait_ge(spv_done.sem, n)
                    dve.wait_ge(oa_ok.sem, oa_ok.now)
                    oa_ok.on(dve.scalar_tensor_tensor(out=OA[:, :], in0=O[:, 0:256], scalar=FS, in1=OA[:, :],
                                                      op0=ALU.mult, op1=ALU.add))
            dve.wait_ge(oa_ok.sem, 3)
            for e in range(2):
                chain(dve.tensor_scalar(OM[:, e, :], OA[:, e * HD:(e + 1) * HD], CS[:, 264 + P + e:264 + P + e + 1],
                                        None, ALU.mult))
                c = dve.scalar_tensor_tensor(
                    out=OM[:, e, :], in0=OA[:, (2 + e) * HD:(3 + e) * HD], scalar=CS[:, 264 + P + 2 + e:264 + P + 3 + e],
                    in1=OM[:, e, :], op0=ALU.mult, op1=ALU.add)
            om_ok.on(c)
            drain_os(dve, 0)
            dve.wait_ge(os_hi.sem, 1)
            q_wait_drained(dve, Q_SMP + 1 + 2 * (NS + 1))
            for m in range(KD):
                g_ready.on(dve.tensor_tensor(G[:, m, 1, SEQ:T], OS[:, m, :], G[:, m, 0, SEQ:T].bitcast(F32), ALU.subtract))

        def drain_kts(eng, mine, q0, br, n):
            x = NS * br + n
            drains(eng, mine, q0 + n, [(KTS[:, n % 2, :, :].rearrange("p g k -> p (g k)"), M[:, (q0 + n) % 2, :])],
                   [(kts_used.sem, x - 1)] if x >= 2 else [])

        def drain_p(eng, mine, n):
            if n == 0:
                drains(eng, mine, Q_SMP, [(PTN[:, :], M[:, Q_SMP % 2, 0:P])], [(at_g.sem, 10)])
                return
            q = Q_SMP + (NS + 1) * n
            src = M[:, q % 2, :]
            copies = [(PTP[:, kt, s, s * 16:(s + 1) * 16], src[:, kt * P + s * 16:kt * P + (s + 1) * 16])
                      for kt in range(2) for s in range(NS)]
            copies.append((PTN[0:NS, :], src[0:NS, 2 * P:3 * P]))
            drains(eng, mine, q, copies, [(spv_done.sem, 1)] if n == 2 else [(sv_done.sem, 1)])

        def drain_os(eng, mine):
            q = Q_SMP + 1 + 2 * (NS + 1)
            src = M[:, q % 2, 0:P].rearrange("p (n h) -> p h n", h=16)
            drains(eng, mine, q, [(OS[r, tiles, :], src[r, row0:row0 + 4, :])
                                  for gp in range(2) for e in range(2) for r, tiles, row0 in (split_heads(gp, e),)])

        def act_inq(act):
            act.wait_ge(g_ready.sem, 8 + KF)
            for n, job in enumerate(SETUP):
                if n % 8 == 0 and n < 24:
                    split_hi(act, (S0["inq"] + n // 8 + 1) % 2, raw_of("inq", n // 8 + 1),
                             (tile_done, U0["inq"] + n // 4))
                if job[0] != "rope":
                    drain_job(act, 1, job)

        def act_attention(act):
            act.wait_ge(q_a.sem, Q_OF["gate", 1] // 2 + 1)
            act.wait_ge(q_v.sem, Q_OF["gate", 0] // 2 + 1)
            gt_ok.on(act.activation(GT[:, :, :], GT[:, :, :], ACT.Sigmoid))
            gt_ok.on(act.activation(SGT[:, :], SGT[:, :], ACT.Sigmoid))
            for job in SETUP_V:
                if job == SETUP_V[0]:
                    act.wait_ge(cmp_done.sem, 1)
                drain_job(act, 1, job)
            for gp in range(2):
                act.wait_ge(c_max.sem, gp + 1)
                c_exp.on(act.activation(TC[gp][:, :, :, :], TC[gp][:, :, :, :], ACT.Exp))
            MX, NB, SUM, F = (ST8[:, 8 * n:8 * n + 8] for n in range(4))

            def exps(hu):
                gp, i, e, br = STEPS[hu]
                o, n = 4 * (hu % 2), (i + 1) * P
                if hu >= 2:
                    act.wait_ge(q_fill.sem, q_step[hu - 2] + STEPS[hu - 2][1] + 1)
                for j in range(4):
                    act.wait_ge(nb_ok.sem, 4 * hu + j + 1)
                    exp_done.on(act.activation(PB[:, hu % 2, j, 0:n], PG[:, j // 2, j % 2, 0:n], ACT.Exp,
                                               bias=NB[:, o + j:o + j + 1], scale=1.0,
                                               accum_out=SUM[:, o + j:o + j + 1]))

            def o_high(un):
                gp, i, e = UNITS[un]
                act.wait_ge(pv_done.sem, q_step[2 * un + 1] + i + 1 - Q_ATT)
                r = slice(e * HD, (e + 1) * HD)
                o_hi.on(act.activation(G[r, gp * 4:gp * 4 + 4, 0, i * P:(i + 1) * P],
                                       M[r, 2 + un % 2, :].rearrange("p (j q) -> p j q", j=4), ACT.Copy))

            exps(0)
            drain_cv(act, 1)
            for hu in range(len(STEPS)):
                bs = turned(hu)
                for q, rows in bs[:2]:
                    drain_pt(act, 1, q, rows)
                if hu % 2 == 0 and hu:
                    o_high(hu // 2 - 1)
                if hu + 1 < len(STEPS):
                    exps(hu + 1)
                for q, rows in bs[2:]:
                    drain_pt(act, 1, q, rows)
                if hu == 1:
                    split_hi(act, S0["out1"] % 2, raw_of("out1", 0), (cmp_done, 2))
            o_high(len(UNITS) - 1)
            act.wait_ge(at_g.sem, 10)
            for n in range(3):
                w = P if n == 0 else 264
                if n:
                    q0 = Q_SMP + 1 + (NS + 1) * (n - 1)
                    for k2 in range(NS):
                        drain_kts(act, 1, q0, n - 1, k2)
                act.wait_ge(snb_ok.sem, n + 1)
                sp_ok.on(act.activation(PS[:, 0:w], SCS[:, 0:w], ACT.Exp, bias=ST8[:, 1:2], scale=1.0,
                                        accum_out=ST8[:, 2:3]))
                drain_p(act, 1, n)
            drain_os(act, 1)
            q_wait_drained(act, Q_SMP + 1 + 2 * (NS + 1))
            os_hi.on(act.activation(G[:, 0:KD, 0, SEQ:T], OS[:, :, :], ACT.Copy))

        G0 = {"out0": 0, "down0": 8, "out1": 8 + KF, "down1": 16 + KF}
        block = ctx.enter_context(nc.Block())
        layer1 = FULL

        @block.sync
        def _(sp):
            sp.dma_start(XL[:, :, :], a["x_prompt"][0].rearrange("(i p) c -> p i c", p=P)).then_inc(d_in, 16)
            sp.dma_start(XS[:, :], a["x_sample"][:, 0, :]).then_inc(d_in, 16)
            sp.dma_start(BASE[:, :], a["c_base"]).then_inc(d_small, 16)
            for r, x in ((0, a["norm_mix"].rearrange("l (k p) -> (l k) p", p=P)),
                         (16, a["norm_ffn"].rearrange("l (k p) -> (l k) p", p=P)),
                         (32, a["norm_final"].rearrange("(k p) -> k p", p=P)),
                         (40, a["conv_w"].rearrange("j (k p) -> (j k) p", p=P)),
                         (52, a["norm_v"].rearrange("(k p) -> k p", p=P))):
                sp.dma_start(GROW[r:r + x.shape[0], :], x).then_inc(d_small, 16)
            sp.dma_start(TRIL[:, :], a["c_tril"]).then_inc(d_small, 16)
            sp.dma_start(SCV[:, :], a["state_conv"].rearrange("n j c -> (n j) c")).then_inc(d_small, 16)
            sp.dma_start(WSP[:, :, :], a["w_spatial"].rearrange("h t s -> t h s")).then_inc(d_small, 16)
            sp.dma_start(BSP[:, :, :].rearrange("p h t -> p (h t)"),
                         a["b_spatial"].rearrange("h t -> (h t)").partition_broadcast(P)
                         ).then_inc(d_small, 16)
            sp.dma_start(W00[:, :, :], a["w_spatial"][:, 0, 0:8].partition_broadcast(P)).then_inc(d_small, 16)
            sp_cols(sp, "in0", w0, 5)
            sp_cols(sp, "out0", wo0, 2)
            sp.dma_start(out[3][:, 0, :], a["state_conv"][:, 1, :]).then_inc(d_out, 16)
            sp.wait_ge(cv_ok.sem, 1)
            sp.dma_start(out[4][:, 0, :], CV[:, :]).then_inc(d_out, 16)
            sp.wait_ge(zo_ok.sem, 1)
            sp.dma_start(out[2][0], ZO[0:2, :]).then_inc(d_out, 16)
            sp.dma_start(out[3][:, 1, :], ZO[2:10, :]).then_inc(d_out, 16)
            outs[0] += 4
            sp_up(sp, "up0", wup[0])
            sp_down(sp, "down0", wdn[0])
            if layer1:
                sp_layer1(sp)
                sp_cols_out1(sp)
                sp_up(sp, "up1", wup[1])
                sp_down(sp, "down1", wdn[1])
            for i in range(QT):
                sp.wait_ge(fin_v.sem, 8 + 2 * (i + 1))
                sp.dma_start(out[0][0, i * P:(i + 1) * P, :], YO[:, i, :]).then_inc(d_out, 16)
                outs[0] += 1
            sp.wait_ge(fin_v.sem, 8 + 10)
            sp.dma_start(out[1][:, 0, :], YS[:, :]).then_inc(d_out, 16)
            outs[0] += 1
            sp.wait_ge(d_out, 16 * outs[0])

        @block.gpsimd
        def _(pool):
            pool.sem_inc(w_split.sem, 2)
            def split_lo(s, b):
                pool.wait_ge(w_hi.sem, s + 1)
                w_split.on(pool.tensor_tensor(WL[:, b, :], WR[:, b, :], WH[:, b, :].bitcast(F32), ALU.subtract))
            def split_slots(s0, n):
                with pool.Fori(0, n // 2) as t:
                    for b in range(2):
                        split_lo(t * 2 + s0 + b, (s0 + b) % 2)
                if n % 2:
                    split_lo(s0 + n - 1, (s0 + n - 1) % 2)
            if not layer1:
                split_slots(0, S0["inq"])
            else:
                split_slots(0, S0["out1"])
                pool_layer1(pool, split_lo)
                pool.wait_ge(at_g.sem, at_g.now)
                split_slots(S0["out1"] + 1, _s - S0["out1"] - 1)

        @block.tensor
        def _(pe):
            fills = [0]

            def fill_start():
                if fills[0] >= 4:
                    pe.wait_ge(t_drain.sem, fills[0] - 3)
                return M[:, fills[0] % 4, :]

            def fill_end(mm):
                t_fill.on(mm)
                fills[0] += 1

            pe.wait_ge(d_small, 16 * N_SMALL)
            bank = fill_start()
            fill_end(pe.transpose(bank[:, 0:N_GAIN], GROW[:, :], IDENT[0:N_GAIN, 0:N_GAIN]))
            bank = fill_start()
            for f in range(FT):
                mm = pe.transpose(bank[:, 16 * f:16 * f + 16], SCV[:, f * P:(f + 1) * P], IDENT[0:16, 0:16])
            fill_end(mm)
            bank = fill_start()
            for h in range(4):
                mm = pe.transpose(bank[:, h * P:(h + 1) * P], WSP[:, h, :], IDENT)
            fill_end(mm)
            pe.wait_ge(d_in, 32)
            bank = fill_start()
            for kk in range(KD):
                mm = pe.transpose(bank[:, 8 * kk:8 * kk + 8], XS[:, kk * P:(kk + 1) * P], IDENT[0:NS, 0:NS])
            fill_end(mm)
            for kk in range(KD):
                bank = fill_start()
                for i in range(QT):
                    mm = pe.transpose(bank[:, i * P:(i + 1) * P], XL[:, i, kk * P:(kk + 1) * P], IDENT)
                fill_end(mm)
            pe.wait_ge(t_drain.sem, 12)
            pe_stat(pe, 0)
            pe_wide(pe, "in0", H, 5, (h_ready, 0))
            pe.wait_ge(accv_ok.sem, FT)
            for hf in range(2):
                mm = pe.matmul(M[:, hf, 0:HALF], ONES, ACV[:, hf * HALF:(hf + 1) * HALF], start=True, stop=True)
            stv_done.on(mm)
            for f in range(FT):
                pe.wait_ge(vn_ok.sem, f + 1)
                if f >= 2:
                    pe.wait_ge(vt_drain.sem, f - 1)
                v = P0[:, 16 + f, :]
                pe.transpose(M[0:NS, 0, f * P:(f + 1) * P], v[:, SEQ:T], IDENT)
                for c in range(QT):
                    mm = pe.transpose(M[:, 2 + f % 2, c * P:(c + 1) * P], v[:, c * P:(c + 1) * P], IDENT)
                vt_fill.on(mm)
            pe.wait_ge(z_ok.sem, FT)
            for f in range(FT):
                mm = pe.transpose(M[0:10, 1, f * P:(f + 1) * P], P0[:, 8 + f, SEQ - 2:T], IDENT)
            zo_fill.on(mm)
            pe.wait_ge(vt_drain.sem, FT)
            for f, bank in enumerate((2, 3, 0, 1)):
                if f == 2:
                    pe.wait_ge(cv_ok.sem, 1)
                if f == 3:
                    pe.wait_ge(zo_ok.sem, 1)
                for c in range(QT):
                    mm = pe.matmul(M[:, bank, c * P:(c + 1) * P], VT[:, f, c, :], WT[:, f, :], start=True, stop=True)
                mixed.on(mm)
            pe_wide(pe, "out0", G, 2, (g_ready, G0["out0"]))
            pe_stat(pe, 1)
            pe_wide(pe, "up0", H, KF // 2, (h_ready, 8))
            pe_down(pe, "down0", (g_ready, G0["down0"]))
            pe_stat(pe, 2)
            if layer1:
                pe_wide(pe, "in1", H, 3, (h_ready, 16), tail=True)
                pe_inq(pe)
                pe_attention(pe)
                pe_wide(pe, "out1", G, 2, (g_ready, G0["out1"]))
                pe_stat(pe, 3)
                pe_wide(pe, "up1", H, KF // 2, (h_ready, 24))
                pe_down(pe, "down1", (g_ready, G0["down1"]))
                pe_stat(pe, 4)
            pe.wait_ge(fin_v.sem, 8)
            for i in range(QT):
                for hf in range(2):
                    n = 2 * i + hf
                    if n >= 4:
                        pe.wait_ge(fin_v.sem, 8 + n - 3)
                    for kk in range(4):
                        mm = pe.transpose(M[:, n % 4, kk * P:(kk + 1) * P],
                                          XT[:, 4 * hf + kk, i * P:(i + 1) * P], IDENT)
                    fin_p.on(mm)
            for hf in range(2):
                pe.wait_ge(fin_v.sem, 8 + 5 + hf)
                for kk in range(4):
                    mm = pe.transpose(M[0:NS, hf, kk * P:(kk + 1) * P], XT[:, 4 * hf + kk, SEQ:T], IDENT)
                fin_p.on(mm)

        @block.scalar
        def _(act):
            split_hi(act, 0, 32)
            for m in range(KD):
                res_act(act, 0, m, G_MIX[0], m % 2, (t_drain.sem, 5 + m))
            norm_act(act, 0)
            split_hi(act, 1, 32)
            with loop(act, 4, [(w_hi, 2)]) as t:
                for j in (1, 2):
                    s = j + 1
                    split_hi(act, s % 2, t * 32 + 32 * (s // 2 + 1), (tile_done, t * 4 + 2 * j))
            split_hi(act, 0, 32 * 6, (tile_done, 18))
            for f in range(FT):
                act.wait_ge(tile_out.sem, U0["in0"] + 16 + f + 3)
                vg_ok.on(act.activation(P0[:, 16 + f, :], P0[:, 16 + f, :], ACT.Gelu_apprx_tanh))
                act.wait_ge(vg_ok.sem, vg_ok.now)
                if f >= 2:
                    act.wait_ge(accv_ok.sem, f - 1)
                vsq_ok.on(act.activation(SQ[:, f % 2, :], P0[:, 16 + f, :], ACT.Square))
            for f in range(FT):
                ug_ok.on(act.activation(P0[:, 12 + f, :], P0[:, 12 + f, :], ACT.Gelu_apprx_tanh))
            act.wait_ge(stv_done.sem, 1)
            stdv_ok.on(act.activation(halves(ACV[:, :]), M[:, 0:2, 0:HALF], ACT.Sqrt, bias=EPSC, scale=1.0 / DC))
            for f in range(2 * FT):
                act.wait_ge(y_ok.sem, f + 1)
                y_hi.on(act.activation(G[:, f, 0, :], TG[:, f % 2, :], ACT.Copy))
            act_residual(act, "out0", 1, G_FFN[0], 4)
            norm_act(act, 1)
            act_up(act, "up0", 0)
            if not layer1:
                act_residual(act, "down0", 2, G_MIX[1], 2, final=True)
                norm_act(act, 2)
            else:
                act_residual(act, "down0", 2, G_MIX[1], 2)
                norm_act(act, 2)
                with loop(act, 3, [(w_hi, 2)]) as t:
                    for j in range(2):
                        split_next_wide(act, "in1", t, j)
                split_next_wide(act, "in1", 3, 0)
                act_inq(act)
                act_attention(act)
                act_residual(act, "out1", 3, G_FFN[1], 4)
                norm_act(act, 3)
                act_up(act, "up1", 1)
                act_residual(act, "down1", 4, G_FIN, 2, final=True)
                norm_act(act, 4)

        @block.vector
        def _(dve):
            dve.sem_inc(tile_out.sem, 2)
            tile_out.n = 2
            acc_ok.on(dve.memset(ACC[:, :], 0.0))

            def take(n, dst, src):
                dve.wait_ge(t_fill.sem, n + 1)
                return dve.tensor_copy(dst, src)
            t_drain.on(take(0, GAINS[:, :], M[:, 0, 0:N_GAIN]))
            t_drain.on(take(1, HT[:, :, :].rearrange("p f n -> p (f n)"), M[:, 1, 0:64]))
            dve.wait_ge(t_fill.sem, 3)
            t_drain.on(dve.tensor_tensor(WT[:, :, :], M[:, 2, :].rearrange("p (h t) -> p h t", h=4),
                                         TRIL[:, :].unsqueeze(1).to_broadcast([P, 4, P]), ALU.mult))
            t_drain.on(take(3, XT[:, :, SEQ:T], M[:, 3, 0:64].rearrange("p (k n) -> p k n", k=KD)))
            for m in range(KD):
                t_drain.on(take(4 + m, XT[:, m, 0:SEQ], M[:, m % 4, :]))
            for m in range(KD):
                res_dve(dve, 0, m, G_MIX[0], m % 2, (t_drain.sem, 5 + m))
            norm_dve(dve, 0)
            dve_project(dve, "in0", 5)
            for f in range(FT):
                dve.wait_ge(vsq_ok.sem, f + 1)
                if f == 0:
                    accv_ok.on(dve.tensor_copy(ACV[:, :], SQ[:, 0, :]))
                else:
                    dve.wait_ge(accv_ok.sem, f)
                    accv_ok.on(dve.tensor_tensor(ACV[:, :], ACV[:, :], SQ[:, f % 2, :], ALU.add))
            for f in range(FT):
                z_ok.on(dve.tensor_tensor(P0[:, 8 + f, :], P0[:, 4 + f, :], P0[:, 8 + f, :], ALU.mult))
            dve.wait_ge(stdv_ok.sem, 1)
            vec.on(dve.reciprocal(ACV[:, :], ACV[:, :]))
            dve.wait_ge(vec.sem, vec.now)
            for f in range(FT):
                v = P0[:, 16 + f, :]
                vn_ok.on(dve.scalar_tensor_tensor(out=v, in0=v, scalar=GAINS[:, G_V + f:G_V + f + 1],
                                                  in1=ACV[:, :], op0=ALU.mult, op1=ALU.mult))
            for f in range(FT):
                dve.wait_ge(vt_fill.sem, f + 1)
                vt_drain.on(dve.tensor_copy(VT[:, f, :, :].rearrange("p c s -> p (c s)"), M[:, 2 + f % 2, :]))
            cv_ok.on(dve.tensor_copy(CV[:, :], M[0:NS, 0, :]))
            dve.wait_ge(zo_fill.sem, 1)
            zo_ok.on(dve.tensor_copy(ZO[:, :], M[0:10, 1, :]))

            def y_low(f):
                dve.wait_ge(y_hi.sem, f + 1)
                g_ready.on(dve.tensor_tensor(G[:, f, 1, :], TG[:, f % 2, :], G[:, f, 0, :].bitcast(F32), ALU.subtract))

            for f in range(FT):
                z, co = P0[:, 8 + f, :], TA[:, f % 2, :]

                def tap(j):
                    c = G_CONV + j * FT + f
                    return GAINS[:, c:c + 1]

                def mac(dst, src, j):
                    dve.wait_ge(vec.sem, vec.now)
                    vec.on(dve.scalar_tensor_tensor(out=dst, in0=src, scalar=tap(j), in1=dst,
                                                    op0=ALU.mult, op1=ALU.add))
                dve.wait_ge(z_ok.sem, FT)
                vec.on(dve.tensor_scalar(co, z, tap(2), None, ALU.mult))
                mac(co[:, 1:SEQ], z[:, 0:SEQ - 1], 1)
                mac(co[:, 2:SEQ], z[:, 0:SEQ - 2], 0)
                mac(co[:, SEQ:T], HT[:, f, 1:16:2], 1)
                mac(co[:, SEQ:T], HT[:, f, 0:16:2], 0)
                dve.wait_ge(vec.sem, vec.now)
                y_ok.on(dve.tensor_tensor(TG[:, f % 2, :], P0[:, f, :], co, ALU.mult))
                dve.wait_ge(y_ok.sem, y_ok.now)
                y_low(f)
            for f, bank in enumerate((2, 3, 0, 1)):
                mv = TA[:, f % 2, :]
                dve.wait_ge(mixed.sem, f + 1)
                dve.tensor_tensor(mv[:, 0:SEQ].rearrange("p (c t) -> p c t", c=QT),
                                  M[:, bank, :].rearrange("p (c t) -> p c t", c=QT),
                                  BSP[:, f, :].unsqueeze(1).to_broadcast([P, QT, P]), ALU.add)
                vec.on(dve.tensor_scalar(mv[:, SEQ:T], P0[:, 16 + f, SEQ:T], W00[:, f, 0:1], BSP[:, f, 0:1],
                                         ALU.mult, ALU.add))
                dve.wait_ge(ug_ok.sem, f + 1)
                dve.wait_ge(vec.sem, vec.now)
                y_ok.on(dve.tensor_tensor(TG[:, f % 2, :], P0[:, 12 + f, :], mv, ALU.mult))
                dve.wait_ge(y_ok.sem, y_ok.now)
                y_low(FT + f)
            dve_residual(dve, "out0", 1, G_FFN[0], 4)
            norm_dve(dve, 1)
            dve_up(dve, "up0", 0)
            dve_residual(dve, "down0", 2, G_MIX[1], 2)
            norm_dve(dve, 2)
            g_fin = G_MIX[1]
            if layer1:
                dve_project(dve, "in1", 3, tail=True, first=8)
                dve_inq(dve)
                dve_attention(dve)
                dve_residual(dve, "out1", 3, G_FFN[1], 4)
                norm_dve(dve, 3)
                dve_up(dve, "up1", 1)
                dve_residual(dve, "down1", 4, G_FIN, 2)
                norm_dve(dve, 4)
                g_fin = G_FIN
            for m in range(KD):
                fin_v.on(dve.scalar_tensor_tensor(out=XT[:, m, :], in0=XT[:, m, :], scalar=GAINS[:, g_fin + m:g_fin + m + 1],
                                                  in1=RSTD[:, :], op0=ALU.mult, op1=ALU.mult))
            for n in range(2 * QT):
                i, hf = n // 2, n % 2
                dve.wait_ge(fin_p.sem, n + 1)
                fin_v.on(dve.tensor_copy(YO[:, i, hf * 512:(hf + 1) * 512], M[:, n % 4, :]))
            for hf in range(2):
                dve.wait_ge(fin_p.sem, 9 + hf)
                fin_v.on(dve.tensor_copy(YS[:, hf * 512:(hf + 1) * 512], M[0:NS, hf, :]))


OUTS = [(1, SEQ, D), (NS, 1, D), (1, 2, DC), (NS, 2, DC), (NS, 1, DC), (1, SEQ, 4, NKV, HD),
        (NS, 1, 4, NKV, HD), (1, SEQ, 2, NKV, HD), (NS, 1, 2, NKV, HD)]
FULL = True


def kernel(**inputs):
    import concourse.bacc as bacc
    from concourse.bass_utils import run_bass_kernel_spmd

    nc = bacc.Bacc("TRN2", target_bir_lowering=False, num_devices=1)
    arrays, aps = {}, {}
    for name, x in {**inputs, **consts()}.items():
        x = np.ascontiguousarray(x)
        arrays["in_" + name] = x
        aps[name] = nc.dram_tensor("in_" + name, x.shape, mybir.dt.from_np(x.dtype), kind="ExternalInput").ap()
    outs = [nc.dram_tensor(f"out_{i}", s, F32, kind="ExternalOutput").ap() for i, s in enumerate(OUTS)]
    program(nc, aps, outs)
    r = run_bass_kernel_spmd(nc, [arrays], core_ids=[0])
    return tuple(r.results[0][f"out_{i}"] for i in range(len(OUTS)))
```

```python
from contextlib import ExitStack, contextmanager

import concourse.bass as bass
import numpy as np
from concourse import mybir

F32, F32R, BF16, I32 = mybir.dt.float32, mybir.dt.float32r, mybir.dt.bfloat16, mybir.dt.int32
ALU, ACT, AX = mybir.AluOpType, mybir.ActivationFunctionType, mybir.AxisListType

P = 128
D = 1024
SEQ, NS = 512, 8
T = SEQ + NS
HALF = T // 2
KD = D // P
DC = 512
FT = DC // P
FF = 2816
KF = FF // P
NH, NKV, HD = 16, 4, 64
PAST, PAGE = 256, 128
NPAGE = PAST // PAGE
SCALE = HD ** -0.5
NEG = -1e30
EPS = 1e-6
QT = SEQ // P
NC = 32
SEGS = 2 * NS * 16 + 2 * 32 + 3
NCOL = SEGS - 1
SLOT = 2048
KH = KF // 2

PHASES = [("in0", 10, 20), ("out0", 4, 8), ("up0", 22, 44), ("down0", 16, 8),
          ("in1", 7, 13), ("inq", 4, 8), ("out1", 4, 8), ("up1", 22, 44), ("down1", 16, 8)]
S0, U0 = {}, {}
_s = _u = 0
for _n, _a, _b in PHASES:
    S0[_n], U0[_n] = _s, _u
    _s, _u = _s + _a, _u + _b
RAW = {n: 64 if n in ("inq", "out1") else 32 for n, _, _ in PHASES}
RAW0, _c = {}, [0, 0]
for _n, _a, _ in PHASES:
    RAW0[_n] = tuple(_c)
    for _k in range(S0[_n], S0[_n] + _a):
        _c[_k % 2] += RAW[_n]
ORDER = [n for n, _, _ in PHASES]


def raw_of(name, j):
    b = (S0[name] + j) % 2
    slots = dict((n, k) for n, k, _ in PHASES)[name]
    if j < slots:
        return RAW0[name][b] + RAW[name] * (j // 2 + 1)
    nxt = ORDER[ORDER.index(name) + 1]
    return RAW0[nxt][b] + RAW[nxt]

G_MIX, G_FFN, G_FIN, G_CONV, G_V = (0, 8), (16, 24), 32, 40, 52
N_GAIN = 56

C_ROT, C_COS, C_SIN = 0, 128, 128 + T
C_CB = 128 + 2 * T
C_CV = C_CB + QT * NC
N_CA = C_CV + QT * NC


def consts():
    p = np.arange(P)
    eye = np.eye(P, dtype=np.float32)
    base = np.concatenate([eye, np.ones((P, P), np.float32), np.full((P, 8), EPS, np.float32)], 1)
    tril = (p[:, None] <= p[None, :]).astype(np.float32)
    rot = np.zeros((P, P), np.float32)
    for m in range(P):
        if m % 64 < 32:
            rot[m + 32, m] = -1.0
        else:
            rot[m - 32, m] = 1.0
    pos = np.concatenate([np.arange(SEQ), np.full(NS, PAST)]).astype(np.float32)
    inv = np.power(np.float32(10000.0), -np.arange(32, dtype=np.float32) * np.float32(2.0) / np.float32(HD))
    ang = inv.astype(np.float32)[p % 32][:, None] * pos[None, :]
    cb = np.zeros((P, QT, NC), np.float32)
    for i in range(QT):
        t = i * P + p[:, None]
        c = np.arange(NC)[None, :]
        cb[:, i] = ((16 * c + 31 <= t) & (c < 31)).astype(np.float32)
    att = np.concatenate([rot, np.cos(ang).astype(np.float32), np.sin(ang).astype(np.float32),
                          ((1 - cb) * np.float32(NEG)).reshape(P, -1), cb.reshape(P, -1)], 1)
    n_r, g_r = p // 16, (p % 16) // 4
    new = np.zeros((P, PAST + NS), np.float32)
    new[:, PAST:] = np.where(n_r[:, None] == np.arange(NS)[None, :], 0.0, NEG)
    cmp_ = np.where((n_r[:, None] == p[None, :] // 16) & (p[None, :] % 16 < 15), 0.0, NEG)
    grp = (g_r[:, None] == np.arange(4)[None, :]).astype(np.float32)
    smp = np.concatenate([new, cmp_, grp], 1).astype(np.float32)
    causal = np.where(p[None, :] > p[:, None], NEG, 0.0).astype(np.float32)
    return {"c_base": base, "c_tril": tril, "c_att": att, "c_smp": smp, "c_causal": causal}


class Count:

    def __init__(self, sem):
        self.sem, self.n, self.term = sem, 0, None

    def on(self, ins):
        ins.then_inc(self.sem, 1)
        self.n += 1
        return ins

    @property
    def now(self):
        return self.n if self.term is None else self.term + self.n


@contextmanager
def loop(eng, trips, per):
    with eng.Fori(0, trips) as t:
        first = {}
        for c, k in per:
            first[c] = c.n
            c.term = t * k
        yield t
        for c, k in per:
            assert c.n - first[c] == k, (c.sem, c.n - first[c], k)
    for c, k in per:
        c.term = None
        c.n += k * (trips - 1)


def program(nc, a, out):
    ctx = ExitStack()
    with ctx:
        lay = [16512]

        def at(name, shape, dt, offset):
            return nc.alloc_sbuf_tensor_at(name, shape, dt, offset=offset)

        def size(shape, dt):
            n = 2 if dt == BF16 else 4
            for k in shape[1:]:
                n *= k
            return (n + 31) // 32 * 32

        def new(name, shape, dt=F32):
            t = at(name, shape, dt, lay[0])
            lay[0] += size(shape, dt)
            return t

        def packed(offset, *tensors):
            got = []
            for name, shape, dt in tensors:
                got.append(at(name, shape, dt, offset))
                offset += size(shape, dt)
            return got, offset

        XT = new("XT", [P, KD, T])
        h_at = lay[0]
        H = new("H", [P, KD, 2, T], F32R)
        g_at = lay[0]
        G = new("G", [P, KF, 2, T], F32R)
        wr_at = lay[0]
        WR = new("WR", [P, 2, SLOT])
        wh_at = lay[0]
        WH = new("WH", [P, 2, SLOT], F32R)
        WL = new("WL", [P, 2, SLOT], F32R)
        BASE = new("BASE", [P, 2 * P + 8])
        IDENT, ONES, EPSC = BASE[:, 0:P], BASE[:, P:2 * P], BASE[:, 2 * P:2 * P + 1]
        GAINS = new("GAINS", [P, N_GAIN])
        rstd_at = lay[0]
        RSTD = new("RSTD", [P, T])
        ACC = new("ACC", [P, T])
        SQ = new("SQ", [P, 2, T])
        tmp_at = lay[0]
        TA = new("TA", [P, 2, T])
        TB = new("TB", [P, T])
        TG = new("TG", [P, 2, T])
        tmp_end = lay[0] + 2048
        assert tmp_end <= 229344, tmp_end
        s_at = g_at + 8 * 2 * T * 4
        s_end = g_at + KF * 2 * T * 4
        P0 = at("P0", [P, 21, T], F32, s_at)
        SQX = at("SQX", [P, KD, T], F32, g_at)
        (XL, XS), _ = packed(s_at, ("XL", [P, QT, D], F32), ("XS", [NS, D], F32))
        (BSP, WT, HT, SCV, WSP, ACV, W00, TRIL, GROW, ZO, CV), e = packed(
            s_at + 20 * T * 4, ("BSP", [P, 4, P], F32), ("WT", [P, 4, P], F32), ("HT", [P, FT, 16], F32),
            ("SCV", [16, DC], F32), ("WSP", [P, 4, P], F32), ("ACV", [P, T], F32), ("W00", [P, 4, 8], F32),
            ("TRIL", [P, P], F32), ("GROW", [N_GAIN, P], F32), ("ZO", [10, DC], F32), ("CV", [NS, DC], F32))
        assert e <= s_end, (e, s_end)
        XG = at("XG", [P, KD, T], F32, h_at)
        YO = at("YO", [P, QT, D], F32, wr_at)
        YS = at("YS", [NS, D], F32, wr_at + QT * D * 4)

        PG = ctx.enter_context(nc.psum_tensor("PG", [P, 2, 2, 512], F32))
        M = ctx.enter_context(nc.psum_tensor("M", [P, 4, 512], F32))

        def sem(name):
            return ctx.enter_context(nc.semaphore(name))

        CT = at("CT", [P, 16, SEGS], F32, g_at)
        NSTG = 5
        PST = at("PST", [P, NSTG, 2, 256], F32, g_at + size([P, 16, SEGS], F32))
        PEK = at("PEK", [32, 2, 2, HD], F32, g_at + size([P, 16, SEGS], F32) + NSTG * 2048)
        WBD = at("WBD", [P, 2, 32, P], F32, wh_at)
        (QR, KP), e = packed(h_at, ("QR", [P, KD, T], F32), ("KP", [P, 2, NKV, SEQ], F32))
        assert e <= g_at
        (VTK, KVO), e = packed(s_at + 21 * T * 4, ("VTK", [P, QT, 2, 256], F32), ("KVO", [P, 1536], F32))
        assert e <= s_end
        (PB, PT), e = packed(s_at + 8 * T * 4, ("PB", [P, 2, 4, SEQ], F32), ("PT", [P, 4, 512], F32))
        assert e <= s_at + 21 * T * 4
        TC = [at(f"TC{gp}", [P, QT, 8, NC], F32, s_at + gp * 4096) for gp in range(2)]
        (CA, CBF, GT, CVT, CKT, CVK, CKP), e = packed(
            tmp_at, ("CA", [P, N_CA], F32), ("CBF", [P, 2 * P], BF16), ("GT", [P, QT, 48], F32),
            ("CVT", [P, NCOL], F32), ("CKT", [P, NCOL], F32), ("CVK", [2 * NC, 2, P], F32), ("CKP", [P, 2, 2, NC], F32))
        assert e <= tmp_end, (e, tmp_end)
        (KN, GS, SGT, ST8, QS, QU, OS), e = packed(
            e, ("KN", [P, 2, 2, NS], F32), ("GS", [P, 3], F32), ("SGT", [NS, 48], F32),
            ("ST8", [P, 96], F32), ("QS", [P, KD, NS], F32), ("QU", [P, KD, NS], F32), ("OS", [P, KD, NS], F32))
        assert e <= 229344, e
        VN = [KVO[0:NS, 512 * b + 768:512 * b + 1024] for b in range(2)]
        CVS = at("CVS", [P, 2, P], F32, tmp_at + size([P, N_CA], F32) + 512 + size([P, QT, 48], F32))
        PTAB = at("PTAB", [1, 16], I32, s_end - 64)
        ROT, COS, SIN = CA[:, 0:P], CA[:, C_COS:C_COS + T], CA[:, C_SIN:C_SIN + T]
        lo_at = wh_at + 2 * SLOT * 4 + (S0["out1"] + 1) % 2 * SLOT * 4
        hi_at = wh_at + (S0["out1"] + 1) % 2 * SLOT * 4
        slot_at = [s_at + 4 * T * 4 + 2048 * n for n in range(4)] + [lo_at + 2048 * n for n in (1, 2, 3)] + [
            s_at + 8 * T * 4 + 2 * 16384]
        assert slot_at[3] + 2048 <= s_at + 8 * T * 4 and slot_at[7] + 2048 <= s_at + 21 * T * 4 + 8192
        SLOTS = [at(f"SLOT{n}", [P, 2, 256], F32, o) for n, o in enumerate(slot_at)]
        SV = at("SV", [P, NS, 2, 256], F32, s_at + 8 * T * 4)
        WK = at("WK", [P, NS, 2, 256], F32, s_at + 8 * T * 4 + 16384)
        KEYS = [SLOTS, [WK[:, n] for n in range(NS)]]
        VALS = [[SV[:, n] for n in range(NS)], SLOTS]
        QPD = at("QPD", [P, 2 * NS * P], F32, hi_at)
        Q2 = at("Q2", [P, 2, 2, P], F32, lo_at)
        CS = at("CS", [P, 264 + P + 4], F32, rstd_at + 2 * T * 4)
        (PTP0, PTP1, KTS, SCS, PS, OA, PTN, OM), e = packed(
            h_at, ("PTP0", [P, 2 * NS * P], F32), ("PTP1", [P, 2 * NS * P], F32), ("KTS", [P, 2, 2, 256], F32),
            ("SCS", [P, 3, 264], F32), ("PS", [P, 3, 264], F32), ("OA", [P, 256], F32), ("PTN", [P, 3, P], F32),
            ("OM", [P, 2, HD], F32))
        assert e <= g_at, (e, g_at)

        w_raw = [sem("w_raw0"), sem("w_raw1")]
        w_hi = Count(sem("w_hi"))
        w_split = Count(sem("w_split"))
        half_used = Count(sem("half_used"))
        tile_done = Count(sem("tile_done"))
        tile_out = Count(sem("tile_out"))
        h_ready = Count(sem("h_ready"))
        g_ready = Count(sem("g_ready"))
        a_hi = Count(sem("a_hi"))
        a_sq = Count(sem("a_sq"))
        x_sq = Count(sem("x_sq"))
        x_sum = Count(sem("x_sum"))
        acc_ok = Count(sem("acc_ok"))
        st_done = Count(sem("st_done"))
        a_std = Count(sem("a_std"))
        rstd_ok = Count(sem("rstd_ok"))
        a_silu = Count(sem("a_silu"))
        t_gate = Count(sem("t_gate"))
        a_ghi = Count(sem("a_ghi"))
        d_base, d_xs, d_gain = sem("d_base"), sem("d_xs"), sem("d_gain")
        d_x = [sem(f"d_x{i}") for i in range(QT)]
        d_small = sem("d_small")
        d_out = sem("d_out")
        outs = [0]
        t_fill = Count(sem("t_fill"))
        t_drain = Count(sem("t_drain"))
        vec = Count(sem("vec"))
        vg_ok = Count(sem("vg_ok"))
        vsq_ok = Count(sem("vsq_ok"))
        accv_ok = Count(sem("accv_ok"))
        stv_done = Count(sem("stv_done"))
        stdv_ok = Count(sem("stdv_ok"))
        vn_ok = Count(sem("vn_ok"))
        vt_fill = Count(sem("vt_fill"))
        vt_drain = Count(sem("vt_drain"))
        cv_ok = Count(sem("cv_ok"))
        z_ok = Count(sem("z_ok"))
        zo_fill = Count(sem("zo_fill"))
        zo_ok = Count(sem("zo_ok"))
        mix_out = Count(sem("mix_out"))
        mixed = Count(sem("mixed"))
        ug_ok = Count(sem("ug_ok"))
        y_ok = Count(sem("y_ok"))
        y_hi = Count(sem("y_hi"))
        at_g = Count(sem("at_g"))
        passed = sem("passed")
        q_fill = Count(sem("q_fill"))
        q_v = Count(sem("q_v"))
        q_a = Count(sem("q_a"))
        ct_prompt = Count(sem("ct_prompt"))
        cmp_done = Count(sem("cmp_done"))
        ck_ok = Count(sem("ck_ok"))
        rope_p = Count(sem("rope_p"))
        rope_in = Count(sem("rope_in"))
        rope_ok = Count(sem("rope_ok"))
        kp_ok = Count(sem("kp_ok"))
        qs_ok = Count(sem("qs_ok"))
        gt_ok = Count(sem("gt_ok"))
        cs_done = Count(sem("cs_done"))
        cs_out = Count(sem("cs_out"))
        c_max = Count(sem("c_max"))
        c_exp = Count(sem("c_exp"))
        ckp_ok = Count(sem("ckp_ok"))
        c_ready = Count(sem("c_ready"))
        s_done = Count(sem("s_done"))
        nb_ok = Count(sem("nb_ok"))
        exp_done = Count(sem("exp_done"))
        p_ready = Count(sem("p_ready"))
        pv_done = Count(sem("pv_done"))
        o_hi = Count(sem("o_hi"))
        o_out = Count(sem("o_out"))
        qpd_ok = Count(sem("qpd_ok"))
        ss_done = Count(sem("ss_done"))
        snb_ok = Count(sem("snb_ok"))
        sp_ok = Count(sem("sp_ok"))
        spv_done = Count(sem("spv_done"))
        oa_ok = Count(sem("oa_ok"))
        om_ok = Count(sem("om_ok"))
        os_hi = Count(sem("os_hi"))
        kts_used = Count(sem("kts_used"))
        d_ca, d_pt, d_pe = (sem(n) for n in ("d_ca", "d_pt", "d_pe"))
        d_wc = [sem("d_wc_k"), sem("d_wc_v")]
        d_kv, d_gs, d_cs = (sem(n) for n in ("d_kv", "d_gs", "d_cs"))
        d_page = [sem(f"d_page{n}") for n in range(NSTG)]
        d_keys = [[sem(f"d_keys{br}_{n}") for n in range(NS)] for br in range(2)]
        d_vals = [sem("d_vals_slc"), sem("d_vals_win")]
        N_PHYS = a["cache_kv"].shape[0]
        fin_p = Count(sem("fin_p"))
        fin_v = Count(sem("fin_v"))
        fin_a = Count(sem("fin_a"))


        def one(i):
            return bass.ds(i, 1)

        def sets(par):
            return PG[:, par, :, 0:HALF]

        def halves(x):
            return x.rearrange("p (h c) -> p h c", h=2)

        def row(x, m):
            return x[:, one(m), :].rearrange("p a (h c) -> p (a h) c", h=2)

        w0 = a["w_in0"].rearrange("(k p) c -> p k c", p=P)
        wo0 = a["w_out0"].rearrange("(k p) c -> p k c", p=P)
        w1 = a["w_in1"].rearrange("(k p) c -> p k c", p=P)
        wo1 = a["w_out1"].rearrange("(g e j d) c -> g j e d c", g=2, e=2, j=4)
        wup = [a["w_ffn_in"][l].rearrange("(k p) c -> p k c", p=P) for l in range(2)]
        wdn = [a["w_ffn_out"][l].rearrange("(k p) c -> p k c", p=P) for l in range(2)]

        def raw(b, cols=256):
            return WR[:, b, 0:KD * 256].rearrange("p (k c) -> p k c", c=256)

        def slot_free(sp, s):
            sp.wait_ge(w_split.sem, s + 1)

        def load_cols(sp, s, b, w, col):
            slot_free(sp, s)
            for j in range(2):
                sp.dma_start(raw(b)[:, 4 * j:4 * j + 4, :],
                             w[:, 4 * j:4 * j + 4, bass.ds(col, 256)]).then_inc(w_raw[b], 16)

        def load_up(sp, s, b, w, m):
            slot_free(sp, s)
            for j in range(2):
                sp.dma_start(raw(b)[:, :, j * P:(j + 1) * P],
                             w[:, :, bass.ds(m * P + j * FF, P)]).then_inc(w_raw[b], 16)

        def load_down(sp, s, b, w, m, half):
            slot_free(sp, s)
            dst = WR[:, b, 0:KH * P].rearrange("p (k c) -> p k c", c=P)
            for lo, hi in ((0, 5), (5, KH)):
                sp.dma_start(dst[:, lo:hi, :],
                             w[:, half * KH + lo:half * KH + hi, bass.ds(m * P, P)]).then_inc(w_raw[b], 16)

        def sp_cols(sp, name, w, trips):
            with sp.Fori(0, trips) as t:
                for j in range(2):
                    load_cols(sp, t * 2 + S0[name] + j, (S0[name] + j) % 2, w, t * 512 + j * 256)

        def sp_up(sp, name, w):
            with sp.Fori(0, KF // 2) as t:
                for j in range(2):
                    load_up(sp, t * 2 + S0[name] + j, (S0[name] + j) % 2, w, t * 2 + j)

        def sp_down(sp, name, w):
            with sp.Fori(0, KD) as t:
                for half in range(2):
                    load_down(sp, t * 2 + S0[name] + half, (S0[name] + half) % 2, w, t, half)

        def gemm_tile(pe, src, k0, nk, b, first_col, step, par, first, last, ready=None, between=None,
                      order=None):
            for at_k, kk in enumerate(order or range(nk)):
                if ready is not None:
                    pe.wait_ge(ready[0].sem, ready[1] + k0 + at_k + 1)
                c = kk * step + first_col
                wh, wl = WH[:, b, c:c + P], WL[:, b, c:c + P]
                for hf, n, w in ((0, 0, wh), (0, 1, wh), (1, 0, wh), (1, 1, wh), (0, 2, wl), (1, 2, wl)):
                    cols = slice(hf * HALF, (hf + 1) * HALF)
                    x = src[:, k0 + kk, 1 if n == 1 else 0, cols]
                    mm = pe.matmul(PG[:, par, hf, 0:HALF], w, x, start=(first and at_k == 0 and n == 0),
                                   stop=(last and at_k == nk - 1 and n == 2))
                if between is not None and at_k % 2 and at_k < nk - 1:
                    between()
            return mm

        def pe_wide(pe, name, src, trips, ready, tail=False, stat=None, order=None):
            def body(t, j0, slots, tiles_of, stat=None, ready=None):
                for j in range(j0, j0 + slots):
                    s, b = t * 2 + S0[name] + j, (S0[name] + j) % 2
                    pe.wait_ge(w_split.sem, s + 3)
                    for c in range(tiles_of):
                        u, par = t * 4 + U0[name] + 2 * j + c, (U0[name] + c) % 2
                        pe.wait_ge(tile_out.sem, u + 1)
                        tile_done.on(gemm_tile(pe, src, 0, KD, b, c * P, 256, par, True, True,
                                               ready if j == j0 and c == 0 else None, order=order))
                        if stat is not None and j == j0 and c == 0:
                            pe_stat(pe, stat)
            body(0, 0, 2, 2, stat, ready)
            with loop(pe, trips - 1, [(tile_done, 4)]) as t:
                body(t, 2, 2, 2)
            if tail:
                body(trips, 0, 1, 1)

        def pe_down(pe, name, ready):
            with loop(pe, KD // 2, [(tile_done, 2), (half_used, 2)]) as t:
                for c in range(2):
                    u, par = t * 2 + U0[name] + c, (U0[name] + c) % 2
                    pe.wait_ge(tile_out.sem, u + 1)
                    for half in range(2):
                        s, b = t * 4 + S0[name] + 2 * c + half, (S0[name] + half) % 2
                        pe.wait_ge(w_split.sem, s + 3)
                        mm = gemm_tile(pe, G, half * KH, KH, b, 0, P, par, half == 0, half == 1,
                                       ready if c == 0 else None)
                        (tile_done if half else half_used).on(mm)

        def pe_stat(pe, i):
            if i:
                pe.wait_ge(acc_ok.sem, 9 * i)
            else:
                pe.wait_ge(x_sum.sem, 15)
            for hf in range(2):
                mm = pe.matmul(M[:, hf, 0:HALF], ONES, ACC[:, hf * HALF:(hf + 1) * HALF], start=True, stop=True)
            st_done.on(mm)

        N_SMALL = 5

        def plain(act):
            act.sem_inc(passed, 1)

        def split_hi(act, b, raw_count, freed=None):
            act.wait_ge(w_raw[b], raw_count)
            if freed is not None:
                act.wait_ge(freed[0].sem, freed[1])
            plain(act)
            w_hi.on(act.activation(WH[:, b, :], WR[:, b, :], ACT.Copy))

        def split_next_wide(act, name, t, j):
            b = (S0[name] + j + 1) % 2
            count = raw_of(name, 2 * t + j + 1) if isinstance(t, int) else t * 32 + raw_of(name, j + 1)
            split_hi(act, b, count, (tile_done, t * 4 + U0[name] + 2 * j))

        def split_next_down(act, name, t, j):
            b = (S0[name] + j + 1) % 2
            n = 8 * (name == "down1")
            freed = (tile_done, t * 2 + U0[name] + j // 2) if j % 2 == 0 else \
                (half_used, t * 2 + n + j // 2 + 1)
            count = raw_of(name, 4 * t + j + 1) if isinstance(t, int) else t * 64 + raw_of(name, j + 1)
            split_hi(act, b, count, freed)

        def res_act(act, i, m, gcol, par, new_x):
            act.wait_ge(*new_x)

            def high():
                plain(act)
                dst = H[:, one(m), 0, :] if i < 4 else XG[:, one(m), :]
                a_hi.on(act.activation(dst, XT[:, one(m), :], ACT.Copy, scale=GAINS[:, bass.ds(m + gcol, 1)]))
            if i < 4:
                high()
            act.wait_ge(acc_ok.sem, m + 9 * (i - 1))
            plain(act)
            a_sq.on(act.activation(SQ[:, par, :], XT[:, one(m), :].rearrange("p a c -> p (a c)"), ACT.Square))
            if i == 4:
                high()

        def res_dve(dve, i, m, gcol, par, done):
            r = m + 8 * i
            if i < 4:
                dve.wait_ge(a_hi.sem, r + 1)
                dve.wait_ge(*done)
                h_ready.on(dve.scalar_tensor_tensor(
                    out=row2(H, m, 1), in0=row1(XT, m), scalar=GAINS[:, bass.ds(m + gcol, 1)],
                    in1=row2(H, m, 0).bitcast(F32), op0=ALU.mult, op1=ALU.subtract))
            dve.wait_ge(a_sq.sem, r - 8 + 1)
            dve.wait_ge(acc_ok.sem, acc_ok.now)
            acc_ok.on(dve.tensor_tensor(ACC[:, :], ACC[:, :], SQ[:, par, :], ALU.add))

        def row1(x, m):
            return x[:, one(m), :].rearrange("p a c -> p (a c)")

        def row2(x, m, part):
            return x[:, one(m), part, :].rearrange("p a c -> p (a c)")

        def norm_act(act, i):
            act.wait_ge(st_done.sem, i + 1)
            a_std.on(act.activation(halves(RSTD[:, :]), M[:, 0:2, 0:HALF], ACT.Sqrt, bias=EPSC, scale=1.0 / D))

        def norm_dve(dve, i):
            dve.wait_ge(a_std.sem, i + 1)
            rstd_ok.on(dve.reciprocal(RSTD[:, :], RSTD[:, :]))
            acc_ok.on(dve.memset(ACC[:, :], 0.0))
            dve.wait_ge(rstd_ok.sem, rstd_ok.now)

        def dve_project(dve, name, trips, tail=False, first=0):
            def drain(m, c):
                dve.wait_ge(tile_done.sem, m + U0[name] + 1)
                tile_out.on(dve.tensor_tensor(row(P0, m + first), sets((U0[name] + c) % 2), halves(RSTD[:, :]), ALU.mult))
            with loop(dve, trips, [(tile_out, 4)]) as t:
                for c in range(4):
                    drain(t * 4 + c, c)
            if tail:
                drain(4 * trips, 0)

        def dve_residual(dve, name, i, gcol, per):
            with loop(dve, KD // per, [(tile_out, per), (acc_ok, per)] + [(h_ready, per)] * (i < 4)) as t:
                for c in range(per):
                    m = t * per + c
                    dve.wait_ge(tile_done.sem, m + U0[name] + 1)
                    tile_out.on(dve.tensor_tensor(row(XT, m), row(XT, m), sets((U0[name] + c) % 2), ALU.add))
                    res_dve(dve, i, m, gcol, c % 2, (tile_out.sem, tile_out.now))

        def act_out(act, name, i, gcol):
            def body(t, c):
                if c % 2 == 0:
                    split_next_wide(act, name, t, c // 2)
                res_act(act, i, t * 4 + c, gcol, c % 2, (tile_out.sem, t * 4 + c + U0[name] + 3))
            if name == "out1":
                for m in range(KD):
                    body(m // 4, m % 4)
                return
            with loop(act, 2, [(w_hi, 2), (a_sq, 4), (a_hi, 4)]) as t:
                for c in range(4):
                    body(t, c)

        def act_down(act, name, i, gcol, final=False):
            def body(t, last=False):
                for c in range(2):
                    m = t * 2 + c
                    if not (final and last and c):
                        split_next_down(act, name, t, 2 * c + 1)
                    if not (last and c):
                        split_next_down(act, name, t, 2 * c + 2)
                    res_act(act, i, m, gcol, c, (tile_out.sem, m + U0[name] + 3))
            with loop(act, KD // 2 - 1, [(w_hi, 4), (a_sq, 2), (a_hi, 2)]) as t:
                body(t)
            body(KD // 2 - 1, True)

        def dve_up(dve, name, l):
            def body(t, j):
                m = t * 2 + j
                ua = m * 2 + U0[name]
                dve.wait_ge(tile_done.sem, ua + 1)
                tile_out.on(dve.tensor_tensor(halves(TA[:, j, :]), sets(U0[name] % 2), halves(RSTD[:, :]), ALU.mult))
                dve.wait_ge(tile_done.sem, ua + 2)
                tile_out.on(dve.tensor_tensor(halves(TB[:, :]), sets((U0[name] + 1) % 2), halves(RSTD[:, :]), ALU.mult))
                dve.wait_ge(a_silu.sem, m + KF * l + 1)
                dve.wait_ge(tile_out.sem, tile_out.now)
                t_gate.on(dve.tensor_tensor(TG[:, j, :], TA[:, j, :], TB[:, :], ALU.mult))
                dve.wait_ge(a_ghi.sem, m + KF * l + 1)
                dve.wait_ge(t_gate.sem, t_gate.now)
                g_ready.on(dve.tensor_tensor(row2(G, m, 1), TG[:, j, :], row2(G, m, 0).bitcast(F32), ALU.subtract))
            with loop(dve, KF // 2, [(tile_out, 4), (t_gate, 2), (g_ready, 2)]) as t:
                for j in range(2):
                    body(t, j)

        def act_up(act, name, l, i):
            def body(t, j, norm=False, down=None):
                m = t * 2 + j
                split_next_wide(act, name, t, j)
                if norm:
                    norm_act(act, i)
                if down is not None:
                    split_next_down(act, down, 0, 0)
                act.wait_ge(tile_out.sem, m * 2 + U0[name] + 3)
                plain(act)
                a_silu.on(act.activation(TA[:, j % 2, :], TA[:, j % 2, :], ACT.Silu))
                act.wait_ge(t_gate.sem, m + KF * l + 1)
                plain(act)
                a_ghi.on(act.activation(row2(G, m, 0), TG[:, j % 2, :], ACT.Copy))
            body(0, 0, True)
            body(0, 1)
            with loop(act, KF // 2 - 2, [(w_hi, 2), (a_silu, 2), (a_ghi, 2)]) as t:
                for j in range(2):
                    body(t, j + 2)
            body(KF // 2 - 1, 0)
            body(KF // 2 - 1, 1, down=f"down{l}")

        PAIRS = [(gp, i) for gp in range(2) for i in range(QT)]
        STEPS = [(gp, i, e, br) for gp, i in PAIRS for e in range(2) for br in range(2)]
        SETUP = [("rope", 0), ("gate", 0), ("rope", 1), ("gate", 1), ("rope", 2), ("page", 0), ("rope", 3), ("page", 1)]
        for _i in range(QT + 1):
            SETUP += [("tok", _i, _b) for _b in range(3)] + [("page", _i + 2)]
        SETUP += [("page", NS - 1), ("pe", 0)]
        SETUP_V = [("page", NS + _n) for _n in range(NS)] + [("pe", 1)]
        Q_OF = {x: n for n, x in enumerate(x for x in SETUP + SETUP_V if x[0] != "rope")}
        Q_CV = len(Q_OF)
        Q_ATT = Q_CV + 2
        q_pair, q_step, q = [], [], Q_ATT
        for _, i in PAIRS:
            q_pair.append(q)
            q += 1
            for _ in range(4):
                q_step.append(q)
                q += i + 1
        Q_SMP = q
        KV_TILE = (12, 16)

        def by_act(q):
            return Q_ATT <= q < Q_SMP or q % 2 == 1

        DRAINED = [[by_act(x) for x in range(q + 1)].count(by_act(q)) for q in range(Q_SMP + 2 * NS + 4)]

        def q_wait_drained(eng, q):
            eng.wait_ge((q_a if by_act(q) else q_v).sem, DRAINED[q])

        def q_bank(pe, q):
            if q >= 2:
                q_wait_drained(pe, q - 2)
            return M[:, q % 2, :]

        def drains(eng, mine, q, copies, after=()):
            if by_act(q) != mine:
                return
            eng.wait_ge(q_fill.sem, q + 1)
            for s, v in after:
                eng.wait_ge(s, v)
            for dst, src in copies:
                ins = eng.activation(dst, src, ACT.Copy) if mine else eng.tensor_copy(dst, src)
            (q_a if mine else q_v).on(ins)

        def drain_job(eng, mine, job):
            q = Q_OF[job]
            bank = M[:, q % 2, :]
            if job[0] == "gate":
                copies = [(SGT[:, :], bank[0:NS, 80:128]) if job[1] else
                          (GT[:, :, :], bank.rearrange("p (i c) -> p i c", i=QT)[:, :, 80:128])]
                drains(eng, mine, q, copies)
            elif job[0] == "tok":
                _, i, b = job
                rows = P if i < QT else NS
                copies = [(KVO[0:rows, b * 512:(b + 1) * 512], bank[0:rows])]
                if b and i < QT:
                    copies.append((VTK[:, i, b - 1, :], bank[:, 256:512]))
                drains(eng, mine, q, copies, [(d_kv, 32 * i)] if i else [])
            elif job[0] == "page":
                src = bank.rearrange("p (g s r) -> p g s r", g=2, r=16)
                n = job[1] % NS
                drains(eng, mine, q, [(CT[:, :, g * P + n * 16:g * P + n * 16 + 16], src[:, g].rearrange("p s r -> p r s"))
                                      for g in range(2)])
            else:
                drains(eng, mine, q, [(CT[:, :, NCOL - 2:NCOL], bank[:, 0:32].rearrange("p (h r) -> p r h", h=2))])

        def drain_cv(eng, mine):
            drains(eng, mine, Q_CV, [(CVK[e * NC:(e + 1) * NC, gp, e * HD:(e + 1) * HD],
                                      M[e * NC:(e + 1) * NC, Q_CV % 2, (2 * gp + e) * P + e * HD:(2 * gp + e) * P + (e + 1) * HD])
                                     for gp in range(2) for e in range(2)], [(at_g.sem, 4)])
            drains(eng, mine, Q_CV + 1, [(CVS[:, :, :].rearrange("c g d -> c (g d)"), M[:, (Q_CV + 1) % 2, 0:2 * P])])

        def sp_layer1(sp):
            with sp.Fori(0, 3) as t:
                for j in range(2):
                    load_cols(sp, t * 2 + S0["in1"] + j, (S0["in1"] + j) % 2, w1, t * 512 + D + j * 256)
            s = S0["in1"] + 6
            slot_free(sp, s)
            for j in range(2):
                sp.dma_start(raw(s % 2)[:, 4 * j:4 * j + 4, 0:P],
                             w1[:, 4 * j:4 * j + 4, 2480:2608]).then_inc(w_raw[s % 2], 16)
            sp.wait_ge(g_ready.sem, 8 + KF)
            sp.wait_ge(tile_done.sem, U0["in1"])
            sp.dma_start(CA[:, :], a["c_att"]).then_inc(d_ca, 16)
            sp.wait_ge(rstd_ok.sem, 3)
            sp.dma_start(SQ[:, 0, 0:P], a["c_causal"]).then_inc(d_ca, 16)
            sp.dma_start(PTAB[:, :], a["page_table"].rearrange("n g -> (n g)").rearrange("(o x) -> o x", o=1)
                         ).then_inc(d_pt, 16)
            for e in range(2):
                for kv in range(2):
                    sp.dma_start(PEK[:, kv, e, :], a["pe_cmp"][kv]).then_inc(d_pe, 16)
            sp.wait_ge(d_pt, 16)
            for x in range(NSTG):
                load_page(sp, x)
            for m in range(4):
                b = (S0["inq"] + m) % 2
                slot_free(sp, S0["inq"] + m)
                for jj in range(2):
                    for e in range(2):
                        sp.dma_start(raw(b)[:, :, jj * P + e * HD:jj * P + (e + 1) * HD],
                                     w1[:, :, bass.ds(m // 2 * 512 + 256 * e + P * (m % 2) + HD * jj, HD)]
                                     ).then_inc(w_raw[b], 16)
            for job in SETUP:
                if job[0] == "tok" and job[2] == 2:
                    i = job[1]
                    for b in range(3):
                        q_wait_drained(sp, Q_OF["tok", i, b])
                    n = P if i < QT else NS
                    kv = out[5][0, i * P:(i + 1) * P] if i < QT else out[6][:, 0]
                    win = out[7][0, i * P:(i + 1) * P] if i < QT else out[8][:, 0]
                    sp.dma_start(kv.rearrange("n a g d -> n (a g d)"), KVO[0:n, 0:1024]).then_inc(d_kv, 16)
                    sp.dma_start(win.rearrange("n a g d -> n (a g d)"), KVO[0:n, 1024:1536]).then_inc(d_kv, 16)
                elif job[0] == "page":
                    sp.wait_ge(q_fill.sem, Q_OF[job] + 1)
                    load_page(sp, job[1] + NSTG)
            load_out1(sp, 0)
            load_out1(sp, 1)
            sp.wait_ge(tile_done.sem, U0["out1"])
            for kk in range(2):
                for e in range(2):
                    r = slice(e * HD, (e + 1) * HD)
                    sp.dma_start(WBD[r, kk, :, r], a["w_cmp"][kk].rearrange("l d e -> d l e")).then_inc(d_wc[kk], 16)
            for x in range(NS, 2 * NS - NSTG):
                sp.wait_ge(q_fill.sem, Q_OF["page", x] + 1)
                load_page(sp, x + NSTG)
            sp.wait_ge(gt_ok.sem, 2)
            sp.dma_start(GS[:, :], SGT[:, :]).then_inc(d_gs, 16)
            sp.wait_ge(qs_ok.sem, 1)
            sp.dma_start(CS[:, :], a["c_smp"]).then_inc(d_cs, 16)

            def cache(br, n, v):
                dst, sem = (VALS if v else KEYS)[br][n], d_vals[br] if v else d_keys[br][n]
                if br:
                    sp.dma_start(dst[:, :, :], a["cache_win"][n, :, v].rearrange("(g p) h d -> p g (h d)", p=P)
                                 ).then_inc(sem, 16)
                    return
                for g in range(NPAGE):
                    page = sp.value_load(PTAB[0:1, n * NPAGE + g:n * NPAGE + g + 1], min_val=0, max_val=N_PHYS - 1)
                    sp.dma_start(dst[:, g, :], a["cache_kv"][bass.ds(page, 1), :, 2 + v, :, :].rearrange("a p g d -> p (a g d)")
                                 ).then_inc(sem, 16)
            sp.wait_ge(cs_done.sem, len(PAIRS))
            for n in range(4):
                cache(0, n, 0)
            sp.wait_ge(cmp_done.sem, 2)
            for n in range(4, 7):
                cache(0, n, 0)
            sp.wait_ge(pv_done.sem, Q_SMP - Q_ATT)
            cache(0, 7, 0)
            for n in range(NS):
                cache(1, n, 0)
            for n in range(NS):
                cache(0, n, 1)
            sp.wait_ge(ss_done.sem, 2)
            for n in range(NS):
                cache(1, n, 1)
            sp.wait_ge(d_kv, 32 * (QT + 1))

        def load_page(sp, x):
            kv, n = x // NS, x % NS
            for g in range(NPAGE):
                page = sp.value_load(PTAB[0:1, n * NPAGE + g:n * NPAGE + g + 1], min_val=0, max_val=N_PHYS - 1)
                sp.dma_start(PST[:, x % NSTG, g, :],
                             a["cache_kv"][bass.ds(page, 1), :, kv, :, :].rearrange("a p g d -> p (a g d)")
                             ).then_inc(d_page[x % NSTG], 16)

        def load_out1(sp, m):
            s = S0["out1"] + m
            slot_free(sp, s)
            for e in range(2):
                for g in range(2):
                    sp.dma_start(WR[e * HD:(e + 1) * HD, s % 2, g * 1024:(g + 1) * 1024].rearrange("d (j c) -> d j c", j=4),
                                 wo1[g, :, e, :, m * 256:(m + 1) * 256].rearrange("j d c -> d j c")
                                 ).then_inc(w_raw[s % 2], 16)

        def sp_cols_out1(sp):
            load_out1(sp, 2)
            load_out1(sp, 3)

        def pool_layer1(pool, split_lo):
            def clear(x):
                if at_g.n:
                    pool.wait_ge(at_g.sem, at_g.now)
                at_g.on(pool.memset(x, 0.0))
            pool.wait_ge(tile_done.sem, U0["in1"])
            clear(CT[:, :, NCOL:SEGS])
            pool.wait_ge(g_ready.sem, 8 + KF)
            clear(CKP[0:HD, :, 1, :])
            clear(CKP[HD:P, :, 0, :])
            clear(CVK[:, :, :])
            pool.wait_ge(tile_done.sem, U0["out1"])
            clear(WBD[0:HD, :, :, HD:P])
            clear(WBD[HD:P, :, :, 0:HD])
            clear(KP[0:HD, :, 1:NKV:2, :])
            clear(KP[HD:P, :, 0:NKV:2, :])
            pool.wait_ge(cmp_done.sem, 2)
            clear(QPD[:, :])
            clear(Q2[:, :, :, :])
            pool.wait_ge(at_g.sem, at_g.now)
            split_lo(S0["out1"], S0["out1"] % 2)
            pool.wait_ge(w_split.sem, 2 + S0["out1"] + 1)
            pool.wait_ge(s_done.sem, 4 * len(STEPS))
            pool.wait_ge(qs_ok.sem, 1)
            clear(PTP0[:, :])
            clear(PTP1[:, :])

        def rope_banks(r):
            return M[:, 2:4, 0:HALF] if r < 4 else sets(r % 2)

        def rope_pe(pe, r, m):
            if r == 4:
                pe.wait_ge(tile_out.sem, U0["out1"] + 2)
            if 1 <= r < 4:
                pe.wait_ge(rope_in.sem, r)
            elif r >= 6:
                pe.wait_ge(rope_in.sem, r - 1)
            for hf in range(2):
                mm = pe.matmul(rope_banks(r)[:, hf, :], ROT, P0[:, m, hf * HALF:(hf + 1) * HALF], start=True, stop=True)
            rope_p.on(mm)

        def rope_dve(dve, r, m, dst):
            dve.wait_ge(rope_p.sem, r + 1)
            rope_in.on(dve.tensor_tensor(halves(SQ[:, r % 2, :]), rope_banks(r), halves(SIN), ALU.mult))
            vec.on(dve.tensor_tensor(dst, P0[:, m, :], COS, ALU.mult))
            dve.wait_ge(rope_in.sem, rope_in.now)
            dve.wait_ge(vec.sem, vec.now)
            rope_ok.on(dve.tensor_tensor(dst, dst, SQ[:, r % 2, :], ALU.add))

        ROPE_K = (12, 13, 16, 17)

        def pe_job(pe, job):
            if job[0] == "rope":
                return rope_pe(pe, job[1], ROPE_K[job[1]])
            bank = q_bank(pe, Q_OF[job])
            if job[0] == "gate":
                if job[1]:
                    mm = pe.transpose(bank[0:NS, 0:P], P0[:, 20, SEQ:T], IDENT)
                else:
                    for i in range(QT):
                        mm = pe.transpose(bank[:, i * P:(i + 1) * P], P0[:, 20, i * P:(i + 1) * P], IDENT)
            elif job[0] == "tok":
                _, i, b = job
                rows, cols = (P, slice(i * P, (i + 1) * P)) if i < QT else (NS, slice(SEQ, T))
                if b:
                    pe.wait_ge(rope_ok.sem, 2 * b)
                for c in range(4):
                    mm = pe.transpose(bank[0:rows, c * P:(c + 1) * P], P0[:, 8 + 4 * b + c, cols], IDENT)
            elif job[0] == "page":
                x = job[1]
                pe.wait_ge(d_page[x % NSTG], 32 * (x // NSTG + 1))
                for gp in range(2):
                    for kt in range(NPAGE):
                        c = (2 * gp + kt) * P
                        mm = pe.transpose(bank[:, c:c + P], PST[:, x % NSTG, kt, gp * P:(gp + 1) * P], IDENT)
            else:
                pe.wait_ge(d_pe, 64)
                mm = pe.transpose(bank[:, 0:32], PEK[:, job[1], :, :].rearrange("l e d -> l (e d)"), IDENT[0:32, 0:32])
            q_fill.on(mm)

        def pe_inq(pe):
            jobs = iter(SETUP)

            def setup():
                job = next(jobs, None)
                if job is not None:
                    pe_job(pe, job)
            pe.wait_ge(d_ca, 32)
            pe.wait_ge(tile_out.sem, U0["inq"] + 2)
            for u in range(KD):
                n, b = U0["inq"] + u, (S0["inq"] + u // 2) % 2
                if u % 2 == 0:
                    pe.wait_ge(w_split.sem, S0["inq"] + u // 2 + 3)
                pe.wait_ge(tile_out.sem, n + 1)
                tile_done.on(gemm_tile(pe, H, 0, KD, b, u % 2 * P, 256, n % 2, True, True, between=setup))
                setup()
            assert next(jobs, None) is None

        def pe_attention(pe):
            def compress(kv, between):
                q_wait_drained(pe, Q_OF["pe", kv])
                q_wait_drained(pe, Q_OF["pe", kv] - 1)
                pe.wait_ge(ct_prompt.sem, kv + 1)
                pe.wait_ge(d_wc[kv], 32)
                pe.wait_ge(at_g.sem, 6)
                if kv:
                    pe.wait_ge(ck_ok.sem, 1)
                for l in range(32):
                    if l in between:
                        between[l]()
                    h = l // 16
                    mm = pe.matmul(M[:, 3, 0:NCOL], WBD[:, kv, l, :], CT[:, l % 16, h:h + NCOL],
                                   start=l == 0, stop=l == 31)
                cmp_done.on(mm)

            def cmp_scores(cu):
                gp, i = PAIRS[cu]
                if cu == 0:
                    pe.wait_ge(ckp_ok.sem, 1)
                    pe.wait_ge(rope_in.sem, 4 + KD)
                for j in range(4):
                    c = i % 2 * 256 + j * 2 * NC
                    mm = pe.matmul(PG[:, gp, i // 2, c:c + 2 * NC], P0[:, gp * 4 + j, i * P:(i + 1) * P],
                                   CKP[:, gp, :, :].rearrange("p e c -> p (e c)"), start=True, stop=True)
                cs_done.on(mm)

            def scores(hu):
                gp, i, e, br = STEPS[hu]
                n = (i + 1) * P
                if hu == 0:
                    pe.wait_ge(cs_out.sem, 2)
                    pe.wait_ge(rope_ok.sem, 4 + KD)
                    pe.wait_ge(kp_ok.sem, 1)
                    pe.wait_ge(at_g.sem, 8)
                for j in range(4):
                    if hu:
                        pe.wait_ge(exp_done.sem, 4 * (hu - 1) + j + 1)
                    bank = PG[:, j // 2, j % 2, :]
                    pe.matmul(bank[:, 0:n], QR[:, gp * 4 + j, i * P:(i + 1) * P], KP[:, br, 2 * gp + e, 0:n],
                              start=True, stop=False)
                    s_done.on(pe.matmul(bank[:, n - P:n], CBF[:, 0:P], CBF[:, P:2 * P], start=False, stop=True))

            for m in range(KD):
                rope_pe(pe, 4 + m, m)
            compress(0, {})
            for n, job in enumerate(SETUP_V):
                if n == 0:
                    pe.wait_ge(cmp_done.sem, 1)
                pe_job(pe, job)
                if n >= 1:
                    cmp_scores(n - 1)
            compress(1, {16: lambda: scores(0)})

            def banks(hu):
                gp, i, e, br = STEPS[hu]
                return [(q_pair[hu // 4], None)] * (hu % 4 == 0) + [(q_step[hu] + kt, kt) for kt in range(i + 1)]

            def turn(hu, q, kt):
                gp, i, e, br = STEPS[hu]
                bank = q_bank(pe, q)
                if kt is None:
                    pe.wait_ge(c_ready.sem, gp + 1)
                for j in range(4):
                    if kt is not None:
                        pe.wait_ge(p_ready.sem, 4 * hu + j + 1)
                    if kt is None:
                        mm = pe.transpose(bank[0:2 * NC, j * P:(j + 1) * P],
                                          TC[gp][:, i, 2 * j:2 * j + 2, :].rearrange("p e c -> p (e c)"), IDENT)
                    else:
                        mm = pe.transpose(bank[:, j * P:(j + 1) * P], PB[:, hu % 2, j, kt * P:(kt + 1) * P], IDENT)
                q_fill.on(mm)

            def pv(hu, q, kt):
                gp, i, e, br = STEPS[hu]
                q_wait_drained(pe, q)
                if kt is None:
                    pv_done.on(pe.matmul(M[:, 2 + hu // 4 % 2, :], CVK[:, gp, :], PT[0:2 * NC, (q - Q_ATT) % 4, :],
                                         start=True, stop=False))
                else:
                    r = slice(e * HD, (e + 1) * HD)
                    c = gp * P + e * HD
                    pv_done.on(pe.matmul(M[r, 2 + hu // 4 % 2, :], VTK[:, kt, br, c:c + HD], PT[:, (q - Q_ATT) % 4, :],
                                         start=False, stop=br == 1 and kt == i))

            bank = q_bank(pe, Q_CV)
            pe.wait_ge(ck_ok.sem, 2)
            for gp in range(2):
                c = 256 + gp * NC
                pe.transpose(bank[0:NC, 2 * gp * P:(2 * gp + 1) * P], CVT[:, c:c + NC], IDENT)
                mm = pe.transpose(bank[0:2 * NC, (2 * gp + 1) * P:(2 * gp + 2) * P], CVT[:, c - NC:c + NC], IDENT)
            q_fill.on(mm)
            bank = q_bank(pe, Q_CV + 1)
            for gp in range(2):
                mm = pe.transpose(bank[:, gp * P:(gp + 1) * P], CVT[:, gp * P:(gp + 1) * P], IDENT)
            q_fill.on(mm)
            for hu in range(len(STEPS)):
                bs = banks(hu)
                for q, kt in bs[:2]:
                    turn(hu, q, kt)
                if hu + 1 < len(STEPS):
                    scores(hu + 1)
                if hu % 4 == 0 and hu >= 8:
                    pe.wait_ge(o_out.sem, hu // 4 - 1)
                if hu == 0:
                    q_wait_drained(pe, Q_CV)
                for n, (q, kt) in enumerate(bs):
                    pv(hu, q, kt)
                    if n + 2 < len(bs):
                        turn(hu, *bs[n + 2])
            pe_samples(pe)

        Q_KEYS = [[Q_SMP + n for n in range(NS)], [Q_SMP + NS + 1 + n + (n >= 4) for n in range(NS)]]
        Q_P = (Q_SMP + NS, Q_SMP + NS + 5, Q_SMP + 2 * NS + 2)
        Q_OM = Q_SMP + 2 * NS + 3
        S_SMP = (PG[:, 0, 0, :], PG[:, 1, 0, :], PG[:, 1, 1, :])
        O_SMP = (PG[:, 0, 1, :], M[:, 2, :], M[:, 3, :])

        def pe_samples(pe):
            pe.wait_ge(qpd_ok.sem, 1)
            pe.wait_ge(exp_done.sem, 4 * len(STEPS))
            for gp in range(2):
                mm = pe.matmul(S_SMP[0][:, 0:P], Q2[:, 1, gp, :], CKT[:, gp * P:(gp + 1) * P], start=gp == 0, stop=gp == 1)
            ss_done.on(mm)

            def keys(br, before={}):
                S = S_SMP[1 + br]
                for n in range(NS + 1):
                    if n in before:
                        before[n]()
                    if n < NS:
                        bank = q_bank(pe, Q_KEYS[br][n])
                        pe.wait_ge(d_keys[br][n], (32, 16)[br])
                        for gp in range(2):
                            for kt in range(NPAGE):
                                c = (2 * gp + kt) * P
                                mm = pe.transpose(bank[:, c:c + P], KEYS[br][n][:, kt, gp * P:(gp + 1) * P], IDENT)
                        q_fill.on(mm)
                    if n:
                        q_wait_drained(pe, Q_KEYS[br][n - 1])
                        for gp in range(2):
                            c = (gp * NS + n - 1) * P
                            mm = pe.matmul(S[:, 0:256], QPD[:, c:c + P], KTS[:, (n - 1) % 2, gp, :],
                                           start=n == 1 and gp == 0, stop=n == NS and gp == 1)
                        kts_used.on(mm)
                for gp in range(2):
                    mm = pe.matmul(S[:, 256:264], Q2[:, 0, gp, :], KN[:, br, gp, :], start=gp == 0, stop=gp == 1)
                ss_done.on(mm)

            def turn_p(n):
                bank = q_bank(pe, Q_P[n])
                pe.wait_ge(sp_ok.sem, n + 1)
                if n == 0:
                    mm = pe.transpose(bank[:, 0:P], PS[:, 0, 0:P], IDENT)
                else:
                    for kt in range(2):
                        pe.transpose(bank[:, kt * P:(kt + 1) * P], PS[:, n, kt * P:(kt + 1) * P], IDENT)
                    mm = pe.transpose(bank[0:NS, 2 * P:3 * P], PS[:, n, 256:264], IDENT)
                q_fill.on(mm)

            def values_cmp():
                q_wait_drained(pe, Q_P[0])
                q_wait_drained(pe, Q_CV + 1)
                spv_done.on(pe.matmul(O_SMP[0][:, 0:256], PTN[:, 0, :], CVS[:, :, :].rearrange("c g d -> c (g d)"),
                                      start=True, stop=True))

            def values(n):
                q_wait_drained(pe, Q_P[n])
                pe.wait_ge(o_out.sem, len(PAIRS) - 2 + n)
                pe.wait_ge(d_vals[n - 1], (32, 16)[n - 1] * NS)
                O = O_SMP[n]
                for s in range(NS):
                    if n == 1 and s == 6:
                        turn_p(2)
                    for kt in range(2):
                        c = (kt * NS + s) * P
                        pe.matmul(O[:, 0:256], (PTP0, PTP1)[n - 1][:, c:c + P], VALS[n - 1][s][:, kt, :],
                                  start=s == 0 and kt == 0, stop=False)
                spv_done.on(pe.matmul(O[:, 0:256], PTN[0:NS, n, :], VN[n - 1], start=False, stop=True))

            keys(0)
            turn_p(0)
            keys(1, {2: values_cmp, 4: lambda: turn_p(1)})
            values(1)
            values(2)
            bank = q_bank(pe, Q_OM)
            pe.wait_ge(om_ok.sem, 1)
            q_fill.on(pe.transpose(bank[:, 0:P], OM[:, :, :].rearrange("p e d -> p (e d)"), IDENT))

        def split_heads(gp, e):
            r = slice(e * HD, (e + 1) * HD)
            return r, slice(gp * 4, gp * 4 + 4), (2 * gp + e) * 4

        def dve_inq(dve):
            dve.wait_ge(d_ca, 32)
            dve.tensor_copy(CBF[:, 0:P], IDENT)
            vec.on(dve.tensor_copy(CBF[:, P:2 * P], SQ[:, 0, 0:P]))
            dve.wait_ge(vec.sem, vec.now)
            dve.wait_ge(tile_out.sem, U0["inq"] + 2)
            prompt_ct(dve, 0)
            for n, job in enumerate(SETUP):
                if job[0] == "rope":
                    rope_dve(dve, job[1], ROPE_K[job[1]], P0[:, ROPE_K[job[1]], :])
                else:
                    drain_job(dve, 0, job)
                if n % 4 == 3:
                    project(dve, "inq", n // 4)
                if n == 7:
                    dve.wait_ge(rope_ok.sem, 4)
                    for br in range(2):
                        for gp in range(2):
                            kn = dve.tensor_copy(KN[:, br, gp, :], P0[:, KV_TILE[br] + gp, SEQ:T])
                    vec.on(kn)
            project(dve, "inq", KD - 1)

        def project(dve, name, m):
            u = U0[name] + m
            dve.wait_ge(tile_done.sem, u + 1)
            tile_out.on(dve.tensor_tensor(row(P0, m), sets(u % 2), halves(RSTD[:, :]), ALU.mult))

        def prompt_ct(dve, kv):
            for gp in range(2):
                c = dve.tensor_copy(CT[:, :, 256 + gp * NC:256 + (gp + 1) * NC],
                                    P0[:, 8 + 2 * kv + gp, 0:SEQ].rearrange("p (s r) -> p r s", r=16))
            ct_prompt.on(c)

        def dve_attention(dve):
            NB, SUM, F = (ST8[:, 8 * n:8 * n + 8] for n in (1, 2, 3))
            CM = [ST8[:, 32 * n:32 * n + 32].rearrange("p (i x) -> p i x", i=QT) for n in (1, 2)]

            def chain(ins):
                vec.on(ins)
                dve.wait_ge(vec.sem, vec.now)

            def drain_ck(kv):
                dve.wait_ge(cmp_done.sem, kv + 1)
                chain(dve.tensor_copy(F[:, 0:1], M[:, 3, NCOL - 2:NCOL - 1]))
                ck_ok.on(dve.tensor_scalar((CKT, CVT)[kv][:, :], M[:, 3, 0:NCOL], F[:, 0:1], None, ALU.add))
                dve.wait_ge(ck_ok.sem, ck_ok.now)

            dve.wait_ge(tile_out.sem, tile_out.now)
            for m in range(KD):
                rope_dve(dve, 4 + m, m, QR[:, m, :])
            dve.wait_ge(rope_ok.sem, 4 + KD)
            dve.tensor_copy(QU[:, :, :], P0[:, 0:KD, SEQ:T])
            qs_ok.on(dve.tensor_copy(QS[:, :, :], QR[:, :, SEQ:T]))
            for gp in range(2):
                for e in range(2):
                    r = slice(e * HD, (e + 1) * HD)
                    for br in range(2):
                        c = dve.tensor_scalar(KP[r, br, 2 * gp + e, :], P0[r, KV_TILE[br] + gp, 0:SEQ], SCALE, None, ALU.mult)
            kp_ok.on(c)
            drain_ck(0)
            for gp in range(2):
                for e in range(2):
                    r = slice(e * HD, (e + 1) * HD)
                    c = dve.tensor_copy(CKP[r, gp, e, :], CKT[r, 256 + gp * NC:256 + (gp + 1) * NC])
            ckp_ok.on(c)
            prompt_ct(dve, 1)
            for job in SETUP_V:
                drain_job(dve, 0, job)

            def bias01(base):
                return CA[:, base:base + QT * NC].rearrange("p (i c) -> p i c", i=QT)

            dve.wait_ge(qs_ok.sem, 1)
            for gp in range(2):
                dve.wait_ge(cs_done.sem, 4 * gp + 4)
                for i in range(QT):
                    c = dve.scalar_tensor_tensor(
                        out=TC[gp][:, i], in0=PG[:, gp, i // 2, i % 2 * 256:i % 2 * 256 + 256].rearrange("p (x c) -> p x c", c=NC),
                        scalar=SCALE, in1=bias01(C_CB)[:, i].unsqueeze(1).to_broadcast([P, 8, NC]),
                        op0=ALU.mult, op1=ALU.add)
                cs_out.on(c)
            dve.wait_ge(cs_out.sem, 2)
            for gp in range(2):
                vec.on(dve.tensor_reduce(CM[gp], TC[gp][:, :, :, :], AX.X, ALU.max))
            dve.wait_ge(vec.sem, vec.now)
            for gp in range(2):
                c_max.on(dve.tensor_tensor(TC[gp][:, :, :, :], TC[gp][:, :, :, :],
                                           CM[gp].unsqueeze(3).to_broadcast([P, QT, 8, NC]), ALU.subtract))
            for gp in range(2):
                dve.wait_ge(c_exp.sem, gp + 1)
                for i in range(QT):
                    c = dve.tensor_tensor(TC[gp][:, i], TC[gp][:, i],
                                          bias01(C_CV)[:, i].unsqueeze(1).to_broadcast([P, 8, NC]), ALU.mult)
                vec.on(c)
            dve.wait_ge(vec.sem, vec.now)
            for gp in range(2):
                vec.on(dve.tensor_reduce(CM[gp], TC[gp][:, :, :, :], AX.X, ALU.add))
            CM2 = ST8[:, 32:96]
            dve.wait_ge(vec.sem, vec.now)
            chain(dve.tensor_scalar(CM2, CM2, 1e-30, None, ALU.max))
            chain(dve.reciprocal(CM2, CM2))
            dve.wait_ge(gt_ok.sem, 1)
            for gp in range(2):
                g = GT[:, :, :].rearrange("p i (g j b) -> p i g j b", g=NKV, b=3)[:, :, 2 * gp:2 * gp + 2, :, 0]
                for i in range(QT):
                    cm = CM[gp][:, i, :].rearrange("p (j e) -> p e j", e=2)
                    c = dve.tensor_tensor(cm, cm, g[:, i], ALU.mult)
            chain(c)
            for gp in range(2):
                c_ready.on(dve.tensor_tensor(TC[gp][:, :, :, :], TC[gp][:, :, :, :],
                                             CM[gp].unsqueeze(3).to_broadcast([P, QT, 8, NC]), ALU.mult))

            def row_max(hu):
                gp, i, e, br = STEPS[hu]
                o = 4 * (hu % 2)
                for j in range(4):
                    dve.wait_ge(s_done.sem, 4 * hu + j + 1)
                    nb_ok.on(dve.tensor_reduce(NB[:, o + j:o + j + 1], PG[:, j // 2, j % 2, 0:(i + 1) * P], AX.X, ALU.max,
                                               negate=True))

            def scale_probs(hu):
                gp, i, e, br = STEPS[hu]
                o = 4 * (hu % 2)
                for n in range(5):
                    if n < 4:
                        dve.wait_ge(exp_done.sem, 4 * hu + n + 1)
                        vec.on(dve.reciprocal(F[:, o + n:o + n + 1], SUM[:, o + n:o + n + 1]))
                    if n:
                        j = n - 1
                        pj = PB[:, hu % 2, j, 0:(i + 1) * P]
                        g = 3 * (4 * (2 * gp + e) + j) + 1 + br
                        dve.wait_ge(vec.sem, vec.now - (n < 4))
                        p_ready.on(dve.tensor_scalar(pj, pj, F[:, o + j:o + j + 1], GT[:, i, g:g + 1], ALU.mult, ALU.mult))

            def o_low(cu):
                gp, i = PAIRS[cu]
                dve.wait_ge(o_hi.sem, cu + 1)
                o_out.on(dve.tensor_tensor(
                    G[:, gp * 4:gp * 4 + 4, 1, i * P:(i + 1) * P], M[:, 2 + cu % 2, :].rearrange("p (j q) -> p j q", j=4),
                    G[:, gp * 4:gp * 4 + 4, 0, i * P:(i + 1) * P].bitcast(F32), ALU.subtract))

            def pad_queries(x):
                gp, e = x // 2, x % 2
                r, tiles, row0 = split_heads(gp, e)
                dve.wait_ge(at_g.sem, 10)
                for rot, src in ((0, QS[r, tiles, :]), (1, QU[r, tiles, :])):
                    dve.tensor_copy(Q2[r, rot, gp, :].rearrange("p (n h) -> p h n", h=16)[:, row0:row0 + 4, :], src)
                for view, n0, n1 in own_rows(QPD[r, gp * NS * P:(gp + 1) * NS * P]):
                    c = dve.tensor_copy(view[:, :, row0:row0 + 4], QS[r, tiles, n0:n1].rearrange("p t n -> p n t"))
                if x == 3:
                    qpd_ok.on(c)

            row_max(0)
            drain_ck(1)
            drain_cv(dve, 0)
            scale_probs(0)
            for hu in range(len(STEPS)):
                if hu % 4 == 0 and hu:
                    o_low(hu // 4 - 1)
                if hu + 1 < len(STEPS):
                    row_max(hu + 1)
                    if 4 <= hu < 8:
                        pad_queries(hu - 4)
                    scale_probs(hu + 1)
            o_low(len(PAIRS) - 1)
            dve_samples(dve, chain)

        def turned(hu):
            return [(q_pair[hu // 4], 2 * NC)] * (hu % 4 == 0) + [(q_step[hu] + kt, P) for kt in range(STEPS[hu][1] + 1)]

        def drain_pt(act, q, rows):
            x = q - Q_ATT
            drains(act, 1, q, [(PT[0:rows, x % 4, :], M[0:rows, q % 2, :])], [(pv_done.sem, x - 3)] if x >= 4 else [])

        def own_rows(x):
            w = P + 16
            return [(x[:, 0:7 * w].rearrange("p (n c) -> p n c", c=w)[:, :, 0:16], 0, 7),
                    (x[:, 7 * w:7 * w + 16].rearrange("p (n c) -> p n c", n=1), 7, 8)]

        def smp_stats(n):
            return [ST8[:, 32 + 8 * n + k:33 + 8 * n + k] for k in range(4)]

        def dve_samples(dve, chain):
            def soft_in(n):
                MXS, NBS, _, _ = smp_stats(n)
                w, base = (P, 264) if n == 0 else (264, 0)
                dve.wait_ge(ss_done.sem, n + 1)
                dve.wait_ge(d_cs, 16)
                chain(dve.scalar_tensor_tensor(out=SCS[:, n, 0:w], in0=S_SMP[n][:, 0:w], scalar=SCALE,
                                               in1=CS[:, base:base + w], op0=ALU.mult, op1=ALU.add))
                chain(dve.tensor_reduce(MXS, SCS[:, n, 0:w], AX.X, ALU.max))
                snb_ok.on(dve.tensor_scalar(NBS, MXS, -1.0, None, ALU.mult))

            def gate(n):
                _, _, SMS, FS = smp_stats(n)
                dve.wait_ge(sp_ok.sem, n + 1)
                dve.wait_ge(d_gs, 16)
                chain(dve.reciprocal(FS, SMS))
                chain(dve.tensor_tensor(FS, FS, GS[:, n:n + 1], ALU.mult))

            def add_branch(n):
                FS = smp_stats(n)[3]
                dve.wait_ge(spv_done.sem, n + 1)
                if n == 0:
                    oa_ok.on(dve.tensor_scalar(OA[:, :], O_SMP[0][:, 0:256], FS, None, ALU.mult))
                else:
                    oa_ok.on(dve.scalar_tensor_tensor(out=OA[:, :], in0=O_SMP[n][:, 0:256], scalar=FS, in1=OA[:, :],
                                                      op0=ALU.mult, op1=ALU.add))
                dve.wait_ge(oa_ok.sem, oa_ok.now)

            soft_in(0)
            for n in range(2):
                drain_kts(dve, 0, 0, n)
            gate(0)
            for n in range(2, NS):
                drain_kts(dve, 0, 0, n)
            soft_in(1)
            drain_p(dve, 0, 0)
            gate(1)
            for n in range(4):
                drain_kts(dve, 0, 1, n)
            drain_p(dve, 0, 1)
            add_branch(0)
            for n in range(4, NS):
                drain_kts(dve, 0, 1, n)
            soft_in(2)
            gate(2)
            drain_p(dve, 0, 2)
            add_branch(1)
            add_branch(2)
            for e in range(2):
                chain(dve.tensor_scalar(OM[:, e, :], OA[:, e * HD:(e + 1) * HD], CS[:, 264 + P + e:264 + P + e + 1],
                                        None, ALU.mult))
                c = dve.scalar_tensor_tensor(
                    out=OM[:, e, :], in0=OA[:, (2 + e) * HD:(3 + e) * HD], scalar=CS[:, 264 + P + 2 + e:264 + P + 3 + e],
                    in1=OM[:, e, :], op0=ALU.mult, op1=ALU.add)
            om_ok.on(c)
            drain_os(dve, 0)
            dve.wait_ge(os_hi.sem, 1)
            q_wait_drained(dve, Q_OM)
            for m in range(KD):
                g_ready.on(dve.tensor_tensor(G[:, m, 1, SEQ:T], OS[:, m, :], G[:, m, 0, SEQ:T].bitcast(F32), ALU.subtract))

        def drain_kts(eng, mine, br, n):
            x = NS * br + n
            q = Q_KEYS[br][n]
            drains(eng, mine, q, [(KTS[:, n % 2, :, :].rearrange("p g k -> p (g k)"), M[:, q % 2, :])],
                   [(kts_used.sem, x - 1)] if x >= 2 else [])

        def drain_p(eng, mine, n):
            q = Q_P[n]
            src = M[:, q % 2, :]
            if n == 0:
                drains(eng, mine, q, [(PTN[:, 0, :], src[:, 0:P])])
                return
            copies = [(view, src[:, kt * P + n0 * 16:kt * P + n1 * 16].rearrange("p (n h) -> p n h", h=16))
                      for kt in range(2)
                      for view, n0, n1 in own_rows((PTP0, PTP1)[n - 1][:, kt * NS * P:(kt + 1) * NS * P])]
            copies.append((PTN[0:NS, n, :], src[0:NS, 2 * P:3 * P]))
            drains(eng, mine, q, copies, [(at_g.sem, 10 + n)])

        def drain_os(eng, mine):
            q = Q_OM
            src = M[:, q % 2, 0:P].rearrange("p (n h) -> p h n", h=16)
            drains(eng, mine, q, [(OS[r, tiles, :], src[r, row0:row0 + 4, :])
                                  for gp in range(2) for e in range(2) for r, tiles, row0 in (split_heads(gp, e),)])

        def act_inq(act):
            act.wait_ge(g_ready.sem, 8 + KF)
            for n, job in enumerate(SETUP):
                if n % 8 == 0 and n < 24:
                    split_hi(act, (S0["inq"] + n // 8 + 1) % 2, raw_of("inq", n // 8 + 1),
                             (tile_done, U0["inq"] + n // 4))
                if job[0] != "rope":
                    drain_job(act, 1, job)

        def act_attention(act):
            act.wait_ge(q_a.sem, Q_OF["gate", 1] // 2 + 1)
            act.wait_ge(q_v.sem, Q_OF["gate", 0] // 2 + 1)
            gt_ok.on(act.activation(GT[:, :, :], GT[:, :, :], ACT.Sigmoid))
            gt_ok.on(act.activation(SGT[:, :], SGT[:, :], ACT.Sigmoid))
            for job in SETUP_V:
                if job == SETUP_V[0]:
                    act.wait_ge(cmp_done.sem, 1)
                drain_job(act, 1, job)
            for gp in range(2):
                act.wait_ge(c_max.sem, gp + 1)
                c_exp.on(act.activation(TC[gp][:, :, :, :], TC[gp][:, :, :, :], ACT.Exp))
            NB, SUM, F = (ST8[:, 8 * n:8 * n + 8] for n in (1, 2, 3))

            def exps(hu):
                gp, i, e, br = STEPS[hu]
                o, n = 4 * (hu % 2), (i + 1) * P
                if hu >= 2:
                    act.wait_ge(q_fill.sem, q_step[hu - 2] + STEPS[hu - 2][1] + 1)
                for j in range(4):
                    act.wait_ge(nb_ok.sem, 4 * hu + j + 1)
                    exp_done.on(act.activation(PB[:, hu % 2, j, 0:n], PG[:, j // 2, j % 2, 0:n], ACT.Exp,
                                               bias=NB[:, o + j:o + j + 1], scale=1.0,
                                               accum_out=SUM[:, o + j:o + j + 1]))

            def o_high(cu):
                gp, i = PAIRS[cu]
                act.wait_ge(pv_done.sem, q_step[4 * cu + 3] + i + 1 - Q_ATT)
                o_hi.on(act.activation(G[:, gp * 4:gp * 4 + 4, 0, i * P:(i + 1) * P],
                                       M[:, 2 + cu % 2, :].rearrange("p (j q) -> p j q", j=4), ACT.Copy))

            exps(0)
            drain_cv(act, 1)
            for hu in range(len(STEPS)):
                bs = turned(hu)
                for q, rows in bs[:2]:
                    drain_pt(act, q, rows)
                if hu % 4 == 0 and hu:
                    o_high(hu // 4 - 1)
                if hu + 1 < len(STEPS):
                    exps(hu + 1)
                for q, rows in bs[2:]:
                    drain_pt(act, q, rows)
                if hu == 1:
                    split_hi(act, S0["out1"] % 2, raw_of("out1", 0), (cmp_done, 2))
            o_high(len(PAIRS) - 1)
            def exp_s(n):
                _, NBS, SMS, _ = smp_stats(n)
                w = P if n == 0 else 264
                act.wait_ge(snb_ok.sem, n + 1)
                sp_ok.on(act.activation(PS[:, n, 0:w], SCS[:, n, 0:w], ACT.Exp, bias=NBS, scale=1.0, accum_out=SMS))
            for n in range(2):
                drain_kts(act, 1, 0, n)
            exp_s(0)
            for n in range(2, NS):
                drain_kts(act, 1, 0, n)
            exp_s(1)
            drain_p(act, 1, 0)
            for n in range(4):
                drain_kts(act, 1, 1, n)
            drain_p(act, 1, 1)
            for n in range(4, NS):
                drain_kts(act, 1, 1, n)
            exp_s(2)
            drain_p(act, 1, 2)
            drain_os(act, 1)
            q_wait_drained(act, Q_OM)
            os_hi.on(act.activation(G[:, 0:KD, 0, SEQ:T], OS[:, :, :], ACT.Copy))

        FO = (2, 3, 0, 1)
        MIX_BANK = (2, 3, 0, 1)
        Y_TILE = [FT + f for f in FO] + list(FO)
        G0 = {"out0": 0, "down0": 8, "out1": 8 + KF, "down1": 16 + KF}

        FINAL = [(0, 0, M[:, 0]), (1, 0, M[:, 1]), (2, 0, M[:, 2]), (3, 0, PG[:, 0, 0]), (0, 1, PG[:, 0, 1]),
                 (1, 1, PG[:, 1, 0]), (2, 1, PG[:, 1, 1]), (3, 1, M[:, 0]), (QT, 0, M[:, 1]), (QT, 1, M[:, 2])]

        def fin_wait(eng, k):
            eng.wait_ge((fin_a if k % 2 else fin_v).sem, k // 2 + 1)

        def pe_final(pe):
            def turn(k):
                i, hf, bank = FINAL[k]
                rows, cols = (P, slice(i * P, (i + 1) * P)) if i < QT else (NS, slice(SEQ, T))
                if k >= 7:
                    fin_wait(pe, k - 7)
                if k == 3:
                    pe.wait_ge(tile_out.sem, U0["down1"] + KD + 2)
                pe.wait_ge(a_hi.sem, 8 * 4 + (8 if hf else 4))
                for kk in range(4):
                    mm = pe.transpose(bank[0:rows, kk * P:(kk + 1) * P], XG[:, 4 * hf + kk, cols], IDENT)
                fin_p.on(mm)
            for k in range(3):
                turn(k)
            pe.wait_ge(acc_ok.sem, 9 * 4)
            for i in range(QT + 1):
                rows, cols = (P, slice(i * P, (i + 1) * P)) if i < QT else (NS, slice(SEQ, T))
                mm = pe.matmul(M[0:rows, 3, i:i + 1], ACC[:, cols], ONES[:, 0:1], start=True, stop=True)
            st_done.on(mm)
            for k in range(3, 10):
                turn(k)

        def fin_out(k):
            i, hf, bank = FINAL[k]
            rows = P if i < QT else NS
            dst = YO[:, i, hf * 512:(hf + 1) * 512] if i < QT else YS[:, hf * 512:(hf + 1) * 512]
            return dst, bank[0:rows, :], RSTD[0:rows, i:i + 1]

        def act_final(act):
            act.wait_ge(st_done.sem, 5)
            act.activation(RSTD[:, 0:QT], M[:, 3, 0:QT], ACT.Sqrt, bias=EPSC, scale=1.0 / D)
            a_std.on(act.activation(RSTD[0:NS, QT:QT + 1], M[0:NS, 3, QT:QT + 1], ACT.Sqrt, bias=EPSC[0:NS, :], scale=1.0 / D))
            act.wait_ge(rstd_ok.sem, 6)
            for k in range(1, 10, 2):
                dst, src, r = fin_out(k)
                act.wait_ge(fin_p.sem, k + 1)
                fin_a.on(act.activation(dst, src, ACT.Copy, scale=r))

        def dve_final(dve):
            dve.wait_ge(a_std.sem, 5)
            rstd_ok.on(dve.reciprocal(RSTD[:, 0:QT], RSTD[:, 0:QT]))
            rstd_ok.on(dve.reciprocal(RSTD[0:NS, QT:QT + 1], RSTD[0:NS, QT:QT + 1]))
            dve.wait_ge(rstd_ok.sem, 6)
            for k in range(0, 10, 2):
                dst, src, r = fin_out(k)
                dve.wait_ge(fin_p.sem, k + 1)
                fin_v.on(dve.tensor_scalar(dst, src, r, None, ALU.mult))

        block = ctx.enter_context(nc.Block())

        @block.sync
        def _(sp):
            sp.dma_start(BASE[:, :], a["c_base"]).then_inc(d_base, 16)
            def load_in0(s):
                load_cols(sp, s, s % 2, w0, (9 - s) * 256)

            for i in range(QT):
                sp.dma_start(XL[:, i, :], a["x_prompt"][0, i * P:(i + 1) * P, :]).then_inc(d_x[i], 16)
                if i == 1:
                    load_in0(0)
            sp.dma_start(XS[:, :], a["x_sample"][:, 0, :]).then_inc(d_xs, 16)
            for r, x in ((0, a["norm_mix"].rearrange("l (k p) -> (l k) p", p=P)),
                         (16, a["norm_ffn"].rearrange("l (k p) -> (l k) p", p=P)),
                         (32, a["norm_final"].rearrange("(k p) -> k p", p=P)),
                         (40, a["conv_w"].rearrange("j (k p) -> (j k) p", p=P)),
                         (52, a["norm_v"].rearrange("(k p) -> k p", p=P))):
                sp.dma_start(GROW[r:r + x.shape[0], :], x).then_inc(d_gain, 16)
            load_in0(1)
            sp.dma_start(TRIL[:, :], a["c_tril"]).then_inc(d_small, 16)
            sp.dma_start(SCV[:, :], a["state_conv"].rearrange("n j c -> (n j) c")).then_inc(d_small, 16)
            sp.dma_start(WSP[:, :, :], a["w_spatial"].rearrange("h t s -> t h s")).then_inc(d_small, 16)
            sp.dma_start(BSP[:, :, :].rearrange("p h t -> p (h t)"),
                         a["b_spatial"].rearrange("h t -> (h t)").partition_broadcast(P)
                         ).then_inc(d_small, 16)
            sp.dma_start(W00[:, :, :], a["w_spatial"][:, 0, 0:8].partition_broadcast(P)).then_inc(d_small, 16)
            for s in range(2, 10):
                load_in0(s)
            sp_cols(sp, "out0", wo0, 2)
            sp.dma_start(out[3][:, 0, :], a["state_conv"][:, 1, :]).then_inc(d_out, 16)
            sp.wait_ge(cv_ok.sem, 1)
            sp.dma_start(out[4][:, 0, :], CV[:, :]).then_inc(d_out, 16)
            sp.wait_ge(zo_ok.sem, 1)
            sp.dma_start(out[2][0], ZO[0:2, :]).then_inc(d_out, 16)
            sp.dma_start(out[3][:, 1, :], ZO[2:10, :]).then_inc(d_out, 16)
            outs[0] += 4
            sp_up(sp, "up0", wup[0])
            sp_down(sp, "down0", wdn[0])
            sp_layer1(sp)
            sp_cols_out1(sp)
            sp_up(sp, "up1", wup[1])
            sp_down(sp, "down1", wdn[1])
            for k, (i, hf, _) in enumerate(FINAL):
                fin_wait(sp, k)
                if i < QT:
                    sp.dma_start(out[0][0, i * P:(i + 1) * P, hf * 512:(hf + 1) * 512],
                                 YO[:, i, hf * 512:(hf + 1) * 512]).then_inc(d_out, 16)
                else:
                    sp.dma_start(out[1][:, 0, hf * 512:(hf + 1) * 512], YS[:, hf * 512:(hf + 1) * 512]).then_inc(d_out, 16)
                outs[0] += 1
            sp.wait_ge(d_out, 16 * outs[0])

        @block.gpsimd
        def _(pool):
            pool.sem_inc(w_split.sem, 2)

            def x_sums(need, c0, c1):
                pool.wait_ge(x_sq.sem, need)
                for k in (4, 2, 1):
                    dst = SQX[:, 0:k, c0:c1] if k > 1 else ACC[:, c0:c1].unsqueeze(1)
                    if k < 4:
                        pool.wait_ge(x_sum.sem, x_sum.now)
                    x_sum.on(pool.tensor_tensor(dst, SQX[:, 0:k, c0:c1], SQX[:, k:2 * k, c0:c1], ALU.add))
            for i in range(2):
                x_sums(2 * i + 2, i * P, (i + 1) * P)
            def split_lo(s, b):
                pool.wait_ge(w_hi.sem, s + 1)
                w_split.on(pool.tensor_tensor(WL[:, b, :], WR[:, b, :], WH[:, b, :].bitcast(F32), ALU.subtract))
            def split_slots(s0, n):
                with pool.Fori(0, n // 2) as t:
                    for b in range(2):
                        split_lo(t * 2 + s0 + b, (s0 + b) % 2)
                if n % 2:
                    split_lo(s0 + n - 1, (s0 + n - 1) % 2)
            split_lo(0, 0)
            x_sums(6, 2 * P, 3 * P)
            x_sums(8, 3 * P, SEQ)
            x_sums(9, SEQ, T)
            split_slots(1, S0["out1"] - 1)
            pool_layer1(pool, split_lo)
            pool.wait_ge(at_g.sem, at_g.now)
            split_slots(S0["out1"] + 1, _s - S0["out1"] - 1)

        @block.tensor
        def _(pe):
            fills = [0]

            def fill_start():
                if fills[0] >= 4:
                    pe.wait_ge(t_drain.sem, fills[0] - 3)
                return M[:, fills[0] % 4, :]

            def fill_end(mm):
                t_fill.on(mm)
                fills[0] += 1

            pe.wait_ge(d_base, 16)
            for i in range(QT):
                pe.wait_ge(d_x[i], 16)
                for hf in range(2):
                    bank = fill_start()
                    for kk in range(4):
                        mm = pe.transpose(bank[:, kk * P:(kk + 1) * P], XL[:, i, (4 * hf + kk) * P:(4 * hf + kk + 1) * P], IDENT)
                    fill_end(mm)
            pe.wait_ge(d_xs, 16)
            bank = fill_start()
            for kk in range(KD):
                mm = pe.transpose(bank[:, 8 * kk:8 * kk + 8], XS[:, kk * P:(kk + 1) * P], IDENT[0:NS, 0:NS])
            fill_end(mm)
            pe.wait_ge(d_gain, 16 * 5)
            bank = fill_start()
            fill_end(pe.transpose(bank[:, 0:N_GAIN], GROW[:, :], IDENT[0:N_GAIN, 0:N_GAIN]))

            def v_sums():
                pe.wait_ge(accv_ok.sem, FT)
                for hf in range(2):
                    mm = pe.matmul(M[:, hf, 0:HALF], ONES, ACV[:, hf * HALF:(hf + 1) * HALF], start=True, stop=True)
                stv_done.on(mm)

            def turn_small():
                pe.wait_ge(d_small, 16 * N_SMALL)
                bank = fill_start()
                for f in range(FT):
                    mm = pe.transpose(bank[:, 16 * f:16 * f + 16], SCV[:, f * P:(f + 1) * P], IDENT[0:16, 0:16])
                fill_end(mm)
                bank = fill_start()
                for h in range(4):
                    mm = pe.transpose(bank[:, h * P:(h + 1) * P], WSP[:, h, :], IDENT)
                fill_end(mm)

            def turn_v(x):
                pe.wait_ge(vn_ok.sem, x + 1)
                if x >= 2:
                    pe.wait_ge(vt_drain.sem, x - 1)
                f, v = FO[x], P0[:, 16 + FO[x], :]
                pe.transpose(M[0:NS, 0, f * P:(f + 1) * P], v[:, SEQ:T], IDENT)
                for c in range(QT):
                    mm = pe.transpose(M[:, 2 + x % 2, c * P:(c + 1) * P], v[:, c * P:(c + 1) * P], IDENT)
                vt_fill.on(mm)

            def mix(x):
                pe.wait_ge(vt_drain.sem, FT)
                if x == 2:
                    pe.wait_ge(cv_ok.sem, 1)
                f = FO[x]
                for c in range(QT):
                    mm = pe.matmul(M[:, MIX_BANK[x], c * P:(c + 1) * P], P0[:, 16 + f, c * P:(c + 1) * P], WT[:, f, :],
                                   start=True, stop=True)
                mixed.on(mm)

            def conv_states():
                pe.wait_ge(mix_out.sem, FT)
                pe.wait_ge(z_ok.sem, FT)
                for f in range(FT):
                    mm = pe.transpose(M[0:10, 1, f * P:(f + 1) * P], P0[:, 8 + f, SEQ - 2:T], IDENT)
                zo_fill.on(mm)

            extra = {0: [None, None, None, lambda: pe_stat(pe, 0)], 3: [turn_small], 7: [None, v_sums],
                     8: [None, lambda: turn_v(0), lambda: turn_v(1)], 9: [lambda: turn_v(2), lambda: turn_v(3)],
                     10: [None, lambda: mix(0), lambda: mix(1)], 11: [lambda: mix(2), lambda: mix(3)],
                     17: [conv_states]}
            for u in range(20):
                todo = iter(extra.get(u, ()))

                def between():
                    f = next(todo, None)
                    if f is not None:
                        f()
                if u % 2 == 0:
                    pe.wait_ge(w_split.sem, u // 2 + 3)
                pe.wait_ge(tile_out.sem, u + 1)
                tile_done.on(gemm_tile(pe, H, 0, KD, u // 2 % 2, u % 2 * P, 256, u % 2, True, True,
                                       (h_ready, 0) if u == 0 else None, between))
                between()
            pe_wide(pe, "out0", G, 2, (g_ready, G0["out0"]), order=[FT + f for f in FO] + list(FO))
            pe_wide(pe, "up0", H, KF // 2, (h_ready, 8), stat=1)
            pe_down(pe, "down0", (g_ready, G0["down0"]))
            pe_wide(pe, "in1", H, 3, (h_ready, 16), tail=True, stat=2)
            pe_inq(pe)
            pe_attention(pe)
            pe_wide(pe, "out1", G, 2, (g_ready, G0["out1"]))
            pe_wide(pe, "up1", H, KF // 2, (h_ready, 24), stat=3)
            pe_down(pe, "down1", (g_ready, G0["down1"]))
            pe_final(pe)

        @block.scalar
        def _(act):
            def x_square(n):
                act.wait_ge(t_drain.sem, n + 1)
                kk, cols = ((slice(n % 2 * 4, n % 2 * 4 + 4), slice(n // 2 * P, (n // 2 + 1) * P)) if n < 8 else
                            (slice(0, KD), slice(SEQ, T)))
                x_sq.on(act.activation(SQX[:, kk, cols], XT[:, kk, cols], ACT.Square))
            for n in range(4):
                x_square(n)
            split_hi(act, 0, 32)
            for n in range(4, 9):
                x_square(n)
            act.wait_ge(t_drain.sem, 10)
            for m in range(KD):
                a_hi.on(act.activation(H[:, m, 0, :], XT[:, m, :], ACT.Copy, scale=GAINS[:, m:m + 1]))

            def gelu_v(x):
                act.wait_ge(tile_out.sem, x + 3)
                v = P0[:, 16 + FO[x], :]
                vg_ok.on(act.activation(v, v, ACT.Gelu_apprx_tanh))
                act.wait_ge(vg_ok.sem, vg_ok.now)
                if x >= 2:
                    act.wait_ge(accv_ok.sem, x - 1)
                vsq_ok.on(act.activation(SQ[:, x % 2, :], v, ACT.Square))

            def gelu_u(x):
                act.wait_ge(tile_out.sem, 4 + x + 3)
                u = P0[:, 12 + FO[x], :]
                ug_ok.on(act.activation(u, u, ACT.Gelu_apprx_tanh))

            def y_high(k):
                if k < FT:
                    act.wait_ge(y_ok.sem, k + 1)
                else:
                    act.wait_ge(tile_out.sem, 16 + k - FT + 3)
                y_hi.on(act.activation(G[:, Y_TILE[k], 0, :], TG[:, k % 2, :], ACT.Copy))

            for s in range(10):
                count = raw_of("in0", s + 1)
                if s:
                    split_hi(act, (s + 1) % 2, count, (tile_done, 2 * s))
                else:
                    split_hi(act, 1, count)
                    norm_act(act, 0)
                if s in (1, 2):
                    for x in range(2):
                        gelu_v(2 * (s - 1) + x)
                if s == 3:
                    act.wait_ge(stv_done.sem, 1)
                    stdv_ok.on(act.activation(halves(ACV[:, :]), M[:, 0:2, 0:HALF], ACT.Sqrt, bias=EPSC, scale=1.0 / DC))
                if s in (3, 4):
                    for x in range(2):
                        gelu_u(2 * (s - 3) + x)
                if s in (6, 7):
                    for x in range(2):
                        y_high(2 * (s - 6) + x)
            for x in range(FT):
                y_high(FT + x)
            act_out(act, "out0", 1, G_FFN[0])
            act_up(act, "up0", 0, 1)
            act_down(act, "down0", 2, G_MIX[1])
            split_next_wide(act, "in1", 0, 0)
            norm_act(act, 2)
            split_next_wide(act, "in1", 0, 1)
            with loop(act, 2, [(w_hi, 2)]) as t:
                for j in range(2):
                    split_next_wide(act, "in1", t, j + 2)
            split_next_wide(act, "in1", 3, 0)
            act_inq(act)
            act_attention(act)
            act_out(act, "out1", 3, G_FFN[1])
            act_up(act, "up1", 1, 3)
            act_down(act, "down1", 4, G_FIN, final=True)
            act_final(act)

        @block.vector
        def _(dve):
            dve.sem_inc(tile_out.sem, 2)
            tile_out.n = 2

            def take(n, dst, src):
                dve.wait_ge(t_fill.sem, n + 1)
                return dve.tensor_copy(dst, src)
            for i in range(QT):
                for hf in range(2):
                    n = 2 * i + hf
                    t_drain.on(take(n, XT[:, 4 * hf:4 * hf + 4, i * P:(i + 1) * P],
                                    M[:, n % 4, :].rearrange("p (k t) -> p k t", k=4)))
            t_drain.on(take(8, XT[:, :, SEQ:T], M[:, 0, 0:64].rearrange("p (k n) -> p k n", k=KD)))
            t_drain.on(take(9, GAINS[:, :], M[:, 1, 0:N_GAIN]))
            dve.wait_ge(t_drain.sem, 10)
            for m in range(KD):
                dve.wait_ge(a_hi.sem, m + 1)
                h_ready.on(dve.scalar_tensor_tensor(
                    out=H[:, m, 1, :], in0=XT[:, m, :], scalar=GAINS[:, m:m + 1],
                    in1=H[:, m, 0, :].bitcast(F32), op0=ALU.mult, op1=ALU.subtract))
            norm_dve(dve, 0)

            def in0_out(u):
                dve.wait_ge(tile_done.sem, u + 1)
                tile_out.on(dve.tensor_tensor(halves(P0[:, 18 - u // 2 * 2 + u % 2, :]), sets(u % 2), halves(RSTD[:, :]),
                                              ALU.mult))

            def v_square(x):
                dve.wait_ge(vsq_ok.sem, x + 1)
                if x == 0:
                    accv_ok.on(dve.tensor_copy(ACV[:, :], SQ[:, 0, :]))
                else:
                    dve.wait_ge(accv_ok.sem, x)
                    accv_ok.on(dve.tensor_tensor(ACV[:, :], ACV[:, :], SQ[:, x % 2, :], ALU.add))

            def v_norm():
                dve.wait_ge(stdv_ok.sem, 1)
                vec.on(dve.reciprocal(ACV[:, :], ACV[:, :]))
                dve.wait_ge(vec.sem, vec.now)
                for f in FO:
                    v = P0[:, 16 + f, :]
                    vn_ok.on(dve.scalar_tensor_tensor(out=v, in0=v, scalar=GAINS[:, G_V + f:G_V + f + 1],
                                                      in1=ACV[:, :], op0=ALU.mult, op1=ALU.mult))

            def v_turned(x):
                dve.wait_ge(vt_fill.sem, x + 1)
                vt_drain.on(dve.tensor_copy(P0[:, 16 + FO[x], 0:SEQ], M[:, 2 + x % 2, :]))

            def y_low(k):
                dve.wait_ge(y_hi.sem, k + 1)
                g_ready.on(dve.tensor_tensor(G[:, Y_TILE[k], 1, :], TG[:, k % 2, :], G[:, Y_TILE[k], 0, :].bitcast(F32),
                                             ALU.subtract))

            def chunk_y(x):
                f, mv = FO[x], TA[:, x % 2, :]
                dve.wait_ge(mixed.sem, x + 1)
                mix_out.on(dve.tensor_tensor(mv[:, 0:SEQ].rearrange("p (c t) -> p c t", c=QT),
                                             M[:, MIX_BANK[x], :].rearrange("p (c t) -> p c t", c=QT),
                                             BSP[:, f, :].unsqueeze(1).to_broadcast([P, QT, P]), ALU.add))
                vec.on(dve.tensor_scalar(mv[:, SEQ:T], P0[:, 16 + f, SEQ:T], W00[:, f, 0:1], BSP[:, f, 0:1],
                                         ALU.mult, ALU.add))
                dve.wait_ge(ug_ok.sem, x + 1)
                dve.wait_ge(mix_out.sem, mix_out.now)
                dve.wait_ge(vec.sem, vec.now)
                y_ok.on(dve.tensor_tensor(TG[:, x % 2, :], P0[:, 12 + f, :], mv, ALU.mult))
                dve.wait_ge(y_ok.sem, y_ok.now)
                y_low(x)

            def conv(x):
                f = FO[x]
                z, co = P0[:, 8 + f, :], P0[:, 4 + f, :]
                dve.wait_ge(tile_out.sem, tile_out.now)
                z_ok.on(dve.tensor_tensor(z, co, z, ALU.mult))
                dve.wait_ge(z_ok.sem, z_ok.now)

                def tap(j):
                    c = G_CONV + j * FT + f
                    return GAINS[:, c:c + 1]

                def mac(dst, src, j):
                    dve.wait_ge(vec.sem, vec.now)
                    vec.on(dve.scalar_tensor_tensor(out=dst, in0=src, scalar=tap(j), in1=dst,
                                                    op0=ALU.mult, op1=ALU.add))
                vec.on(dve.tensor_scalar(co, z, tap(2), None, ALU.mult))
                mac(co[:, 1:SEQ], z[:, 0:SEQ - 1], 1)
                mac(co[:, 2:SEQ], z[:, 0:SEQ - 2], 0)
                mac(co[:, SEQ:T], HT[:, f, 1:16:2], 1)
                mac(co[:, SEQ:T], HT[:, f, 0:16:2], 0)
                dve.wait_ge(vec.sem, vec.now)
                vec.on(dve.tensor_tensor(co, co, RSTD[:, :], ALU.mult))

            def conv_y(x):
                dve.wait_ge(tile_done.sem, 16 + x + 1)
                dve.wait_ge(vec.sem, vec.now)
                tile_out.on(dve.tensor_tensor(halves(TG[:, x % 2, :]), sets(x % 2), halves(P0[:, 4 + FO[x], :]), ALU.mult))
                dve.wait_ge(tile_out.sem, tile_out.now)
                y_low(FT + x)

            for u in range(16):
                if u == 6:
                    v_square(2)
                    v_square(3)
                if u == 7:
                    v_norm()
                in0_out(u)
                if u == 3:
                    dve.wait_ge(t_fill.sem, 11)
                    t_drain.on(dve.tensor_copy(HT[:, :, :].rearrange("p f n -> p (f n)"), M[:, 2, 0:64]))
                    dve.wait_ge(t_fill.sem, 12)
                    t_drain.on(dve.tensor_tensor(WT[:, :, :], M[:, 3, :].rearrange("p (h t) -> p h t", h=4),
                                                 TRIL[:, :].unsqueeze(1).to_broadcast([P, 4, P]), ALU.mult))
                    v_square(0)
                    v_square(1)
                if u in (8, 9):
                    for x in range(2):
                        v_turned(2 * (u - 8) + x)
                if u == 9:
                    cv_ok.on(dve.tensor_copy(CV[:, :], M[0:NS, 0, :]))
                if 11 <= u < 15:
                    chunk_y(u - 11)
                if u >= 12:
                    conv(u - 12)
            for x in range(FT):
                if x == 2:
                    dve.wait_ge(zo_fill.sem, 1)
                    zo_ok.on(dve.tensor_copy(ZO[:, :], M[0:10, 1, :]))
                conv_y(x)
            dve_residual(dve, "out0", 1, G_FFN[0], 4)
            norm_dve(dve, 1)
            dve_up(dve, "up0", 0)
            dve_residual(dve, "down0", 2, G_MIX[1], 2)
            norm_dve(dve, 2)
            dve_project(dve, "in1", 3, tail=True, first=8)
            dve_inq(dve)
            dve_attention(dve)
            dve_residual(dve, "out1", 3, G_FFN[1], 4)
            norm_dve(dve, 3)
            dve_up(dve, "up1", 1)
            dve_residual(dve, "down1", 4, G_FIN, 2)
            dve_final(dve)


OUTS = [(1, SEQ, D), (NS, 1, D), (1, 2, DC), (NS, 2, DC), (NS, 1, DC), (1, SEQ, 4, NKV, HD),
        (NS, 1, 4, NKV, HD), (1, SEQ, 2, NKV, HD), (NS, 1, 2, NKV, HD)]


def kernel(**inputs):
    import concourse.bacc as bacc
    from concourse.bass_utils import run_bass_kernel_spmd

    nc = bacc.Bacc("TRN2", target_bir_lowering=False, num_devices=1)
    arrays, aps = {}, {}
    for name, x in {**inputs, **consts()}.items():
        x = np.ascontiguousarray(x)
        arrays["in_" + name] = x
        aps[name] = nc.dram_tensor("in_" + name, x.shape, mybir.dt.from_np(x.dtype), kind="ExternalInput").ap()
    outs = [nc.dram_tensor(f"out_{i}", s, F32, kind="ExternalOutput").ap() for i, s in enumerate(OUTS)]
    program(nc, aps, outs)
    r = run_bass_kernel_spmd(nc, [arrays], core_ids=[0])
    return tuple(r.results[0][f"out_{i}"] for i in range(len(OUTS)))
```
